# Optimizing a Trainium2 kernel written in Bass

```python
import jax, jax.numpy as jnp
from jax import lax
import numpy as np

D_MODEL = 1024
BATCH = 1
SEQ = 256
DEPTH = 2

N_EVEN = (DEPTH + 1) // 2
N_ODD = DEPTH // 2
EPS = 1e-6
GRID_W = 64

MEM_LEN = 256
MEM_HEADS = 4
MEM_HEAD_DIM = 64
MEM_WIDTH = MEM_HEADS * MEM_HEAD_DIM

NA_HEADS = 12
NA_HEAD_DIM = 64
NA_WIDTH = NA_HEADS * NA_HEAD_DIM
NA_WIN_ROWS = 8
NA_WIN_COLS = 16
NA_QBLOCK = 16
NA_BAND = 32

GLA_HEADS = 4
GLA_DK = 96
GLA_DV = 192
GLA_KW = GLA_HEADS * GLA_DK
GLA_VW = GLA_HEADS * GLA_DV
GLA_GATE_RANK = 16
GLA_GATE_NORM = 16.0
GLA_CHUNK = 64

D_FF = 2816
N_EXPERTS = 8
TOP_K = 2
D_FF_EXPERT = 3584
MOE_BLOCK = 256

MIX_WIDTH = NA_WIDTH + MEM_WIDTH
EVEN_IN = 3 * NA_WIDTH + MEM_WIDTH
ODD_IN = 2 * GLA_KW + 2 * GLA_VW + 2 * GLA_GATE_RANK + MEM_WIDTH

kernel_name = "hybrid_natten_gla_moe_encoder"

def rms_norm(x, g):
    xf = x.astype(jnp.float32)
    y = xf * lax.rsqrt(jnp.mean(xf * xf, axis=-1, keepdims=True) + EPS)
    return (y * g.astype(jnp.float32)).astype(x.dtype)

def swiglu(x, w_gate, w_up, w_down):
    return (jax.nn.silu(x @ w_gate) * (x @ w_up)) @ w_down

def memory_attention(q, mem_k, mem_v):
    s = jnp.einsum('bthd,bmhd->bhtm', q, mem_k).astype(jnp.float32) * (MEM_HEAD_DIM ** -0.5)
    p = jax.nn.softmax(s, axis=-1).astype(mem_v.dtype)
    o = jnp.einsum('bhtm,bmhd->bthd', p, mem_v)
    return o.reshape(q.shape[0], q.shape[1], MEM_WIDTH)

def neighbourhood_attention(q, k, v, rpb):
    B, T, H, dh = q.shape
    rows = T // GRID_W
    kr = min(NA_WIN_ROWS, rows)
    n_cb = GRID_W // NA_QBLOCK
    qc = np.arange(GRID_W).reshape(n_cb, NA_QBLOCK)
    band0 = np.clip(np.arange(n_cb) * NA_QBLOCK - NA_WIN_COLS // 2, 0, GRID_W - NA_BAND)
    kc = band0[:, None] + np.arange(NA_BAND)[None, :]
    cs = np.clip(qc - NA_WIN_COLS // 2, 0, GRID_W - NA_WIN_COLS)
    col_ok = (kc[:, None, :] >= cs[:, :, None]) & (kc[:, None, :] < cs[:, :, None] + NA_WIN_COLS)
    dc = np.clip(kc[:, None, :] - qc[:, :, None], -(NA_WIN_COLS - 1), NA_WIN_COLS - 1) + NA_WIN_COLS - 1
    col_mask = jnp.asarray(col_ok)
    bias_c = rpb[:, :, dc].astype(jnp.float32)
    kg = k.reshape(B, rows, GRID_W, H, dh)
    vg = v.reshape(B, rows, GRID_W, H, dh)
    qg = jnp.moveaxis(q.reshape(B, rows, n_cb, NA_QBLOCK, H, dh), 1, 0)
    scale = dh ** -0.5

    def row_step(args):
        q_r, r = args
        r0 = jnp.clip(r - kr // 2, 0, rows - kr)
        k_band = lax.dynamic_slice_in_dim(kg, r0, kr, axis=1)[:, :, kc]
        v_band = lax.dynamic_slice_in_dim(vg, r0, kr, axis=1)[:, :, kc]
        dr = r0 + jnp.arange(kr) - r + NA_WIN_ROWS - 1
        bias = jnp.transpose(bias_c[:, dr], (0, 2, 3, 1, 4))
        s = jnp.einsum('bjqhd,bajuhd->bhjqau', q_r, k_band).astype(jnp.float32) * scale + bias[None]
        s = jnp.where(col_mask[None, None, :, :, None, :], s, -jnp.inf)
        shp = s.shape
        p = jax.nn.softmax(s.reshape(shp[0], shp[1], shp[2], shp[3], kr * NA_BAND), axis=-1)
        p = p.reshape(shp).astype(v_band.dtype)
        return jnp.einsum('bhjqau,bajuhd->bjqhd', p, v_band)

    o = lax.map(row_step, (qg, jnp.arange(rows)))
    return jnp.moveaxis(o, 0, 1).reshape(B, T, H * dh)

def gla_direction(q, k, v, g, include_diag):
    C = q.shape[3]
    b = jnp.cumsum(g, axis=3)
    b_last = b[:, :, :, -1:, :]
    q_t = q * jnp.exp(b)
    k_t = k * jnp.exp(-b)
    mask = jnp.asarray(np.tril(np.ones((C, C), dtype=bool), 0 if include_diag else -1))
    a = jnp.where(mask, jnp.einsum('bhncd,bhnsd->bhncs', q_t, k_t), 0.0)
    o_intra = jnp.einsum('bhncs,bhnsv->bhncv', a, v)
    ds = jnp.einsum('bhncd,bhncv->bhndv', k * jnp.exp(b_last - b), v)
    decay = jnp.exp(b_last[:, :, :, 0, :])

    def step(s, inp):
        d_n, ds_n = inp
        return d_n[..., None] * s + ds_n, s

    s0 = jnp.zeros(ds.shape[:2] + ds.shape[3:], jnp.float32)
    _, s_in = lax.scan(step, s0, (jnp.moveaxis(decay, 2, 0), jnp.moveaxis(ds, 2, 0)))
    s_in = jnp.moveaxis(s_in, 0, 2)
    return o_intra + jnp.einsum('bhncd,bhndv->bhncv', q_t, s_in)

def gla_mixer(q, k, v, gk_f, gk_b, gate, g_norm):
    B, T, H, _ = q.shape
    n = T // GLA_CHUNK

    def to_chunks(a):
        return jnp.transpose(a.reshape(B, n, GLA_CHUNK, H, a.shape[-1]), (0, 3, 1, 2, 4)).astype(jnp.float32)

    def from_chunks(a):
        return jnp.transpose(a, (0, 2, 3, 1, 4)).reshape(B, T, H, a.shape[-1])

    def flip(a):
        return a[:, ::-1]

    qs = q * (GLA_DK ** -0.5)
    fwd = gla_direction(to_chunks(qs), to_chunks(k), to_chunks(v), to_chunks(gk_f), True)
    bwd = gla_direction(to_chunks(flip(qs)), to_chunks(flip(k)), to_chunks(flip(v)), to_chunks(flip(gk_b)), False)
    o = from_chunks(fwd) + flip(from_chunks(bwd))
    o = o * lax.rsqrt(jnp.mean(o * o, axis=-1, keepdims=True) + EPS) * g_norm.astype(jnp.float32)
    o = o.reshape(B, T, GLA_VW) * jax.nn.silu(gate.astype(jnp.float32))
    return o.astype(q.dtype)

def moe_swiglu(x, w_router, w_gate, w_up, w_down):
    B, T, D = x.shape
    xf = x.reshape(-1, D)
    n = xf.shape[0]
    logits = (xf @ w_router).astype(jnp.float32)
    top_val, top_idx = lax.top_k(logits, TOP_K)
    weights = jax.nn.softmax(top_val, axis=-1)
    e_flat = top_idx.reshape(-1)
    tok_flat = jnp.repeat(jnp.arange(n), TOP_K)
    w_flat = weights.reshape(-1)
    order = jnp.argsort(e_flat)
    e_s, tok_s, w_s = e_flat[order], tok_flat[order], w_flat[order]
    counts = jnp.bincount(e_flat, length=N_EXPERTS)
    start = jnp.cumsum(counts) - counts
    padded = (counts + MOE_BLOCK - 1) // MOE_BLOCK * MOE_BLOCK
    pend = jnp.cumsum(padded)
    pstart = pend - padded
    dest = pstart[e_s] + jnp.arange(n * TOP_K) - start[e_s]
    cap = n * TOP_K + N_EXPERTS * MOE_BLOCK
    n_blocks = cap // MOE_BLOCK
    x_pad = jnp.zeros((cap, D), x.dtype).at[dest].set(xf[tok_s])
    block_expert = jnp.clip(jnp.searchsorted(pend, jnp.arange(n_blocks) * MOE_BLOCK, side='right'), 0, N_EXPERTS - 1)

    def expert_block(args):
        xb, e = args
        return swiglu(xb, w_gate[e], w_up[e], w_down[e])

    y_pad = lax.map(expert_block, (x_pad.reshape(n_blocks, MOE_BLOCK, D), block_expert)).reshape(cap, D)
    y = y_pad[dest] * w_s[:, None].astype(x.dtype)
    return jax.ops.segment_sum(y, tok_s, num_segments=n).reshape(B, T, D)

def setup_inputs(seed: int = 0) -> dict:
    key = jax.random.key(seed)
    ks = iter(jax.random.split(key, 32))
    D = D_MODEL

    def nrm(shape, scale):
        return scale * jax.random.normal(next(ks), shape, jnp.float32)

    def gain(shape):
        return 1.0 + nrm(shape, 0.02)

    return {
        "x": nrm((BATCH, SEQ, D), 1.0),
        "mem": nrm((BATCH, MEM_LEN, D), 1.0),
        "even_norm1": gain((N_EVEN, D)),
        "even_w_in": nrm((N_EVEN, D, EVEN_IN), D ** -0.5),
        "even_rpb": nrm((N_EVEN, NA_HEADS, 2 * NA_WIN_ROWS - 1, 2 * NA_WIN_COLS - 1), 0.2),
        "even_w_out": nrm((N_EVEN, MIX_WIDTH, D), MIX_WIDTH ** -0.5),
        "even_norm2": gain((N_EVEN, D)),
        "even_w_gate": nrm((N_EVEN, D, D_FF), D ** -0.5),
        "even_w_up": nrm((N_EVEN, D, D_FF), D ** -0.5),
        "even_w_down": nrm((N_EVEN, D_FF, D), D_FF ** -0.5),
        "odd_norm1": gain((N_ODD, D)),
        "odd_w_in": nrm((N_ODD, D, ODD_IN), D ** -0.5),
        "odd_w_gk_fwd": nrm((N_ODD, GLA_GATE_RANK, GLA_KW), GLA_GATE_RANK ** -0.5),
        "odd_b_gk_fwd": nrm((N_ODD, GLA_KW), 0.1),
        "odd_w_gk_bwd": nrm((N_ODD, GLA_GATE_RANK, GLA_KW), GLA_GATE_RANK ** -0.5),
        "odd_b_gk_bwd": nrm((N_ODD, GLA_KW), 0.1),
        "odd_g_norm": gain((N_ODD, GLA_DV)),
        "odd_w_out": nrm((N_ODD, MIX_WIDTH, D), MIX_WIDTH ** -0.5),
        "odd_norm2": gain((N_ODD, D)),
        "odd_w_router": nrm((N_ODD, D, N_EXPERTS), D ** -0.5),
        "odd_w_gate": nrm((N_ODD, N_EXPERTS, D, D_FF_EXPERT), D ** -0.5),
        "odd_w_up": nrm((N_ODD, N_EXPERTS, D, D_FF_EXPERT), D ** -0.5),
        "odd_w_down": nrm((N_ODD, N_EXPERTS, D_FF_EXPERT, D), D_FF_EXPERT ** -0.5),
        "mem_norm": gain((D,)),
        "w_mem_kv": nrm((D, 2 * MEM_WIDTH), D ** -0.5),
        "final_norm": gain((D,)),
    }

def reference(x, mem, even_norm1, even_w_in, even_rpb, even_w_out, even_norm2, even_w_gate, even_w_up,
              even_w_down, odd_norm1, odd_w_in, odd_w_gk_fwd, odd_b_gk_fwd, odd_w_gk_bwd, odd_b_gk_bwd,
              odd_g_norm, odd_w_out, odd_norm2, odd_w_router, odd_w_gate, odd_w_up, odd_w_down,
              mem_norm, w_mem_kv, final_norm):
    B, T, _ = x.shape
    M = mem.shape[1]
    mem_kv = (rms_norm(mem, mem_norm) @ w_mem_kv).reshape(B, M, 2, MEM_HEADS, MEM_HEAD_DIM)
    mem_k, mem_v = mem_kv[:, :, 0], mem_kv[:, :, 1]
    h = x
    for i in range(DEPTH):
        j = i // 2
        if i % 2 == 0:
            u = rms_norm(h, even_norm1[j])
            q, k, v, qm = jnp.split(u @ even_w_in[j], [NA_WIDTH, 2 * NA_WIDTH, 3 * NA_WIDTH], axis=-1)
            mix = neighbourhood_attention(q.reshape(B, T, NA_HEADS, NA_HEAD_DIM),
                                          k.reshape(B, T, NA_HEADS, NA_HEAD_DIM),
                                          v.reshape(B, T, NA_HEADS, NA_HEAD_DIM), even_rpb[j])
            mo = memory_attention(qm.reshape(B, T, MEM_HEADS, MEM_HEAD_DIM), mem_k, mem_v)
            h = h + jnp.concatenate([mix, mo], axis=-1) @ even_w_out[j]
            h = h + swiglu(rms_norm(h, even_norm2[j]), even_w_gate[j], even_w_up[j], even_w_down[j])
        else:
            u = rms_norm(h, odd_norm1[j])
            splits = [GLA_KW, 2 * GLA_KW, 2 * GLA_KW + GLA_VW, 2 * GLA_KW + 2 * GLA_VW,
                      2 * GLA_KW + 2 * GLA_VW + GLA_GATE_RANK, 2 * GLA_KW + 2 * GLA_VW + 2 * GLA_GATE_RANK]
            q, k, v, g, zf, zb, qm = jnp.split(u @ odd_w_in[j], splits, axis=-1)
            gk_f = jax.nn.log_sigmoid((zf @ odd_w_gk_fwd[j] + odd_b_gk_fwd[j]).astype(jnp.float32)) / GLA_GATE_NORM
            gk_b = jax.nn.log_sigmoid((zb @ odd_w_gk_bwd[j] + odd_b_gk_bwd[j]).astype(jnp.float32)) / GLA_GATE_NORM
            mix = gla_mixer(q.reshape(B, T, GLA_HEADS, GLA_DK), k.reshape(B, T, GLA_HEADS, GLA_DK),
                            v.reshape(B, T, GLA_HEADS, GLA_DV),
                            gk_f.reshape(B, T, GLA_HEADS, GLA_DK), gk_b.reshape(B, T, GLA_HEADS, GLA_DK),
                            g, odd_g_norm[j])
            mo = memory_attention(qm.reshape(B, T, MEM_HEADS, MEM_HEAD_DIM), mem_k, mem_v)
            h = h + jnp.concatenate([mix, mo], axis=-1) @ odd_w_out[j]
            h = h + moe_swiglu(rms_norm(h, odd_norm2[j]), odd_w_router[j], odd_w_gate[j], odd_w_up[j], odd_w_down[j])
    return rms_norm(h, final_norm)


_drawn_inputs = setup_inputs


def setup_inputs(seed=0):
    import zlib

    import numpy as np

    out = dict(_drawn_inputs(seed))
    spreads = {}
    factors = {'even_norm1': 2.964,
     'odd_b_gk_fwd': 17.678,
     'mem_norm': 8.0,
     'final_norm': 21.973,
     'even_norm2': 5.982,
     'odd_w_gk_fwd': 7.024,
     'odd_w_gk_bwd': 8.0,
     'odd_b_gk_bwd': 8.0,
     'odd_g_norm': 59.508,
     'odd_norm2': 8.0,
     'odd_norm1': 2.762}
    for name, (base, spread) in spreads.items():
        noise = np.random.default_rng([zlib.crc32(name.encode()), seed]).standard_normal(out[name].shape)
        drawn = base * np.exp(spread * noise) if base else spread * noise
        out[name] = __import__('jax').numpy.asarray(drawn.astype(out[name].dtype))
    for name, factor in factors.items():
        out[name] = (out[name] * factor).astype(out[name].dtype)
    return out
```

```python
from contextlib import ExitStack

import concourse.bass as bass
from concourse import mybir

ALU = mybir.AluOpType
ACT = mybir.ActivationFunctionType
F32 = mybir.dt.float32
F32R = mybir.dt.float32r
I32 = mybir.dt.int32
AX_X = mybir.AxisListType.X

P = 128
D = 1024
T = 256
TT = T // P
KD = D // P
EPS = 1e-6
HEAD = 64
NA_HEADS, MEM_HEADS = 12, 4
GRID_W = 64
ROWS = T // GRID_W
RPB_R, RPB_C = 15, 31
DR0 = 5
NDR = 6
GH, DK, DV = 4, 96, 192
KW, VW = GH * DK, GH * DV
CH = 64
NCH = T // CH
RANK = 16
D_FF = 2816
E = 8
FE = 3584
NEG = -1e30

RAW = 6
CUT = 3
SLOT = 2048

FF_W = 256
FF_N = D_FF // FF_W
FC = 512
NC = FE // FC
UNIT_SLOTS = 6 * NC
UNIT_LAND = 16 * UNIT_SLOTS // RAW
MAX_UNITS = E + 3
UCOLS = MAX_UNITS + 1

N_KV, N_IN0, N_OUT, N_FF, N_IN1 = 2, 10, 4, 3 * FF_N, 14
S_IN0 = N_KV
S_OUT0 = S_IN0 + N_IN0
S_FF = S_OUT0 + N_OUT
S_IN1 = S_FF + N_FF
S_OUT1 = S_IN1 + N_IN1
S_MOE = S_OUT1 + N_OUT
IN1_COLS = [(0, KW), (KW, KW)] + [(2 * KW + 384 * i, 384) for i in range(4)] + [(2 * KW + 2 * VW, 2 * RANK + 256)]


def slot_width(n):
    return 4 * IN1_COLS[(n - S_IN1) // 2][1] if S_IN1 <= n < S_OUT1 else SLOT


def ff_slot(kind, c):
    if kind == "down":
        return S_FF + (3 * (c + 1) + 1 if c + 1 < FF_N else 3 * FF_N - 1)
    return S_FF + (0 if c == 0 else 3 * c - 1) + (1 if kind == "up" else 0)


def mix_tile(item):
    return item // 2 if item < 16 else 6 + (item - 16) // 2


def shape_constants(np):
    i = np.arange(P)[:, None]
    j = np.arange(P)[None, :]
    same = (i // CH) == (j // CH)
    col = {}
    parts = []

    def put(name, a):
        full = np.zeros((P, a.shape[1]), np.float32)
        full[: a.shape[0]] = a
        col[name] = (sum(x.shape[1] for x in parts), a.shape[1])
        parts.append(full)

    put("ident", (i == j) * 1.0)
    put("tri_f", (same & (i <= j)) / 16.0)
    put("tri_b", (same & (i >= j)) / 16.0)
    put("strict_b", (same & (i > j)) * 1.0)
    put("before", (i < j) * 1.0)
    put("ones", np.ones((P, P)))
    put("iota", np.broadcast_to(np.arange(P), (P, P)))
    c = np.arange(P) % GRID_W
    start = np.clip(c - 8, 0, GRID_W - 16)[:, None]
    cc = np.arange(GRID_W)[None, :]
    put("col_mask", np.where((cc >= start) & (cc < start + 16), 0.0, NEG))
    put("shift", (np.arange(RPB_C)[:, None] + np.arange(127)[None, :] == 78) * 1.0)
    return np.concatenate(parts, 1), col


def moe_slot(kind, c, half):
    if kind == "down":
        return (4 + 6 * c + 4 if c + 1 < NC else 4 + 6 * c) + half
    base = 0 if c == 0 else 4 + 6 * (c - 1)
    return base + (2 if kind == "up" else 0) + half


def build(nc, col, tables, x, mem, gains, rpb, gate_aug, g_norm, router, mem_kv, even_in, even_out,
          even_gate, even_up, even_down, odd_in, odd_out, exp_gate, exp_up, exp_down, out):
    with ExitStack() as ctx:
        def sb(name, shape, dt=F32):
            return ctx.enter_context(nc.sbuf_tensor(name, shape, dt))

        def sem(name):
            return ctx.enter_context(nc.semaphore(name))

        ps = ctx.enter_context(nc.psum_tensor("ps", [P, 8, 512], F32))

        raw = sb("raw", [P, RAW, SLOT])
        w_hi = sb("w_hi", [P, CUT, SLOT], F32R)
        w_lo = sb("w_lo", [P, CUT, SLOT], F32R)
        h = sb("h", [P, TT, D])
        xn = sb("xn", [P, TT, D])
        xt_hi = sb("xt_hi", [P, KD, T], F32R)
        xt_lo = sb("xt_lo", [P, KD, T], F32R)
        hT_hi = sb("hT_hi", [P, 2, 512], F32R)
        hT_lo = sb("hT_lo", [P, 2, 512], F32R)
        gain = sb("gain", [P, D])
        cst = sb("cst", [P, max(a + n for a, n in col.values())])
        mkT = sb("mkT", [P, 2, T])
        mv = sb("mv", [P, 2, 256])
        ss = sb("ss", [P, 12])
        ms = sb("ms", [P, 12])
        rstd = sb("rstd", [P, 12])
        mhalf = sb("mhalf", [P, 8])
        stat = sb("stat", [P, 20, 2, 3])
        gnb = sb("gnb", [P, DV])
        rt_sb = sb("rt_sb", [P, KD, E])
        rt_hi = sb("rt_hi", [P, KD, E], F32R)
        rt_lo = sb("rt_lo", [P, KD, E], F32R)
        unit_i = sb("unit_i", [P, 4], I32)
        states = sb("states", [P, 2, 3, DV])
        ARENA = 13520
        arena = sb("arena", [P, ARENA])
        top = [0]

        def take(n):
            a = top[0]
            top[0] += n
            assert top[0] <= ARENA, top[0]
            return arena[:, a:a + n]

        def const(name, rows=P):
            a, n = col[name]
            return cst[0:rows, a:a + n]

        ident, iota = const("ident"), const("iota")

        qkT = take(14 * T).rearrange("p (i t) -> p i t", t=T)
        v0 = take(TT * 768).rearrange("p (t n) -> p t n", t=TT)
        bias = take(NA_HEADS * NDR * GRID_W).rearrange("p (x c) -> p x c", c=GRID_W)
        s_a = take(3 * 2 * T).rearrange("p (b t m) -> p b t m", b=3, t=2)
        pT_a = take(2 * 2 * T).rearrange("p (b j q) -> p b j q", b=2, j=2)
        rp_a = take(NA_HEADS * RPB_R).rearrange("p (h r) -> p h r", r=RPB_R)
        mem_sb = arena[:, 0:TT * D].rearrange("p (t d) -> p t d", t=TT)
        top[0] = 0
        qg = take(GH * T).rearrange("p (h t) -> p h t", h=GH)
        kg = take(GH * T).rearrange("p (h t) -> p h t", h=GH)
        v1 = take(TT * VW).rearrange("p (t n) -> p t n", t=TT)
        sg = take(TT * VW).rearrange("p (t n) -> p t n", t=TT)
        qm1 = take(2 * T).rearrange("p (i t) -> p i t", i=2)
        z_sb = take(TT * 32).rearrange("p (t n) -> p t n", t=TT)
        glog = take(2 * TT * KW).rearrange("p (d t n) -> p d t n", d=2, t=TT)
        kdt = glog
        bt = take(2 * GH * T).rearrange("p (d x) -> p d x", d=2)
        qe_at = top[0]
        qe = take(2 * GH * T).rearrange("p (d x) -> p d x", d=2)
        ke_at = top[0]
        ke = take(2 * GH * T).rearrange("p (d x) -> p d x", d=2)
        blast = take(2 * GH * NCH).rearrange("p (d n) -> p d n", d=2)
        decay = take(2 * GH * NCH).rearrange("p (d n) -> p d n", d=2)
        gss = take(3 * 2 * GH).rearrange("p (x n) -> p x n", x=3)
        junk = arena[:, qe_at - 2 * DV:qe_at].rearrange("p (b n) -> p b n", b=2)
        top[0] = qe_at
        s_b = take(3 * 2 * T).rearrange("p (b t m) -> p b t m", b=3, t=2)
        pT_b = states[:].rearrange("p d k n -> p (d k n)")[:, 0:4 * T].rearrange("p (b j q) -> p b j q", b=2, j=2)
        top[0] = ke_at
        gk_w = take(2 * KW)
        zT = take(2 * T).rearrange("p (d t) -> p d t", d=2)
        xn_flat = xn[:].rearrange("p t d -> p (t d)")
        o1 = xn_flat[:, 0:TT * VW].rearrange("p (t n) -> p t n", t=TT)
        at = xn_flat[:, TT * VW:TT * VW + 2 * TT * P].rearrange("p (b t s) -> p b t s", b=2, t=TT)
        top[0] = 0
        silu_sb = take(2 * 512).rearrange("p (b n) -> p b n", b=2)
        hid = take(2 * 512).rearrange("p (b n) -> p b n", b=2)
        y_sb = take(D)
        pick = take(TT * P).rearrange("p (t s) -> p t s", t=TT)
        pick_w = take(TT * P).rearrange("p (t s) -> p t s", t=TT)
        pick_wT = take(TT * P).rearrange("p (t s) -> p t s", t=TT)
        u_slot = take(TT * UCOLS).rearrange("p (t u) -> p t u", t=TT)
        u_wt = take(TT * UCOLS).rearrange("p (t u) -> p t u", t=TT)
        unit_f = take(4)
        r_at = top[0]
        gx_hi, gx_lo = xt_hi[:, :, 0:P], xt_lo[:, :, 0:P]

        top[0] = r_at

        def by_expert():
            return take(TT * E).rearrange("p (t e) -> p t e", t=TT)

        r_logit, r_cand, r_one1, r_one2, r_rest, r_mask = (by_expert() for _ in range(6))
        r_m1, r_m2, r_idx, r_gap, r_gap_exp, r_w1, r_w2 = (take(TT) for _ in range(7))
        r_over, r_number = take(E), take(E)
        r_sel = take(3 * E).rearrange("p (j e) -> p j e", j=3)
        r_prod = take(3 * E).rearrange("p (j e) -> p j e", j=3)
        r_sum = take(3)

        def STATE_PS(d, k):
            bank, place = ((0, 0), (1, 0), (0, 1))[k] if d == 0 else ((1, 1), (2, 0), (5, 0))[k]
            return ps[0:DK, bank, DV * place:DV * (place + 1)]

        landed = [sem(f"landed_{r}") for r in range(RAW)]
        hi_ready, lo_ready, slot_done = sem("hi_ready"), sem("lo_ready"), sem("slot_done")
        tables_in, rpb_in, mem_in, x_in, gain_in = (
            sem("tables_in"), sem("rpb_in"), sem("mem_in"), sem("x_in"), sem("gain_in"))
        gnorm_in, router_in, gate_w_in, stored = (
            sem("gnorm_in"), sem("router_in"), sem("gate_w_in"), sem("stored"))
        half_ready, zT_ones, at_zeroed = sem("half_ready"), sem("zT_ones"), sem("at_zeroed")
        sumsq_ready, ms_ready, rstd_ready, xn_ready = (
            sem("sumsq_ready"), sem("ms_ready"), sem("rstd_ready"), sem("xn_ready"))
        turned, xt_hi_ready, xt_lo_ready = sem("turned"), sem("xt_hi_ready"), sem("xt_lo_ready")
        kv_copied_a, kv_copied_v = sem("kv_copied_a"), sem("kv_copied_v")
        bias_mm, bias_ready = sem("bias_mm"), sem("bias_ready")
        in0_copied_a, in0_copied_v = sem("in0_copied_a"), sem("in0_copied_v")
        scores_done, scores_max, probs_exp, probs_ready, probs_turned, probsT_ready, heads_done = (
            sem("scores_done"), sem("scores_max"), sem("probs_exp"), sem("probs_ready"),
            sem("probs_turned"), sem("probsT_ready"), sem("heads_done"))
        mix_hi, mix_lo, out_added = sem("mix_hi"), sem("mix_lo"), sem("out_added")
        ff_silu, ff_hid, ff_hi, ff_lo, ff_added = (
            sem("ff_silu"), sem("ff_hid"), sem("ff_hi"), sem("ff_lo"), sem("ff_added"))
        in1_copied_a, in1_copied_v = sem("in1_copied_a"), sem("in1_copied_v")
        zT_done, zT_ready, gate_done, gate_abs, gate_exp, gate_ln, gate_ready = (
            sem("zT_done"), sem("zT_ready"), sem("gate_done"), sem("gate_abs"), sem("gate_exp"),
            sem("gate_ln"), sem("gate_ready"))
        cum_done, cum_copied, blast_ready, decay_ready, exps_done, diff_ready, qk_ready = (
            sem("cum_done"), sem("cum_copied"), sem("blast_ready"), sem("decay_ready"),
            sem("exps_done"), sem("diff_ready"), sem("qk_ready"))
        kd_exp, kd_ready, kd_turned, kdt_ready = (
            sem("kd_exp"), sem("kd_ready"), sem("kd_turned"), sem("kdt_ready"))
        state_done, states_ready, at_done, at_ready, o_done, o_copied, o_squared, o_ms, o_rstd, o_ready = (
            sem("state_done"), sem("states_ready"), sem("at_done"), sem("at_ready"), sem("o_done"),
            sem("o_copied"), sem("o_squared"), sem("o_ms"), sem("o_rstd"), sem("o_ready"))
        sgn_ready, o_turned = sem("sgn_ready"), sem("o_turned")
        rt_cut = sem("rt_cut")
        dve_own = sem("dve_own")
        logits_done, gap_ready, gap_exp, masks_ready, ranks_done, units_ready = (
            sem("logits_done"), sem("gap_ready"), sem("gap_exp"), sem("masks_ready"),
            sem("ranks_done"), sem("units_ready"))
        silu_ready, hid_ready, hid_turned, hT_hi_ready, hT_lo_ready = (
            sem("silu_ready"), sem("hid_ready"), sem("hid_turned"), sem("hT_hi_ready"), sem("hT_lo_ready"))
        pick_ready, pick_turned, pickT_ready, gathered, gx_hi_ready, gx_lo_ready = (
            sem("pick_ready"), sem("pick_turned"), sem("pickT_ready"), sem("gathered"),
            sem("gx_hi_ready"), sem("gx_lo_ready"))
        y_ready_a, y_ready_v, scattered, h_added = (
            sem("y_ready_a"), sem("y_ready_v"), sem("scattered"), sem("h_added"))

        kp = "(k p) n -> p k n"
        block = ctx.enter_context(nc.Block())

        @block.sync
        def _(sp):
            def put(n, src):
                if n >= RAW:
                    sp.wait_ge(lo_ready, n - RAW + 1)
                k, width = src.shape[1], src.shape[2]
                sp.dma_start(raw[:, n % RAW, 0:k * width].rearrange("p (k n) -> p k n", k=k),
                             src).then_inc(landed[n % RAW], 16)

            def halves(n, w, c0, width):
                for half in range(2):
                    put(n + half, w.rearrange(kp, p=P)[:, 4 * half:4 * half + 4, c0:c0 + width])

            def next_gain(i):
                if i >= 1:
                    sp.wait_ge(xn_ready, 2 * i)
                sp.dma_start(gain[:], gains[i:i + 1, :].partition_broadcast(P)).then_inc(gain_in, 16)

            sp.dma_start(cst[:], tables).then_inc(tables_in, 16)
            sp.dma_start(rp_a[0:RPB_C], rpb).then_inc(rpb_in, 16)
            sp.dma_start(rt_sb[:], router.rearrange(kp, p=P)).then_inc(router_in, 16)
            sp.dma_start(mem_sb, mem.rearrange("(t p) d -> p t d", p=P)).then_inc(mem_in, 16)
            next_gain(0)
            sp.dma_start(h[:], x.rearrange("(t p) d -> p t d", p=P)).then_inc(x_in, 16)
            halves(0, mem_kv, 0, 512)
            sp.dma_start(gnb[:], g_norm.partition_broadcast(P)).then_inc(gnorm_in, 16)
            halves(S_IN0, even_in, 0, 512)
            next_gain(1)
            for c in range(1, 5):
                halves(S_IN0 + 2 * c, even_in, 512 * c, 512)
            next_gain(2)
            for c in range(2):
                halves(S_OUT0 + 2 * c, even_out, 512 * c, 512)
            g3, u3, d3 = (w.rearrange(kp, p=P) for w in (even_gate, even_up, even_down))
            for c in range(FF_N + 1):
                if c < FF_N:
                    put(ff_slot("gate", c), g3[:, :, FF_W * c:FF_W * (c + 1)])
                    put(ff_slot("up", c), u3[:, :, FF_W * c:FF_W * (c + 1)])
                if c >= 1:
                    put(ff_slot("down", c - 1), d3[:, 2 * (c - 1):2 * c, :])
                if c == 3:
                    next_gain(3)
            for i, (c0, width) in enumerate(IN1_COLS):
                halves(S_IN1 + 2 * i, odd_in, c0, width)
                if i == 2:
                    sp.wait_ge(ff_added, 4)
                    sp.dma_start(gk_w[0:RANK + 1, :], gate_aug).then_inc(gate_w_in, 16)
                    next_gain(4)
            for c in range(2):
                halves(S_OUT1 + 2 * c, odd_out, 512 * c, 512)

            def expert_loads(base, e, count=UNIT_SLOTS):
                wg, wu, wd = (w[bass.ds(e, 1)].rearrange("e (k p) f -> p (e k) f", p=P)
                              for w in (exp_gate, exp_up, exp_down))
                src = {}
                for c in range(NC):
                    for half in range(2):
                        cols = slice(FC * c, FC * (c + 1))
                        src[moe_slot("gate", c, half)] = wg[:, 4 * half:4 * half + 4, cols]
                        src[moe_slot("up", c, half)] = wu[:, 4 * half:4 * half + 4, cols]
                        src[moe_slot("down", c, half)] = wd[:, 4 * c + 2 * half:4 * c + 2 * half + 2, :]
                for j in range(count):
                    r = (S_MOE + j) % RAW
                    sp.wait_ge(lo_ready, base + (S_MOE + j - RAW + 1))
                    sp.dma_start(raw[:, r, :].rearrange("p (k n) -> p k n", k=src[j].shape[1]),
                                 src[j]).then_inc(landed[r], 16)

            with sp.Fori(0, E) as u:
                expert_loads(u * UNIT_SLOTS, u)
            sp.wait_ge(units_ready, 1)
            n_more = sp.value_load(unit_i[0:1, 0:1], min_val=0, max_val=3)
            for i in range(MAX_UNITS - E):
                with sp.If(n_more > i):
                    e = sp.value_load(unit_i[0:1, 1 + i:2 + i], min_val=0, max_val=E - 1)
                    expert_loads((E + i) * UNIT_SLOTS, e)
            expert_loads((n_more + E) * UNIT_SLOTS, 0, count=CUT)
            next_gain(5)
            sp.wait_ge(xn_ready, 12)
            sp.dma_start(out.rearrange("(t p) d -> p t d", p=P), xn[:]).then_inc(stored, 16)
            sp.wait_ge(stored, 16)

        @block.scalar
        def _(act):
            cut = [0]

            def high_to(last):
                while cut[0] <= last:
                    n = cut[0]
                    w = slot_width(n)
                    act.wait_ge(landed[n % RAW], 16 * (n // RAW + 1))
                    if n >= CUT:
                        act.wait_ge(slot_done, n - CUT + 1)
                    act.activation(w_hi[:, n % CUT, 0:w], raw[:, n % RAW, 0:w], ACT.Copy).then_inc(hi_ready, 1)
                    cut[0] += 1

            def products(n):
                high_to(n + CUT)
                act.wait_ge(slot_done, n + 1)

            def norm(i, src):
                if i >= 1:
                    act.wait_ge(turned, 4 * min(i, 5))
                for t in range(TT):
                    act.activation(xn[:, t, :], src[:, t, :], ACT.Square,
                                   accum_out=ss[:, 2 * i + t:2 * i + t + 1]).then_inc(sumsq_ready, 1)

            def turned_high(i):
                for b in range(4):
                    act.wait_ge(turned, 4 * i + b + 1)
                    act.activation(xt_hi[:, 2 * b:2 * b + 2, :],
                                   ps[:, b, :].rearrange("p (k t) -> p k t", k=2),
                                   ACT.Copy).then_inc(xt_hi_ready, 1)

            def attention(first, n, s, pT):
                for step in range(n + 3):
                    if step < n:
                        i = first + step
                        act.wait_ge(scores_max, i + 1)
                        for t in range(2):
                            act.activation(s[:, i % 3, t, :], s[:, i % 3, t, :], ACT.Exp,
                                           bias=stat[:, i, t, 0:1],
                                           accum_out=stat[:, i, t, 1:2]).then_inc(probs_exp, 1)
                    if 2 <= step < n + 2:
                        i = first + step - 2
                        act.wait_ge(probs_turned, i + 1)
                        if step >= 4:
                            act.wait_ge(heads_done, i - 1)
                        act.activation(pT[:, i % 2].rearrange("p j q -> p (j q)"), ps[:, 2 + i % 2, :],
                                       ACT.Copy).then_inc(probsT_ready, 1)
                    if step >= 4 and step % 2 == 0:
                        i = first + step - 3
                        act.wait_ge(heads_done, i + 1)
                        act.activation(xt_hi[:, mix_tile(i), :], ps[:, 4 + i // 2 % 2, 0:T],
                                       ACT.Copy).then_inc(mix_hi, 1)

            act.wait_ge(mem_in, 16)
            norm(0, mem_sb)
            turned_high(0)
            act.wait_ge(x_in, 16)
            norm(1, h)
            products(1)
            for b in range(2):
                act.activation(mkT[:, b, :], ps[:, 4 + b, 0:T], ACT.Copy).then_inc(kv_copied_a, 1)
            turned_high(1)
            for c in range(5):
                products(S_IN0 + 2 * c + 1)
                for i in range(2):
                    b = 4 * (c % 2) + i
                    if c < 3:
                        dst, src = qkT[:, 4 * c + i, :], ps[:, b, 0:T]
                    elif c == 3:
                        dst, src = v0[:, 0, 256 * i:256 * (i + 1)], ps[:, b, 0:256]
                    else:
                        dst, src = v0[:, i, 512:768], ps[:, b, 0:256]
                    act.activation(dst, src, ACT.Copy).then_inc(in0_copied_a, 1)
            attention(0, 16, s_a, pT_a)
            high_to(S_OUT0 + 3 + CUT)
            act.wait_ge(out_added, 4)
            norm(2, h)
            turned_high(2)
            for c in range(FF_N):
                products(ff_slot("gate", c))
                if c >= 2:
                    act.wait_ge(ff_hid, c - 1)
                act.activation(silu_sb[:, c % 2, :], ps[:, 2 * (c % 2), :], ACT.Silu).then_inc(ff_silu, 1)
                high_to(ff_slot("up", c) + CUT)
                act.wait_ge(ff_hid, c + 1)
                if c >= 2:
                    act.wait_ge(slot_done, ff_slot("down", c - 2) + 1)
                act.activation(hT_hi[:, c % 2, :], hid[:, c % 2, :], ACT.Copy).then_inc(ff_hi, 1)
            high_to(S_IN1 - 1 + CUT)
            act.wait_ge(ff_added, 4)
            norm(3, h)
            turned_high(3)
            products(S_IN1 + 1)
            for i in (0, 2):
                act.activation(qg[0:DK, i, :], ps[0:DK, i, 0:T], ACT.Copy,
                               scale=float(DK) ** -0.5).then_inc(in1_copied_a, 1)
            products(S_IN1 + 3)
            for i in (0, 2):
                act.activation(kg[0:DK, i, :], ps[0:DK, 4 + i, 0:T], ACT.Copy).then_inc(in1_copied_a, 1)
            for c in range(2):
                products(S_IN1 + 4 + 2 * c + 1)
                act.activation(v1[:, 0, 384 * c:384 * (c + 1)], ps[:, 2 * c, 0:384],
                               ACT.Copy).then_inc(in1_copied_a, 1)
            for c in range(2):
                products(S_IN1 + 8 + 2 * c + 1)
                for t in range(TT):
                    act.activation(sg[:, t, 384 * c:384 * (c + 1)], ps[:, 4 + 2 * c + t, 0:384],
                                   ACT.Silu).then_inc(in1_copied_a, 1)
            products(S_IN1 + 13)
            for t in range(TT):
                act.activation(z_sb[:, t, :], ps[:, t, 0:32], ACT.Copy).then_inc(in1_copied_a, 1)
            for i in range(4):
                act.wait_ge(gate_done, i + 1)
                act.activation(glog[:, i // 2, i % 2, :], ps[:, i, 0:KW], ACT.Abs).then_inc(gate_abs, 1)
            for i in range(4):
                g = glog[:, i // 2, i % 2, :]
                act.wait_ge(gate_abs, i + 1)
                act.activation(g, g, ACT.Exp, scale=-1.0).then_inc(gate_exp, 1)
            for i in range(4):
                g = glog[:, i // 2, i % 2, :]
                act.wait_ge(gate_exp, i + 1)
                act.activation(g, g, ACT.Ln, bias=1.0).then_inc(gate_ln, 1)
            attention(16, 4, s_b, pT_b)
            for i in range(4):
                act.wait_ge(cum_done, i + 1)
                act.activation(bt[0:DK, i // 2, 512 * (i % 2):512 * (i % 2) + 512], ps[0:DK, 4 + i, :],
                               ACT.Copy).then_inc(cum_copied, 1)
            for d in range(2):
                act.wait_ge(cum_copied, 2 * d + 2)
                act.activation(qe[0:DK, d], bt[0:DK, d], ACT.Exp).then_inc(exps_done, 1)
                act.activation(ke[0:DK, d], bt[0:DK, d], ACT.Exp, scale=-1.0).then_inc(exps_done, 1)
                act.wait_ge(blast_ready, d + 1)
                act.activation(decay[0:DK, d], blast[0:DK, d], ACT.Exp).then_inc(decay_ready, 1)
            for d in range(2):
                act.wait_ge(diff_ready, d + 1)
                act.activation(bt[0:DK, d], bt[0:DK, d], ACT.Exp).then_inc(kd_exp, 1)
            for i in range(4):
                act.wait_ge(kd_turned, i + 1)
                act.activation(kdt[:, i // 2, i % 2, :], ps[:, i, 0:KW], ACT.Copy).then_inc(kdt_ready, 1)
            for i in range(GH):
                act.wait_ge(o_done, i + 1)
                act.activation(o1[:, :, DV * i:DV * (i + 1)],
                               ps[:, 6 + i % 2, 0:2 * DV].rearrange("p (t n) -> p t n", t=2),
                               ACT.Copy).then_inc(o_copied, 1)
                act.wait_ge(o_copied, i + 1)
                for t in range(TT):
                    k = 2 * i + t
                    if k >= 2:
                        act.wait_ge(o_squared, k - 1)
                    act.activation(junk[:, k % 2, :], o1[:, t, DV * i:DV * (i + 1)], ACT.Square,
                                   accum_out=gss[:, 0, k:k + 1]).then_inc(o_squared, 1)
            for b in range(3):
                act.wait_ge(o_turned, b + 1)
                act.activation(xt_hi[:, 2 * b:2 * b + 2, :],
                               ps[:, b, :].rearrange("p (k t) -> p k t", k=2), ACT.Copy).then_inc(mix_hi, 1)
            high_to(S_OUT1 + 3 + CUT)
            act.wait_ge(out_added, 8)
            norm(4, h)
            turned_high(4)
            act.wait_ge(gap_ready, 1)
            act.activation(r_gap_exp, r_gap, ACT.Exp).then_inc(gap_exp, 1)

            def gather_high(v):
                for b in range(2):
                    act.wait_ge(gathered, v * 2 + (b + 1))
                    act.activation(gx_hi[:, 4 * b:4 * b + 4, :],
                                   ps[:, 2 + b, :].rearrange("p (k t) -> p k t", k=4),
                                   ACT.Copy).then_inc(gx_hi_ready, 1)

            gather_high(0)
            act.wait_ge(units_ready, 1)
            n_more = act.value_load(unit_i[0:1, 0:1], min_val=0, max_val=3)
            with act.Fori(0, n_more + E) as u:
                done = [CUT]

                def high_unit(last):
                    while done[0] <= last:
                        n = S_MOE + done[0]
                        act.wait_ge(landed[n % RAW], u * UNIT_LAND + 16 * (n // RAW + 1))
                        act.wait_ge(slot_done, u * UNIT_SLOTS + (n - CUT + 1))
                        act.activation(w_hi[:, n % CUT, :], raw[:, n % RAW, :], ACT.Copy).then_inc(hi_ready, 1)
                        done[0] += 1

                def unit_products(j):
                    high_unit(j + CUT)
                    act.wait_ge(slot_done, u * UNIT_SLOTS + (S_MOE + j + 1))

                def hT_high(i):
                    act.wait_ge(hid_turned, u * NC + (i + 1))
                    if i >= 2:
                        act.wait_ge(slot_done, u * UNIT_SLOTS + (S_MOE + moe_slot("down", i - 2, 1) + 1))
                    act.activation(hT_hi[:, i % 2, :], ps[:, 4, :], ACT.Copy).then_inc(hT_hi_ready, 1)

                for c in range(NC):
                    unit_products(moe_slot("gate", c, 1))
                    if c >= 2:
                        act.wait_ge(hid_ready, u * NC + (c - 1))
                    act.activation(silu_sb[:, c % 2, :], ps[:, 2 * (c % 2), :], ACT.Silu).then_inc(silu_ready, 1)
                    if c >= 1:
                        hT_high(c - 1)
                    if c == 4:
                        act.wait_ge(pick_turned, u + 1)
                        act.activation(pick_wT.rearrange("p t s -> p (t s)"), ps[:, 7, 0:2 * P],
                                       ACT.Copy).then_inc(pickT_ready, 1)
                high_unit(UNIT_SLOTS - 1)
                hT_high(NC - 1)
                high_unit(moe_slot("down", NC - 2, 1) + CUT)
                gather_high(u + 1)
                high_unit(moe_slot("down", NC - 1, 0) + CUT)
                act.wait_ge(slot_done, u * UNIT_SLOTS + (S_MOE + UNIT_SLOTS))
                act.activation(y_sb[:, 0:512], ps[:, 5, :], ACT.Copy).then_inc(y_ready_a, 1)
                high_unit(UNIT_SLOTS - 1 + CUT)

            act.wait_ge(h_added, (n_more + E) * 4)
            norm(5, h)

        @block.gpsimd
        def _(pool):
            nc.gpsimd.memset(mhalf[:], -0.5).then_inc(half_ready, 1)
            pool.wait_ge(half_ready, 1)

            def inverse_root(i):
                pool.wait_ge(ms_ready, i + 1)
                pool.tensor_tensor(rstd[:, 2 * i:2 * i + 2], ms[:, 2 * i:2 * i + 2], mhalf[:, 0:2],
                                   ALU.pow).then_inc(rstd_ready, 1)

            for i in range(4):
                inverse_root(i)
            pool.wait_ge(ff_added, 4)
            nc.gpsimd.memset(zT[0:32], 1.0).then_inc(zT_ones, 1)
            pool.wait_ge(turned, 16)
            nc.gpsimd.memset(at, 0.0).then_inc(at_zeroed, 1)
            pool.wait_ge(o_ms, 1)
            pool.tensor_tensor(gss[:, 2, :], gss[:, 1, :], mhalf[:], ALU.pow).then_inc(o_rstd, 1)
            for i in range(4, 6):
                inverse_root(i)

        @block.vector
        def _(dve):
            cut = [0]
            own = [0]

            def mark(ins):
                ins.then_inc(dve_own, 1)
                own[0] += 1

            def settle():
                dve.wait_ge(dve_own, own[0])

            def low_to(last):
                while cut[0] <= last:
                    n = cut[0]
                    w = slot_width(n)
                    dve.wait_ge(hi_ready, n + 1)
                    dve.tensor_tensor(w_lo[:, n % CUT, 0:w], raw[:, n % RAW, 0:w],
                                      w_hi[:, n % CUT, 0:w].bitcast(F32), ALU.subtract).then_inc(lo_ready, 1)
                    cut[0] += 1

            def products(n):
                low_to(n + CUT)
                dve.wait_ge(slot_done, n + 1)

            def norm(i, src):
                dve.wait_ge(sumsq_ready, 2 * i + 2)
                dve.tensor_scalar(ms[:, 2 * i:2 * i + 2], ss[:, 2 * i:2 * i + 2], 1.0 / D, EPS,
                                  ALU.mult, ALU.add).then_inc(ms_ready, 1)
                dve.wait_ge(gain_in, 16 * (i + 1))
                dve.wait_ge(rstd_ready, i + 1)
                for t in range(TT):
                    dve.scalar_tensor_tensor(xn[:, t, :], src[:, t, :], rstd[:, 2 * i + t:2 * i + t + 1], gain[:],
                                             ALU.mult, ALU.mult).then_inc(xn_ready, 1)

            def turned_low(i):
                for b in range(4):
                    dve.wait_ge(xt_hi_ready, 4 * i + b + 1)
                    dve.tensor_tensor(xt_lo[:, 2 * b:2 * b + 2, :],
                                      ps[:, b, :].rearrange("p (k t) -> p k t", k=2),
                                      xt_hi[:, 2 * b:2 * b + 2, :].bitcast(F32),
                                      ALU.subtract).then_inc(xt_lo_ready, 1)

            def attention(first, n, s, pairs0):
                pairs = pairs0
                for step in range(n + 3):
                    if step < n:
                        i = first + step
                        dve.wait_ge(scores_done, i + 1)
                        if step >= 3:
                            dve.wait_ge(probs_turned, i - 2)
                        for t in range(2):
                            src = ps[:, i % 2, T * t:T * (t + 1)]
                            if i < NA_HEADS:
                                x0 = i * NDR + 2 - 2 * t
                                mark(dve.scalar_tensor_tensor(
                                    s[:, i % 3, t, :], src, float(HEAD) ** -0.5,
                                    bias[:, x0:x0 + ROWS, :].rearrange("p x c -> p (x c)"), ALU.mult, ALU.add))
                            else:
                                mark(dve.tensor_scalar(s[:, i % 3, t, :], src, float(HEAD) ** -0.5, None, ALU.mult))
                        settle()
                        dve.tensor_reduce(stat[:, i, :, 0], s[:, i % 3], AX_X, ALU.max,
                                          negate=True).then_inc(scores_max, 1)
                    if 1 <= step <= n:
                        i = first + step - 1
                        dve.wait_ge(probs_exp, 2 * i + 2)
                        mark(dve.reciprocal(stat[:, i, :, 2], stat[:, i, :, 1]))
                        settle()
                        for t in range(2):
                            dve.tensor_scalar(s[:, i % 3, t, :], s[:, i % 3, t, :], stat[:, i, t, 2:3], None,
                                              ALU.mult).then_inc(probs_ready, 1)
                    if step >= 4 and step % 2 == 0:
                        i = first + step - 3
                        pairs += 1
                        dve.wait_ge(mix_hi, pairs)
                        dve.tensor_tensor(xt_lo[:, mix_tile(i), :], ps[:, 4 + i // 2 % 2, 0:T],
                                          xt_hi[:, mix_tile(i), :].bitcast(F32), ALU.subtract).then_inc(mix_lo, 1)

            def add_out(slot0):
                for c in range(2):
                    products(slot0 + 2 * c + 1)
                    for t in range(TT):
                        hs = h[:, t, 512 * c:512 * (c + 1)]
                        dve.tensor_tensor(hs, hs, ps[:, 4 + 2 * c + t, :], ALU.add).then_inc(out_added, 1)

            dve.wait_ge(tables_in, 16)
            for g in range(10):
                n = min(7, GRID_W - 7 * g)
                dve.wait_ge(bias_mm, g + 1)
                dve.tensor_tensor(
                    bias[:, :, 7 * g:7 * g + n],
                    ps[:, 4 + g % 2, 0:72 * n].rearrange("p (c x) -> p x c", c=n),
                    const("col_mask")[:, 7 * g:7 * g + n].unsqueeze(1).broadcast_to([P, 72, n]),
                    ALU.add).then_inc(bias_ready, 1)
            norm(0, mem_sb)
            dve.wait_ge(router_in, 16)
            dve.tensor_copy(rt_hi[:], rt_sb[:]).then_inc(rt_cut, 1)
            dve.wait_ge(rt_cut, 1)
            dve.tensor_tensor(rt_lo[:], rt_sb[:], rt_hi[:].bitcast(F32), ALU.subtract).then_inc(rt_cut, 1)
            turned_low(0)
            low_to(1)
            norm(1, h)
            products(1)
            for t in range(TT):
                dve.tensor_copy(mv[:, t, :], ps[:, 6 + t, 0:256]).then_inc(kv_copied_v, 1)
            turned_low(1)
            for c in range(5):
                products(S_IN0 + 2 * c + 1)
                for i in (2, 3):
                    b = 4 * (c % 2) + i
                    if c < 3:
                        dst, src = qkT[:, 4 * c + i, :], ps[:, b, 0:T]
                    elif c == 3:
                        dst, src = v0[:, 1, 256 * (i - 2):256 * (i - 1)], ps[:, b, 0:256]
                    else:
                        dst, src = qkT[:, 12 + i - 2, :], ps[:, b, 0:T]
                    dve.tensor_copy(dst, src).then_inc(in0_copied_v, 1)
            attention(0, 16, s_a, 0)
            add_out(S_OUT0)
            norm(2, h)
            turned_low(2)
            for c in range(FF_N):
                products(ff_slot("up", c))
                dve.wait_ge(ff_silu, c + 1)
                if c >= 2:
                    dve.wait_ge(ff_lo, c - 1)
                dve.tensor_tensor(hid[:, c % 2, :], silu_sb[:, c % 2, :], ps[:, 2 * (c % 2) + 1, :],
                                  ALU.mult).then_inc(ff_hid, 1)
                dve.wait_ge(ff_hi, c + 1)
                dve.tensor_tensor(hT_lo[:, c % 2, :], hid[:, c % 2, :], hT_hi[:, c % 2, :].bitcast(F32),
                                  ALU.subtract).then_inc(ff_lo, 1)
            products(S_IN1 - 1)
            for t in range(TT):
                for n in range(2):
                    hs = h[:, t, 512 * n:512 * (n + 1)]
                    dve.tensor_tensor(hs, hs, ps[:, 4 + 2 * t + n, :], ALU.add).then_inc(ff_added, 1)
            norm(3, h)
            turned_low(3)
            products(S_IN1 + 1)
            for i in (1, 3):
                dve.tensor_scalar(qg[0:DK, i, :], ps[0:DK, i, 0:T], float(DK) ** -0.5, None,
                                  ALU.mult).then_inc(in1_copied_v, 1)
            products(S_IN1 + 3)
            for i in (1, 3):
                dve.tensor_copy(kg[0:DK, i, :], ps[0:DK, 4 + i, 0:T]).then_inc(in1_copied_v, 1)
            for c in range(2):
                products(S_IN1 + 4 + 2 * c + 1)
                dve.tensor_copy(v1[:, 1, 384 * c:384 * (c + 1)], ps[:, 2 * c + 1, 0:384]).then_inc(in1_copied_v, 1)
            products(S_IN1 + 11)
            products(S_IN1 + 13)
            for i in range(2):
                dve.tensor_copy(qm1[:, i, :], ps[:, 2 + i, 0:T]).then_inc(in1_copied_v, 1)
            dve.wait_ge(zT_done, 1)
            dve.wait_ge(zT_ones, 1)
            dve.tensor_copy(zT[0:RANK], ps[0:RANK, 4, :].rearrange("p (d t) -> p d t", d=2)).then_inc(zT_ready, 1)
            for i in range(4):
                g = glog[:, i // 2, i % 2, :]
                dve.wait_ge(gate_ln, i + 1)
                dve.scalar_tensor_tensor(g, ps[:, i, 0:KW], 0.0, g, ALU.min, ALU.subtract).then_inc(gate_ready, 1)
            dve.wait_ge(gnorm_in, 16)
            sg8 = sg.rearrange("p t (h n) -> p (t h) n", n=DV)
            dve.wait_ge(in1_copied_a, 12)
            dve.tensor_tensor(sg8, sg8, gnb[:].unsqueeze(1).broadcast_to([P, TT * GH, DV]),
                              ALU.mult).then_inc(sgn_ready, 1)
            attention(16, 4, s_b, 8)
            for d in range(2):
                dve.wait_ge(cum_copied, 2 * d + 2)
                ends = bt[0:DK, d].rearrange("p (n c) -> p n c", c=CH)[:, :, CH - 1 if d == 0 else 0]
                dve.tensor_copy(blast[0:DK, d], ends).then_inc(blast_ready, 1)
            for d in range(2):
                dve.wait_ge(exps_done, 2 * d + 2)
                dve.wait_ge(blast_ready, d + 1)
                b3 = bt[0:DK, d].rearrange("p (n c) -> p n c", c=CH)
                dve.tensor_tensor(b3, blast[0:DK, d].unsqueeze(2).broadcast_to([DK, GH * NCH, CH]), b3,
                                  ALU.subtract).then_inc(diff_ready, 1)
                dve.tensor_tensor(qe[0:DK, d], qe[0:DK, d], qg[0:DK].rearrange("p h t -> p (h t)"),
                                  ALU.mult).then_inc(qk_ready, 1)
                dve.tensor_tensor(ke[0:DK, d], ke[0:DK, d], kg[0:DK].rearrange("p h t -> p (h t)"),
                                  ALU.mult).then_inc(qk_ready, 1)
            for d in range(2):
                dve.wait_ge(kd_exp, d + 1)
                dve.tensor_tensor(bt[0:DK, d], bt[0:DK, d], kg[0:DK].rearrange("p h t -> p (h t)"),
                                  ALU.mult).then_inc(kd_ready, 1)
            dve.wait_ge(decay_ready, 2)
            dve.wait_ge(at_zeroed, 1)
            mask_f = const("tri_f").bitcast(I32)
            mask_b = const("strict_b").bitcast(I32)
            for i in range(GH):
                dve.wait_ge(state_done, i + 1)
                if i >= 1:
                    dve.wait_ge(o_done, i)
                for d in range(2):
                    mark(dve.tensor_copy(states[0:DK, d, 0, :], STATE_PS(d, 0)))
                for k in (1, 2):
                    settle()
                    for d in range(2):
                        n = k if d == 0 else 3 - k
                        f = decay[0:DK, d, NCH * i + n:NCH * i + n + 1]
                        ins = dve.scalar_tensor_tensor(states[0:DK, d, k, :], states[0:DK, d, k - 1, :], f,
                                                       STATE_PS(d, k), ALU.mult, ALU.add)
                        if k == 1:
                            mark(ins)
                        else:
                            ins.then_inc(states_ready, 1)
                dve.wait_ge(at_done, i + 1)
                for half in range(2):
                    r = slice(CH * half, CH * (half + 1))
                    for d, mask in enumerate((mask_f, mask_b)):
                        dve.copy_predicated(
                            at[r, i % 2, :, r], mask[r, r].unsqueeze(1).broadcast_to([CH, TT, CH]),
                            ps[r, 3 + i % 2, P * d:P * (d + 1)].rearrange("p (t c) -> p t c", t=TT)
                        ).then_inc(at_ready, 1)
                        if d == 0:
                            dve.wait_ge(at_ready, 4 * i + 2 * half + 1)
            dve.wait_ge(o_squared, 2 * GH)
            dve.tensor_scalar(gss[:, 1, :], gss[:, 0, :], 1.0 / DV, EPS, ALU.mult, ALU.add).then_inc(o_ms, 1)
            dve.wait_ge(o_rstd, 1)
            dve.wait_ge(sgn_ready, 1)
            for t in range(TT):
                for i in range(GH):
                    c = slice(DV * i, DV * (i + 1))
                    dve.scalar_tensor_tensor(o1[:, t, c], o1[:, t, c], gss[:, 2, 2 * i + t:2 * i + t + 1],
                                             sg[:, t, c], ALU.mult, ALU.mult).then_inc(o_ready, 1)
            for b in range(3):
                dve.wait_ge(mix_hi, 10 + b + 1)
                dve.tensor_tensor(xt_lo[:, 2 * b:2 * b + 2, :], ps[:, b, :].rearrange("p (k t) -> p k t", k=2),
                                  xt_hi[:, 2 * b:2 * b + 2, :].bitcast(F32), ALU.subtract).then_inc(mix_lo, 1)
            add_out(S_OUT1)
            norm(4, h)
            turned_low(4)

            i8 = iota[:, 0:E]

            def over_t(a, n=E):
                return a.unsqueeze(1).broadcast_to([P, TT, n])

            def over_e(a):
                return a.unsqueeze(2).broadcast_to([P, TT, E])

            def first_of_largest(src, m, cand, idx, onehot):
                mark(dve.tensor_reduce(m, src, AX_X, ALU.max))
                settle()
                mark(dve.tensor_tensor(cand, src, over_e(m), ALU.is_equal))
                settle()
                mark(dve.scalar_tensor_tensor(cand, cand, -100.0, over_t(i8), ALU.mult, ALU.add))
                settle()
                mark(dve.tensor_reduce(idx, cand, AX_X, ALU.min))
                settle()
                mark(dve.tensor_tensor(onehot, cand, over_e(idx), ALU.is_equal))
                settle()

            dve.wait_ge(logits_done, 1)
            mark(dve.tensor_copy(r_logit, ps[:, 0, 0:TT * E].rearrange("p (t e) -> p t e", t=TT)))
            settle()
            first_of_largest(r_logit, r_m1, r_cand, r_idx, r_one1)
            mark(dve.scalar_tensor_tensor(r_rest, r_one1, NEG, r_logit, ALU.mult, ALU.add))
            settle()
            first_of_largest(r_rest, r_m2, r_cand, r_idx, r_one2)
            dve.tensor_tensor(r_gap, r_m2, r_m1, ALU.subtract).then_inc(gap_ready, 1)
            dve.tensor_tensor(r_mask, r_one1, r_one2, ALU.add).then_inc(masks_ready, 1)
            mark(dve.memset(u_slot, -1.0))
            mark(dve.memset(u_wt, 0.0))
            dve.wait_ge(gap_exp, 1)
            mark(dve.tensor_scalar(r_w1, r_gap_exp, 1.0, None, ALU.add))
            settle()
            mark(dve.reciprocal(r_w1, r_w1))
            settle()
            mark(dve.tensor_tensor(r_w2, r_gap_exp, r_w1, ALU.mult))
            settle()
            mark(dve.tensor_tensor(r_one1, r_one1, over_e(r_w1), ALU.mult))
            mark(dve.tensor_tensor(r_one2, r_one2, over_e(r_w2), ALU.mult))
            settle()
            mark(dve.tensor_tensor(u_wt[:, :, 0:E], r_one1, r_one2, ALU.add))
            dve.wait_ge(ranks_done, 1)
            dve.wait_ge(masks_ready, 1)
            mark(dve.scalar_tensor_tensor(r_cand, ps[:, 1, 0:TT * E].rearrange("p (t e) -> p t e", t=TT), 1.0,
                                          r_mask, ALU.add, ALU.mult))
            settle()
            mark(dve.tensor_scalar(u_slot[:, :, 0:E], r_cand, -1.0, None, ALU.add))
            def build_picks(v):
                for t in range(TT):
                    place, wt = u_slot[:, t, bass.ds(v, 1)], u_wt[:, t, bass.ds(v, 1)]
                    dve.tensor_scalar(pick[:, t, :], iota, place, None, ALU.is_equal).then_inc(pick_ready, 1)
                    dve.tensor_scalar(pick_w[:, t, :], iota, place, wt, ALU.is_equal, ALU.mult
                                      ).then_inc(pick_ready, 1)

            def gather_low(v):
                for b in range(2):
                    dve.wait_ge(gx_hi_ready, v * 2 + (b + 1))
                    dve.tensor_tensor(gx_lo[:, 4 * b:4 * b + 4, :],
                                      ps[:, 2 + b, :].rearrange("p (k t) -> p k t", k=4),
                                      gx_hi[:, 4 * b:4 * b + 4, :].bitcast(F32), ALU.subtract
                                      ).then_inc(gx_lo_ready, 1)

            settle()
            build_picks(0)
            mark(dve.tensor_scalar(r_over, ps[:, 1, TT * E:TT * E + E], float(P), None, ALU.is_gt))
            settle()
            mark(dve.tensor_tensor_scan(r_number, const("ones")[:, 0:E], r_over, 0.0, ALU.mult, ALU.add))
            settle()
            for j in range(3):
                mark(dve.scalar_tensor_tensor(r_sel[:, j, :], r_number, float(j + 1), r_over,
                                              ALU.is_equal, ALU.mult))
            settle()
            for dst, vals, off in ([(unit_f[:, 1:4], i8, 0.0)]
                                   + [(u_slot[:, t, E:E + 3], u_slot[:, t, 0:E], -float(P)) for t in range(TT)]
                                   + [(u_wt[:, t, E:E + 3], u_wt[:, t, 0:E], 0.0) for t in range(TT)]):
                mark(dve.tensor_tensor(r_prod, r_sel, vals.unsqueeze(1).broadcast_to([P, 3, E]), ALU.mult))
                settle()
                mark(dve.tensor_reduce(r_sum, r_prod, AX_X, ALU.add))
                settle()
                mark(dve.tensor_scalar(dst, r_sum, off, None, ALU.add))
                settle()
            mark(dve.tensor_copy(unit_f[:, 0:1], r_number[:, E - 1:E]))
            settle()
            dve.tensor_copy(unit_i[:], unit_f).then_inc(units_ready, 1)

            gather_low(0)
            dve.wait_ge(units_ready, 1)
            n_more = dve.value_load(unit_i[0:1, 0:1], min_val=0, max_val=3)
            with dve.Fori(0, n_more + E) as u:
                done = [CUT]

                def low_unit(last):
                    while done[0] <= last:
                        n = S_MOE + done[0]
                        dve.wait_ge(hi_ready, u * UNIT_SLOTS + (n + 1))
                        dve.tensor_tensor(w_lo[:, n % CUT, :], raw[:, n % RAW, :],
                                          w_hi[:, n % CUT, :].bitcast(F32), ALU.subtract).then_inc(lo_ready, 1)
                        done[0] += 1

                def unit_products(j):
                    low_unit(j + CUT)
                    dve.wait_ge(slot_done, u * UNIT_SLOTS + (S_MOE + j + 1))

                def hT_low(i):
                    dve.wait_ge(hT_hi_ready, u * NC + (i + 1))
                    dve.tensor_tensor(hT_lo[:, i % 2, :], ps[:, 4, :], hT_hi[:, i % 2, :].bitcast(F32),
                                      ALU.subtract).then_inc(hT_lo_ready, 1)

                for c in range(NC):
                    if c >= 1:
                        low_unit(moe_slot("gate", c, 1) + CUT)
                        hT_low(c - 1)
                    unit_products(moe_slot("up", c, 1))
                    dve.wait_ge(silu_ready, u * NC + (c + 1))
                    dve.tensor_tensor(hid[:, c % 2, :], silu_sb[:, c % 2, :], ps[:, 2 * (c % 2) + 1, :],
                                      ALU.mult).then_inc(hid_ready, 1)
                    if c == 5:
                        dve.wait_ge(pick_turned, u + 1)
                        build_picks(u + 1)
                low_unit(UNIT_SLOTS - 1)
                hT_low(NC - 1)
                low_unit(moe_slot("down", NC - 2, 1) + CUT)
                gather_low(u + 1)
                low_unit(moe_slot("down", NC - 1, 0) + CUT)
                dve.wait_ge(slot_done, u * UNIT_SLOTS + (S_MOE + UNIT_SLOTS))
                dve.tensor_copy(y_sb[:, 512:1024], ps[:, 6, :]).then_inc(y_ready_v, 1)
                for q in range(4):
                    hs = h[:, q // 2, 512 * (q % 2):512 * (q % 2) + 512]
                    dve.wait_ge(scattered, u * 4 + (q + 1))
                    dve.tensor_tensor(hs, hs, ps[:, q, :], ALU.add).then_inc(h_added, 1)
                    if q == 1:
                        low_unit(UNIT_SLOTS - 1 + CUT)
            norm(5, h)

        @block.tensor
        def _(pe):
            def mul3(dst, a, b, start, stop):
                pe.matmul(dst, a[0], b[0], start=start, stop=False)
                pe.matmul(dst, a[0], b[1], start=False, stop=False)
                return pe.matmul(dst, a[1], b[0], start=False, stop=stop)

            def slot(n, k):
                w = slot_width(n)
                return [a[:, n % CUT, 0:w].rearrange("p (k n) -> p k n", k=k) for a in (w_hi, w_lo)]

            def part(pair, *idx):
                return [a[(slice(None),) + idx] for a in pair]

            xt = (xt_hi, xt_lo)
            hT = (hT_hi, hT_lo)

            def turn(i):
                for t in range(TT):
                    pe.wait_ge(xn_ready, 2 * i + t + 1)
                    for k in range(KD):
                        o = T * (k % 2) + P * t
                        ins = pe.transpose(ps[:, k // 2, o:o + P], xn[:, t, P * k:P * (k + 1)], ident)
                        if t == 1 and k % 2 == 1:
                            ins.then_inc(turned, 1)

            def project(n0, groups, width):
                for half in range(2):
                    n = n0 + half
                    w = slot(n, 4)
                    pe.wait_ge(lo_ready, n + 1)
                    for dst, form, tok, cols in groups:
                        for k4 in range(4):
                            k = 4 * half + k4
                            a = part(w, k4, cols)
                            b = part(xt, k, tok)
                            if form == "by token":
                                a, b = b, a
                            ins = mul3(dst, a, b, k == 0, k == KD - 1)
                    ins.then_inc(slot_done, 1)

            all_t = slice(0, T)
            tok = [slice(P * t, P * (t + 1)) for t in range(TT)]

            def attention(first, n, pT, q_of, k_of, v_of, pairs0):
                for step in range(n + 3):
                    if step < n:
                        i = first + step
                        r = slice(HEAD * (i % 2), HEAD * (i % 2) + HEAD)
                        if step >= 2:
                            pe.wait_ge(scores_max, i - 1)
                        for t in range(TT):
                            ins = pe.matmul(ps[:, i % 2, T * t:T * (t + 1)], q_of(i)[r, tok[t]], k_of(i)[r, :],
                                            start=True, stop=True)
                        ins.then_inc(scores_done, 1)
                    if 2 <= step < n + 2:
                        i = first + step - 2
                        pe.wait_ge(probs_ready, 2 * i + 2)
                        if step >= 4:
                            pe.wait_ge(probsT_ready, i - 1)
                        s = s_a if first == 0 else s_b
                        for t in range(TT):
                            for j in range(2):
                                o = T * j + P * t
                                ins = pe.transpose(ps[:, 2 + i % 2, o:o + P], s[:, i % 3, t, P * j:P * (j + 1)],
                                                   ident)
                        ins.then_inc(probs_turned, 1)
                    if step >= 3:
                        i = first + step - 3
                        r = slice(HEAD * (i % 2), HEAD * (i % 2) + HEAD)
                        pe.wait_ge(probsT_ready, i + 1)
                        if step >= 7 and i % 2 == 0:
                            pe.wait_ge(mix_lo, pairs0 + (i - first) // 2 - 1)
                        for j in range(2):
                            ins = pe.matmul(ps[r, 4 + i // 2 % 2, 0:T], v_of(i, j), pT[:, i % 2, j, :],
                                            start=(j == 0), stop=(j == 1))
                        ins.then_inc(heads_done, 1)

            pe.wait_ge(tables_in, 16)
            pe.wait_ge(rpb_in, 16)
            for g in range(10):
                n = min(7, GRID_W - 7 * g)
                if g >= 2:
                    pe.wait_ge(bias_ready, g - 1)
                for cc in range(n):
                    c = 7 * g + cc
                    for half in range(2):
                        ins = pe.matmul(ps[64 * half:64 * half + 64, 4 + g % 2, 72 * cc:72 * cc + 72],
                                        const("shift", RPB_C)[:, 63 - c:127 - c],
                                        rp_a[0:RPB_C, :, DR0 - half:DR0 - half + NDR],
                                        start=True, stop=True)
                ins.then_inc(bias_mm, 1)
            turn(0)
            pe.wait_ge(xt_lo_ready, 4)
            pe.wait_ge(bias_ready, 10)
            project(0, [(ps[:, 4 + i, 0:T], "by feature", all_t, slice(P * i, P * (i + 1))) for i in range(2)]
                    + [(ps[:, 6 + t, 0:256], "by token", tok[t], slice(256, 512)) for t in range(TT)], 512)
            turn(1)
            pe.wait_ge(xt_lo_ready, 8)
            for c in range(5):
                if c == 1:
                    pe.wait_ge(kv_copied_a, 2)
                    pe.wait_ge(kv_copied_v, 2)
                if c >= 2:
                    pe.wait_ge(in0_copied_a, 2 * (c - 1))
                    pe.wait_ge(in0_copied_v, 2 * (c - 1))
                b = 4 * (c % 2)
                if c < 3:
                    gs = [(ps[:, b + i, 0:T], "by feature", all_t, slice(P * i, P * (i + 1))) for i in range(4)]
                elif c == 3:
                    gs = [(ps[:, b + i, 0:256], "by token", tok[i // 2], slice(256 * (i % 2), 256 * (i % 2) + 256))
                          for i in range(4)]
                else:
                    gs = [(ps[:, b + t, 0:256], "by token", tok[t], slice(0, 256)) for t in range(TT)]
                    gs += [(ps[:, b + 2 + i, 0:T], "by feature", all_t, slice(256 + P * i, 256 + P * (i + 1)))
                           for i in range(2)]
                project(S_IN0 + 2 * c, gs, 512)
            pe.wait_ge(in0_copied_a, 10)
            pe.wait_ge(in0_copied_v, 10)
            attention(0, 16, pT_a,
                      lambda i: qkT[:, i // 2 if i < 12 else 12 + (i - 12) // 2, :],
                      lambda i: qkT[:, 6 + i // 2, :] if i < 12 else mkT[:, (i - 12) // 2, :],
                      lambda i, j: v0[:, j, HEAD * i:HEAD * (i + 1)] if i < 12
                      else mv[:, j, HEAD * (i - 12):HEAD * (i - 11)], 0)

            def project_out(slot0):
                for c in range(2):
                    project(slot0 + 2 * c, [(ps[:, 4 + 2 * c + t, :], "by token", tok[t], slice(0, 512))
                                            for t in range(TT)], 512)

            pe.wait_ge(mix_lo, 8)
            project_out(S_OUT0)
            turn(2)
            pe.wait_ge(xt_lo_ready, 12)
            for c in range(FF_N + 1):
                if c < FF_N:
                    for kind in ("gate", "up"):
                        n = ff_slot(kind, c)
                        w = slot(n, KD)
                        pe.wait_ge(lo_ready, n + 1)
                        if c >= 2:
                            pe.wait_ge(ff_silu if kind == "gate" else ff_hid, c - 1)
                        for j in range(2):
                            for k in range(KD):
                                ins = mul3(ps[:, 2 * (c % 2) + (kind == "up"), T * j:T * (j + 1)],
                                           part(w, k, slice(P * j, P * (j + 1))), part(xt, k, all_t),
                                           k == 0, k == KD - 1)
                        ins.then_inc(slot_done, 1)
                if c >= 1:
                    i = c - 1
                    n = ff_slot("down", i)
                    w = slot(n, 2)
                    pe.wait_ge(lo_ready, n + 1)
                    pe.wait_ge(ff_lo, i + 1)
                    for t in range(TT):
                        for half in range(2):
                            for j in range(2):
                                ins = mul3(ps[:, 4 + 2 * t + half, :],
                                           part(hT, i % 2, slice(T * j + P * t, T * j + P * (t + 1))),
                                           part(w, j, slice(512 * half, 512 * (half + 1))),
                                           i == 0 and j == 0, i == FF_N - 1 and j == 1)
                    ins.then_inc(slot_done, 1)
            turn(3)
            pe.wait_ge(xt_lo_ready, 16)
            for part_i, b0 in ((0, 0), (1, 4)):
                project(S_IN1 + 2 * part_i,
                        [(ps[0:DK, b0 + i, 0:T], "by feature", all_t, slice(DK * i, DK * (i + 1)))
                         for i in range(GH)], KW)
            for c in range(4):
                b0 = 2 * c
                pe.wait_ge(in1_copied_a, 2 if c < 2 else 4)
                pe.wait_ge(in1_copied_v, 2 if c < 2 else 4)
                project(S_IN1 + 4 + 2 * c, [(ps[:, b0 + t, 0:384], "by token", tok[t], slice(0, 384))
                                            for t in range(TT)], 384)
            pe.wait_ge(in1_copied_a, 6)
            pe.wait_ge(in1_copied_v, 6)
            project(S_IN1 + 12,
                    [(ps[:, t, 0:2 * RANK], "by token", tok[t], slice(0, 2 * RANK)) for t in range(TT)]
                    + [(ps[:, 2 + i, 0:T], "by feature", all_t, slice(32 + P * i, 32 + P * (i + 1)))
                       for i in range(2)], 288)
            pe.wait_ge(in1_copied_a, 12)
            for d in range(2):
                for t in range(TT):
                    ins = pe.matmul(ps[0:RANK, 4, T * d + P * t:T * d + P * (t + 1)],
                                    z_sb[:, t, RANK * d:RANK * (d + 1)], ident, start=True, stop=True)
            ins.then_inc(zT_done, 1)
            pe.wait_ge(zT_ready, 1)
            pe.wait_ge(gate_w_in, 16)
            pe.wait_ge(in1_copied_v, 8)
            for i in range(4):
                d, t = i // 2, i % 2
                pe.matmul(ps[:, i, 0:KW], zT[0:RANK + 1, d, tok[t]], gk_w[0:RANK + 1, KW * d:KW * (d + 1)],
                          start=True, stop=True).then_inc(gate_done, 1)
            pe.wait_ge(gate_ready, 4)
            attention(16, 4, pT_b, lambda i: qm1[:, (i - 16) // 2, :], lambda i: mkT[:, (i - 16) // 2, :],
                      lambda i, j: mv[:, j, HEAD * (i - 16):HEAD * (i - 15)], 8)
            pe.wait_ge(mix_lo, 10)
            for i in range(4):
                d = i // 2
                tri = const("tri_f" if d == 0 else "tri_b")
                for hh in range(2):
                    hd = 2 * (i % 2) + hh
                    for t in range(TT):
                        ins = pe.matmul(ps[0:DK, 4 + i, T * hh + P * t:T * hh + P * (t + 1)],
                                        glog[:, d, t, DK * hd:DK * (hd + 1)], tri, start=True, stop=True)
                ins.then_inc(cum_done, 1)
            for i in range(4):
                d, t = i // 2, i % 2
                pe.wait_ge(kd_ready, d + 1)
                for hd in range(GH):
                    o = T * hd + P * t
                    ins = pe.transpose(ps[:, i, DK * hd:DK * (hd + 1)], bt[0:DK, d, o:o + P], ident[0:DK, 0:DK])
                ins.then_inc(kd_turned, 1)

            def state_products(i):
                for d in range(2):
                    for k in range(3):
                        n = k if d == 0 else 3 - k
                        r = slice(CH * (n % 2), CH * (n % 2) + CH)
                        ins = pe.matmul(STATE_PS(d, k), kdt[r, d, n // 2, DK * i:DK * (i + 1)],
                                        v1[r, n // 2, DV * i:DV * (i + 1)], start=True, stop=True)
                ins.then_inc(state_done, 1)

            def chunk_products(i):
                for t in range(TT):
                    for half in range(2):
                        o = T * i + P * t + CH * half
                        for d in range(2):
                            c0 = P * d + CH * t
                            ins = pe.matmul(ps[CH * half:CH * half + CH, 3 + i % 2, c0:c0 + CH],
                                            ke[0:DK, d, o:o + CH], qe[0:DK, d, o:o + CH], start=True, stop=True)
                ins.then_inc(at_done, 1)

            pe.wait_ge(qk_ready, 4)
            pe.wait_ge(kdt_ready, 4)
            state_products(0)
            chunk_products(0)
            for i in range(GH):
                if i + 1 < GH:
                    if i >= 1:
                        pe.wait_ge(at_ready, 4 * i)
                    chunk_products(i + 1)
                    pe.wait_ge(states_ready, 2 * (i + 1))
                    state_products(i + 1)
                pe.wait_ge(states_ready, 2 * (i + 1))
                pe.wait_ge(at_ready, 4 * (i + 1))
                if i >= 2:
                    pe.wait_ge(o_copied, i - 1)
                for t in range(TT):
                    c0 = DV * t
                    pe.matmul(ps[:, 6 + i % 2, c0:c0 + DV], at[:, i % 2, t, :], v1[:, t, DV * i:DV * (i + 1)],
                              start=True, stop=False, skip_group_check=True)
                    for half in range(2):
                        n = 2 * t + half
                        o = T * i + CH * n
                        for d, k in ((0, n - 1), (1, 2 - n)):
                            if 0 <= k <= 2:
                                ins = pe.matmul(ps[CH * half:CH * half + CH, 6 + i % 2, c0:c0 + DV],
                                                qe[0:DK, d, o:o + CH], states[0:DK, d, k, :],
                                                start=False, stop=True, skip_group_check=True)
                ins.then_inc(o_done, 1)
            pe.wait_ge(o_ready, 2 * GH)
            for b in range(3):
                for k in (2 * b, 2 * b + 1):
                    for t in range(TT):
                        o = T * (k % 2) + P * t
                        ins = pe.transpose(ps[:, b, o:o + P], o1[:, t, P * k:P * (k + 1)], ident)
                ins.then_inc(o_turned, 1)
            pe.wait_ge(mix_lo, 13)
            project_out(S_OUT1)
            turn(4)
            pe.wait_ge(xt_lo_ready, 20)
            pe.wait_ge(rt_cut, 2)
            for t in range(TT):
                for k in range(KD):
                    ins = mul3(ps[:, 0, E * t:E * (t + 1)], part(xt, k, tok[t]), part((rt_hi, rt_lo), k),
                               k == 0, k == KD - 1)
            ins.then_inc(logits_done, 1)
            pe.wait_ge(masks_ready, 1)
            before, ones = const("before"), const("ones")
            pe.matmul(ps[:, 1, 0:E], before, r_mask[:, 0, :], start=True, stop=True)
            for dst, second in ((slice(E, 2 * E), before), (slice(2 * E, 3 * E), ones)):
                pe.matmul(ps[:, 1, dst], ones, r_mask[:, 0, :], start=True, stop=False)
                ins = pe.matmul(ps[:, 1, dst], second, r_mask[:, 1, :], start=False, stop=True)
            ins.then_inc(ranks_done, 1)

            def gather(v):
                pe.wait_ge(pick_ready, v * 4 + 4)
                for b in range(2):
                    for k in range(4 * b, 4 * b + 4):
                        for t in range(TT):
                            ins = pe.matmul(ps[:, 2 + b, P * (k % 4):P * (k % 4 + 1)], xn[:, t, P * k:P * (k + 1)],
                                            pick[:, t, :], start=(t == 0), stop=(t == 1))
                    ins.then_inc(gathered, 1)

            gather(0)
            pe.wait_ge(units_ready, 1)
            n_more = pe.value_load(unit_i[0:1, 0:1], min_val=0, max_val=3)
            gx = (gx_hi, gx_lo)
            with pe.Fori(0, n_more + E) as u:
                def cut_slot(j, k):
                    pe.wait_ge(lo_ready, u * UNIT_SLOTS + (S_MOE + j + 1))
                    return [a[:, (S_MOE + j) % CUT, :].rearrange("p (k n) -> p k n", k=k) for a in (w_hi, w_lo)]

                def hidden(kind, c):
                    for half in range(2):
                        w = cut_slot(moe_slot(kind, c, half), 4)
                        for k4 in range(4):
                            k = 4 * half + k4
                            ins = mul3(ps[:, 2 * (c % 2) + (kind == "up"), :], part(gx, k), part(w, k4),
                                       k == 0, k == KD - 1)
                        ins.then_inc(slot_done, 1)

                def turn_hidden(i):
                    pe.wait_ge(hid_ready, u * NC + (i + 1))
                    if i >= 1:
                        pe.wait_ge(hT_lo_ready, u * NC + i)
                    for j in range(4):
                        ins = pe.transpose(ps[:, 4, P * j:P * (j + 1)], hid[:, i % 2, P * j:P * (j + 1)], ident)
                    ins.then_inc(hid_turned, 1)

                def down(i):
                    pe.wait_ge(hT_lo_ready, u * NC + (i + 1))
                    for half in range(2):
                        w = cut_slot(moe_slot("down", i, half), 2)
                        for k2 in range(2):
                            j = 2 * half + k2
                            for n in range(2):
                                ins = mul3(ps[:, 5 + n, :], part(hT, i % 2, slice(P * j, P * (j + 1))),
                                           part(w, k2, slice(512 * n, 512 * (n + 1))),
                                           i == 0 and j == 0, i == NC - 1 and j == 3)
                        ins.then_inc(slot_done, 1)

                pe.wait_ge(gx_lo_ready, u * 2 + 2)
                for c in range(NC):
                    if c >= 2:
                        pe.wait_ge(silu_ready, u * NC + (c - 1))
                    hidden("gate", c)
                    if c >= 1:
                        turn_hidden(c - 1)
                    if c >= 2:
                        pe.wait_ge(hid_ready, u * NC + (c - 1))
                    hidden("up", c)
                    if c >= 1:
                        down(c - 1)
                    if c == 3:
                        for t in range(TT):
                            ins = pe.transpose(ps[:, 7, P * t:P * (t + 1)], pick_w[:, t, :], ident)
                        ins.then_inc(pick_turned, 1)
                turn_hidden(NC - 1)
                gather(u + 1)
                down(NC - 1)
                pe.wait_ge(pickT_ready, u + 1)
                for q in range(4):
                    if q % 2 == 0:
                        pe.wait_ge(y_ready_a, u + 1)
                    else:
                        pe.wait_ge(y_ready_v, u + 1)
                    if q == 2:
                        pe.wait_ge(gx_lo_ready, u * 2 + 4)
                    pe.matmul(ps[:, q, :], pick_wT[:, q // 2, :], y_sb[:, 512 * (q % 2):512 * (q % 2) + 512],
                              start=True, stop=True).then_inc(scattered, 1)
                pe.wait_ge(h_added, u * 4 + 2)


def kernel(**inputs):
    import numpy as np
    import concourse.bacc as bacc
    from concourse.bass_utils import run_bass_kernel_spmd as run

    a = {k: np.ascontiguousarray(v) for k, v in inputs.items()}
    tables, col = shape_constants(np)
    arrays = {
        "tables": tables,
        "x": a["x"][0],
        "mem": a["mem"][0],
        "gains": np.stack([a["mem_norm"], a["even_norm1"][0], a["even_norm2"][0], a["odd_norm1"][0],
                           a["odd_norm2"][0], a["final_norm"]]),
        "rpb": np.ascontiguousarray(np.transpose(a["even_rpb"][0], (2, 0, 1))),
        "gate_aug": np.concatenate([
            np.concatenate([a["odd_w_gk_fwd"][0], a["odd_w_gk_bwd"][0]], 1),
            np.concatenate([a["odd_b_gk_fwd"][0], a["odd_b_gk_bwd"][0]])[None, :]], 0),
        "g_norm": a["odd_g_norm"],
        "router": a["odd_w_router"][0],
        "mem_kv": a["w_mem_kv"],
        "even_in": a["even_w_in"][0],
        "even_out": a["even_w_out"][0],
        "even_gate": a["even_w_gate"][0],
        "even_up": a["even_w_up"][0],
        "even_down": a["even_w_down"][0],
        "odd_in": a["odd_w_in"][0],
        "odd_out": a["odd_w_out"][0],
        "exp_gate": a["odd_w_gate"][0],
        "exp_up": a["odd_w_up"][0],
        "exp_down": a["odd_w_down"][0],
    }
    nc = bacc.Bacc("TRN2", target_bir_lowering=False, num_devices=1)
    args = [nc.dram_tensor(n, v.shape, mybir.dt.from_np(v.dtype), kind="ExternalInput").ap()
            for n, v in arrays.items()]
    args.append(nc.dram_tensor("out", (T, D), F32, kind="ExternalOutput").ap())
    build(nc, col, *args)
    r = run(nc, [arrays], core_ids=[0])
    return r.results[0]["out"].reshape(1, T, D)
```

```python
from contextlib import ExitStack

import concourse.bass as bass
from concourse import mybir

ALU = mybir.AluOpType
ACT = mybir.ActivationFunctionType
F32 = mybir.dt.float32
F32R = mybir.dt.float32r
I32 = mybir.dt.int32
AX_X = mybir.AxisListType.X

P = 128
D = 1024
T = 256
TT = T // P
KD = D // P
EPS = 1e-6
HEAD = 64
NA_HEADS, MEM_HEADS = 12, 4
GRID_W = 64
ROWS = T // GRID_W
RPB_R, RPB_C = 15, 31
SHIFT_W = 3 * GRID_W - 1
DR0 = 5
NDR = 6
GH, DK, DV = 4, 96, 192
KW, VW = GH * DK, GH * DV
CH = 64
NCH = T // CH
RANK = 16
D_FF = 2816
E = 8
FE = 3584
NEG = -1e30

RAW = 6
CUT = 3
SLOT = 2048

FF_W = 256
FF_N = D_FF // FF_W
FC = 512
NC = FE // FC
UNIT_SLOTS = 6 * NC
UNIT_LAND = 16 * UNIT_SLOTS // RAW
MAX_UNITS = E + 3
UCOLS = MAX_UNITS + 1

N_KV, N_IN0, N_OUT, N_FF, N_IN1 = 2, 10, 4, 3 * FF_N, 14
S_IN0 = N_KV
S_OUT0 = S_IN0 + N_IN0
S_FF = S_OUT0 + N_OUT
S_IN1 = S_FF + N_FF
S_OUT1 = S_IN1 + N_IN1
S_MOE = S_OUT1 + N_OUT
IN1_COLS = [(0, KW), (KW, KW)] + [(2 * KW + 384 * i, 384) for i in range(4)] + [(2 * KW + 2 * VW, 2 * RANK + 256)]


BY_TOKEN = [(t, n) for t in range(TT) for n in range(2)]
BY_HALF = [(t, n) for n in range(2) for t in range(TT)]
BIAS_A, BIAS_B, BIAS_GROUPS = 4, 6, -(-GRID_W // 7)


def slot_width(n):
    return 4 * IN1_COLS[(n - S_IN1) // 2][1] if S_IN1 <= n < S_OUT1 else SLOT


def ff_slot(kind, c):
    if kind == "down":
        return S_FF + (3 * (c + 1) + 1 if c + 1 < FF_N else 3 * FF_N - 1)
    return S_FF + (0 if c == 0 else 3 * c - 1) + (1 if kind == "up" else 0)


def mix_tile(item):
    return item // 2 if item < 16 else 6 + (item - 16) // 2


def shape_constants(np):
    i = np.arange(P)[:, None]
    j = np.arange(P)[None, :]
    same = (i // CH) == (j // CH)
    col = {}
    parts = []

    def put(name, a):
        full = np.zeros((P, a.shape[1]), np.float32)
        full[: a.shape[0]] = a
        col[name] = (sum(x.shape[1] for x in parts), a.shape[1])
        parts.append(full)

    put("ident", (i == j) * 1.0)
    put("tri_f", (same & (i <= j)) / 16.0)
    put("tri_b", (same & (i >= j)) / 16.0)
    put("strict_b", (same & (i > j)) * 1.0)
    put("before", (i < j) * 1.0)
    put("ones", np.ones((P, P)))
    put("iota", np.broadcast_to(np.arange(P), (P, P)))
    c = np.arange(P) % GRID_W
    start = np.clip(c - 8, 0, GRID_W - 16)[:, None]
    cc = np.arange(GRID_W)[None, :]
    put("col_mask", np.where((cc >= start) & (cc < start + 16), 0.0, NEG))
    x, dc = np.arange(SHIFT_W)[None, :], np.arange(RPB_C)[:, None]
    shifts = np.zeros((2, 2, 32, SHIFT_W), np.float32)
    shifts[:, 0, :RPB_C] = x + dc == 78
    shifts[:, 1, :RPB_C] = x + dc == 78 + GRID_W
    shifts = shifts.reshape(P, SHIFT_W)
    return np.concatenate(parts, 1), col, shifts


def moe_slot(kind, c, half):
    if kind == "down":
        return (4 + 6 * c + 4 if c + 1 < NC else 4 + 6 * c) + half
    base = 0 if c == 0 else 4 + 6 * (c - 1)
    return base + (2 if kind == "up" else 0) + half


def build(nc, col, tables, shifts, x, mem, gains, rpb, gate_aug, g_norm, router, mem_kv, even_in, even_out,
          even_gate, even_up, even_down, odd_in, odd_out, exp_gate, exp_up, exp_down, out):
    with ExitStack() as ctx:
        def sb(name, shape, dt=F32):
            return ctx.enter_context(nc.sbuf_tensor(name, shape, dt))

        def sem(name):
            return ctx.enter_context(nc.semaphore(name))

        ps = ctx.enter_context(nc.psum_tensor("ps", [P, 8, 512], F32))

        raw = sb("raw", [P, RAW, SLOT])
        w_hi = sb("w_hi", [P, CUT, SLOT], F32R)
        w_lo = sb("w_lo", [P, CUT, SLOT], F32R)
        h = sb("h", [P, TT, D])
        xn = sb("xn", [P, TT, D])
        xt_hi = sb("xt_hi", [P, KD, T], F32R)
        xt_lo = sb("xt_lo", [P, KD, T], F32R)
        hT_hi = sb("hT_hi", [P, 2, 512], F32R)
        hT_lo = sb("hT_lo", [P, 2, 512], F32R)
        gain = sb("gain", [P, D])
        cst = sb("cst", [P, max(a + n for a, n in col.values())])
        mkT = sb("mkT", [P, 2, T])
        mv = sb("mv", [P, 2, 256])
        ss = sb("ss", [P, 6 * TT, 2])
        rstd = sb("rstd", [P, 6 * TT])
        mhalf = sb("mhalf", [P, 8])
        stat = sb("stat", [P, 20, 2, 3])
        gnb = sb("gnb", [P, DV])
        rt_sb = sb("rt_sb", [P, KD, E])
        rt_hi = sb("rt_hi", [P, KD, E], F32R)
        rt_lo = sb("rt_lo", [P, KD, E], F32R)
        unit_i = sb("unit_i", [P, 4], I32)
        states = sb("states", [P, 2, 3, DV])
        ARENA = 13520
        arena = sb("arena", [P, ARENA])
        top = [0]

        def take(n):
            a = top[0]
            top[0] += n
            assert top[0] <= ARENA, top[0]
            return arena[:, a:a + n]

        def const(name, rows=P):
            a, n = col[name]
            return cst[0:rows, a:a + n]

        ident, iota = const("ident"), const("iota")

        qkT = take(14 * T).rearrange("p (i t) -> p i t", t=T)
        v0 = take(TT * 768).rearrange("p (t n) -> p t n", t=TT)
        bias = take(NA_HEADS * NDR * GRID_W).rearrange("p (x c) -> p x c", c=GRID_W)
        s_a = take(3 * 2 * T).rearrange("p (b t m) -> p b t m", b=3, t=2)
        pT_a = take(2 * 2 * T).rearrange("p (b j q) -> p b j q", b=2, j=2)
        rp_a = take(NA_HEADS * RPB_R).rearrange("p (h r) -> p h r", r=RPB_R)
        shift = take(SHIFT_W)
        shift_r = hT_hi[:, 0, 0:SHIFT_W]
        rp_cut = hT_lo[:, 0, 0:NA_HEADS * NDR].rearrange("p (h r) -> p h r", r=NDR)
        mem_sb = arena[:, 0:TT * D].rearrange("p (t d) -> p t d", t=TT)
        top[0] = 0
        qg = take(GH * T).rearrange("p (h t) -> p h t", h=GH)
        kg = take(GH * T).rearrange("p (h t) -> p h t", h=GH)
        v1 = take(TT * VW).rearrange("p (t n) -> p t n", t=TT)
        sg = take(TT * VW).rearrange("p (t n) -> p t n", t=TT)
        qm1 = take(2 * T).rearrange("p (i t) -> p i t", i=2)
        z_sb = take(TT * 32).rearrange("p (t n) -> p t n", t=TT)
        glog = take(2 * TT * KW).rearrange("p (d t n) -> p d t n", d=2, t=TT)
        kdt = glog
        bt = take(2 * GH * T).rearrange("p (d x) -> p d x", d=2)
        qe_at = top[0]
        qe = take(2 * GH * T).rearrange("p (d x) -> p d x", d=2)
        ke_at = top[0]
        ke = take(2 * GH * T).rearrange("p (d x) -> p d x", d=2)
        blast = take(2 * GH * NCH).rearrange("p (d n) -> p d n", d=2)
        decay = take(2 * GH * NCH).rearrange("p (d n) -> p d n", d=2)
        gss = take(3 * 2 * GH).rearrange("p (x n) -> p x n", x=3)
        junk = arena[:, qe_at - 2 * DV:qe_at].rearrange("p (b n) -> p b n", b=2)
        top[0] = qe_at
        s_b = take(3 * 2 * T).rearrange("p (b t m) -> p b t m", b=3, t=2)
        pT_b = states[:].rearrange("p d k n -> p (d k n)")[:, 0:4 * T].rearrange("p (b j q) -> p b j q", b=2, j=2)
        top[0] = ke_at
        gk_w = take(2 * KW)
        zT = take(2 * T).rearrange("p (d t) -> p d t", d=2)
        xn_flat = xn[:].rearrange("p t d -> p (t d)")
        o1 = xn_flat[:, 0:TT * VW].rearrange("p (t n) -> p t n", t=TT)
        at = xn_flat[:, TT * VW:TT * VW + 2 * TT * P].rearrange("p (b t s) -> p b t s", b=2, t=TT)
        top[0] = 0
        silu_sb = take(2 * 512).rearrange("p (b n) -> p b n", b=2)
        hid = take(2 * 512).rearrange("p (b n) -> p b n", b=2)
        y_sb = take(D)
        pick = take(TT * P).rearrange("p (t s) -> p t s", t=TT)
        pick_w = take(TT * P).rearrange("p (t s) -> p t s", t=TT)
        pick_wT = take(TT * P).rearrange("p (t s) -> p t s", t=TT)
        u_slot = take(TT * UCOLS).rearrange("p (t u) -> p t u", t=TT)
        u_wt = take(TT * UCOLS).rearrange("p (t u) -> p t u", t=TT)
        unit_f = take(4)
        r_at = top[0]
        gx_hi, gx_lo = xt_hi[:, :, 0:P], xt_lo[:, :, 0:P]

        def cum_ps(d):
            return ps[0:DK, 6 - 2 * d:8 - 2 * d, :].rearrange("p b (n c) -> p (b n) c", c=CH)

        def o_ps(i, t):
            return ps[:, 6 + i % 2, DV * t:DV * (t + 1)]

        def out_ps(first_bank, c, t):
            return ps[:, 4 + (first_bank + 2 * c + t) % 4, :]

        top[0] = r_at

        def by_expert():
            return take(TT * E).rearrange("p (t e) -> p t e", t=TT)

        r_logit, r_cand, r_one1, r_one2, r_rest, r_mask = (by_expert() for _ in range(6))
        r_m1, r_m2, r_idx, r_gap, r_gap_exp, r_w1, r_w2 = (take(TT) for _ in range(7))
        r_over, r_number = take(E), take(E)
        r_sel = take(3 * E).rearrange("p (j e) -> p j e", j=3)
        r_prod = take(3 * E).rearrange("p (j e) -> p j e", j=3)
        r_sum = take(3)

        def STATE_PS(d, k):
            bank, place = ((0, 0), (1, 0), (0, 1))[k] if d == 0 else ((1, 1), (2, 0), (5, 0))[k]
            return ps[0:DK, bank, DV * place:DV * (place + 1)]

        landed = [sem(f"landed_{r}") for r in range(RAW)]
        hi_ready, lo_ready, slot_done = sem("hi_ready"), sem("lo_ready"), sem("slot_done")
        tables_in, rpb_in, mem_in, x_in, gain_in = (
            sem("tables_in"), sem("rpb_in"), sem("mem_in"), sem("x_in"), sem("gain_in"))
        gnorm_in, router_in, gate_w_in, stored = (
            sem("gnorm_in"), sem("router_in"), sem("gate_w_in"), sem("stored"))
        half_ready, zT_ones, at_zeroed = sem("half_ready"), sem("zT_ones"), sem("at_zeroed")
        sumsq_ready, eps_added, rstd_ready, xn_ready = (
            sem("sumsq_ready"), sem("eps_added"), sem("rstd_ready"), sem("xn_ready"))
        turned, xt_hi_ready, xt_lo_ready = sem("turned"), sem("xt_hi_ready"), sem("xt_lo_ready")
        kv_copied_a, kv_copied_v = sem("kv_copied_a"), sem("kv_copied_v")
        rp_zeroed, rp_parts, bias_mm, bias_ready = sem("rp_zeroed"), sem("rp_parts"), sem("bias_mm"), sem("bias_ready")
        in0_copied_a, in0_copied_v = sem("in0_copied_a"), sem("in0_copied_v")
        scores_done, scores_max, probs_exp, probs_ready, probs_turned, probsT_ready, heads_done = (
            sem("scores_done"), sem("scores_max"), sem("probs_exp"), sem("probs_ready"),
            sem("probs_turned"), sem("probsT_ready"), sem("heads_done"))
        mix_hi, mix_lo, out_bank, out_added = sem("mix_hi"), sem("mix_lo"), sem("out_bank"), sem("out_added")
        ff_silu, ff_hid, ff_hi, ff_lo, ff_bank, ff_added = (
            sem("ff_silu"), sem("ff_hid"), sem("ff_hi"), sem("ff_lo"), sem("ff_bank"), sem("ff_added"))
        in1_copied_a, in1_copied_v = sem("in1_copied_a"), sem("in1_copied_v")
        zT_done, zT_ready, gate_done, gate_abs, gate_exp, gate_ln, gate_ready = (
            sem("zT_done"), sem("zT_ready"), sem("gate_done"), sem("gate_abs"), sem("gate_exp"),
            sem("gate_ln"), sem("gate_ready"))
        cum_done, blast_ready, decay_ready, exps_done, diff_ready, qk_ready = (
            sem("cum_done"), sem("blast_ready"), sem("decay_ready"),
            sem("exps_done"), sem("diff_ready"), sem("qk_ready"))
        kd_exp, kd_ready, kd_turned, kdt_ready = (
            sem("kd_exp"), sem("kd_ready"), sem("kd_turned"), sem("kdt_ready"))
        state_done, states_ready, at_done, at_ready, o_done, o_squared, o_ms, o_rstd, o_ready = (
            sem("state_done"), sem("states_ready"), sem("at_done"), sem("at_ready"), sem("o_done"),
            sem("o_squared"), sem("o_ms"), sem("o_rstd"), sem("o_ready"))
        sgn_ready, o_turned = sem("sgn_ready"), sem("o_turned")
        rt_cut = sem("rt_cut")
        dve_own = sem("dve_own")
        logits_done, gap_ready, gap_exp, masks_ready, ranks_done, units_ready = (
            sem("logits_done"), sem("gap_ready"), sem("gap_exp"), sem("masks_ready"),
            sem("ranks_done"), sem("units_ready"))
        silu_ready, hid_ready, hid_turned, hT_hi_ready, hT_lo_ready = (
            sem("silu_ready"), sem("hid_ready"), sem("hid_turned"), sem("hT_hi_ready"), sem("hT_lo_ready"))
        pick_ready, pick_turned, pickT_ready, gathered, gx_hi_ready, gx_lo_ready = (
            sem("pick_ready"), sem("pick_turned"), sem("pickT_ready"), sem("gathered"),
            sem("gx_hi_ready"), sem("gx_lo_ready"))
        y_ready_a, y_ready_v, scattered, h_added = (
            sem("y_ready_a"), sem("y_ready_v"), sem("scattered"), sem("h_added"))

        kp = "(k p) n -> p k n"
        block = ctx.enter_context(nc.Block())

        @block.sync
        def _(sp):
            def put(n, src):
                if n >= RAW:
                    sp.wait_ge(lo_ready, n - RAW + 1)
                k, width = src.shape[1], src.shape[2]
                sp.dma_start(raw[:, n % RAW, 0:k * width].rearrange("p (k n) -> p k n", k=k),
                             src).then_inc(landed[n % RAW], 16)

            def halves(n, w, c0, width):
                for half in range(2):
                    put(n + half, w.rearrange(kp, p=P)[:, 4 * half:4 * half + 4, c0:c0 + width])

            def next_gain(i):
                if i >= 1:
                    sp.wait_ge(xn_ready, 4 * i)
                sp.dma_start(gain[:], gains[i:i + 1, :].partition_broadcast(P)).then_inc(gain_in, 16)

            sp.dma_start(cst[:], tables).then_inc(tables_in, 16)
            sp.dma_start(shift, shifts).then_inc(rpb_in, 16)
            sp.wait_ge(rp_zeroed, 1)
            for q in (0, 64):
                sp.dma_start(rp_a[q:q + RPB_C], rpb).then_inc(rpb_in, 16)
                sp.dma_start(rp_a[q + 32:q + 32 + RPB_C, :, 1:RPB_R], rpb[:, :, 0:RPB_R - 1]).then_inc(rpb_in, 16)
            sp.dma_start(mem_sb, mem.rearrange("(t p) d -> p t d", p=P)).then_inc(mem_in, 16)
            next_gain(0)
            put(0, mem_kv.rearrange(kp, p=P)[:, 0:4, :])
            sp.dma_start(h[:], x.rearrange("(t p) d -> p t d", p=P)).then_inc(x_in, 16)
            put(1, mem_kv.rearrange(kp, p=P)[:, 4:8, :])
            halves(S_IN0, even_in, 0, 512)
            next_gain(1)
            sp.dma_start(rt_sb[:], router.rearrange(kp, p=P)).then_inc(router_in, 16)
            sp.dma_start(gnb[:], g_norm.partition_broadcast(P)).then_inc(gnorm_in, 16)
            for c in range(1, 5):
                halves(S_IN0 + 2 * c, even_in, 512 * c, 512)
            next_gain(2)
            for c in range(2):
                halves(S_OUT0 + 2 * c, even_out, 512 * c, 512)
            g3, u3, d3 = (w.rearrange(kp, p=P) for w in (even_gate, even_up, even_down))
            for c in range(FF_N + 1):
                if c < FF_N:
                    put(ff_slot("gate", c), g3[:, :, FF_W * c:FF_W * (c + 1)])
                    put(ff_slot("up", c), u3[:, :, FF_W * c:FF_W * (c + 1)])
                if c >= 1:
                    put(ff_slot("down", c - 1), d3[:, 2 * (c - 1):2 * c, :])
                if c == 3:
                    next_gain(3)
            for i, (c0, width) in enumerate(IN1_COLS):
                halves(S_IN1 + 2 * i, odd_in, c0, width)
                if i == 2:
                    sp.wait_ge(ff_added, 4)
                    sp.dma_start(gk_w[0:RANK + 1, :], gate_aug).then_inc(gate_w_in, 16)
                    next_gain(4)
            for c in range(2):
                halves(S_OUT1 + 2 * c, odd_out, 512 * c, 512)

            def expert_loads(base, e, count=UNIT_SLOTS):
                wg, wu, wd = (w[bass.ds(e, 1)].rearrange("e (k p) f -> p (e k) f", p=P)
                              for w in (exp_gate, exp_up, exp_down))
                src = {}
                for c in range(NC):
                    for half in range(2):
                        cols = slice(FC * c, FC * (c + 1))
                        src[moe_slot("gate", c, half)] = wg[:, 4 * half:4 * half + 4, cols]
                        src[moe_slot("up", c, half)] = wu[:, 4 * half:4 * half + 4, cols]
                        src[moe_slot("down", c, half)] = wd[:, 4 * c + 2 * half:4 * c + 2 * half + 2, :]
                for j in range(count):
                    r = (S_MOE + j) % RAW
                    sp.wait_ge(lo_ready, base + (S_MOE + j - RAW + 1))
                    sp.dma_start(raw[:, r, :].rearrange("p (k n) -> p k n", k=src[j].shape[1]),
                                 src[j]).then_inc(landed[r], 16)

            with sp.Fori(0, E) as u:
                expert_loads(u * UNIT_SLOTS, u)
            sp.wait_ge(units_ready, 1)
            n_more = sp.value_load(unit_i[0:1, 0:1], min_val=0, max_val=3)
            for i in range(MAX_UNITS - E):
                with sp.If(n_more > i):
                    e = sp.value_load(unit_i[0:1, 1 + i:2 + i], min_val=0, max_val=E - 1)
                    expert_loads((E + i) * UNIT_SLOTS, e)
            expert_loads((n_more + E) * UNIT_SLOTS, 0, count=CUT)
            next_gain(5)
            for t in range(TT):
                sp.wait_ge(xn_ready, 20 + 2 * (t + 1))
                sp.dma_start(out[P * t:P * (t + 1), :], xn[:, t, :]).then_inc(stored, 16)
            sp.wait_ge(stored, 16 * TT)

        @block.scalar
        def _(act):
            cut = [0]

            def high_to(last):
                while cut[0] <= last:
                    n = cut[0]
                    w = slot_width(n)
                    act.wait_ge(landed[n % RAW], 16 * (n // RAW + 1))
                    if n >= CUT:
                        act.wait_ge(slot_done, n - CUT + 1)
                    act.activation(w_hi[:, n % CUT, 0:w], raw[:, n % RAW, 0:w], ACT.Copy).then_inc(hi_ready, 1)
                    cut[0] += 1

            def products(n):
                high_to(n + CUT)
                act.wait_ge(slot_done, n + 1)

            def mean_squares(i, src, pieces):
                for t, n in pieces:
                    cols = slice(512 * n, 512 * (n + 1))
                    act.activation(xn[:, t, cols], src[:, t, cols], ACT.Square, scale=float(D) ** -0.5,
                                   accum_out=ss[:, TT * i + t, n:n + 1]).then_inc(sumsq_ready, 1)

            def turned_high(i):
                for b in range(4):
                    act.wait_ge(turned, 4 * i + b + 1)
                    act.activation(xt_hi[:, 2 * b:2 * b + 2, :],
                                   ps[:, b, :].rearrange("p (k t) -> p k t", k=2),
                                   ACT.Copy).then_inc(xt_hi_ready, 1)

            def attention(first, n, s, pT, steps):
                for step in steps:
                    if step < n:
                        i = first + step
                        act.wait_ge(scores_max, i + 1)
                        for t in range(2):
                            act.activation(s[:, i % 3, t, :], s[:, i % 3, t, :], ACT.Exp,
                                           bias=stat[:, i, t, 0:1],
                                           accum_out=stat[:, i, t, 1:2]).then_inc(probs_exp, 1)
                    if 2 <= step < n + 2:
                        i = first + step - 2
                        act.wait_ge(probs_turned, i + 1)
                        if step >= 4:
                            act.wait_ge(heads_done, i - 1)
                        act.activation(pT[:, i % 2].rearrange("p j q -> p (j q)"), ps[:, 2 + i % 2, :],
                                       ACT.Copy).then_inc(probsT_ready, 1)
                    if step >= 4 and step % 2 == 0:
                        i = first + step - 3
                        act.wait_ge(heads_done, i + 1)
                        act.activation(xt_hi[:, mix_tile(i), :], ps[:, 4 + i // 2 % 2, 0:T],
                                       ACT.Copy).then_inc(mix_hi, 1)

            act.wait_ge(mem_in, 16)
            mean_squares(0, mem_sb, BY_TOKEN)
            high_to(0)
            turned_high(0)
            act.wait_ge(x_in, 16)
            mean_squares(1, h, BY_TOKEN)
            high_to(2)
            act.wait_ge(slot_done, 2)
            for b in range(2):
                act.activation(mkT[:, b, :], ps[:, 4 + b, 0:T], ACT.Copy).then_inc(kv_copied_a, 1)
            turned_high(1)
            for c in range(5):
                products(S_IN0 + 2 * c)
                if c == 4:
                    attention(0, 16, s_a, pT_a, range(0, 2))
                if c < 4:
                    products(S_IN0 + 2 * c + 1)
                else:
                    act.wait_ge(slot_done, S_IN0 + 10)
                for i in range(2):
                    b = 4 * ((c + 1) % 2) + i
                    if c < 3:
                        dst, src = qkT[:, 4 * c + i, :], ps[:, b, 0:T]
                    elif c == 3:
                        dst, src = v0[:, 0, 256 * i:256 * (i + 1)], ps[:, b, 0:256]
                    else:
                        dst, src = v0[:, i, 512:768], ps[:, b, 0:256]
                    act.activation(dst, src, ACT.Copy).then_inc(in0_copied_a, 1)
            attention(0, 16, s_a, pT_a, range(2, 19))

            def norm_after_out(i, slot0, added):
                for c in range(2):
                    high_to(slot0 + 2 * c + 1 - c + CUT)
                    for t in range(TT):
                        act.wait_ge(out_added, added + 2 * c + t + 1)
                        mean_squares(i, h, [(t, c)])
                turned_high(i)

            norm_after_out(2, S_OUT0, 0)
            for c in range(FF_N):
                products(ff_slot("gate", c))
                if c >= 2:
                    act.wait_ge(ff_hid, c - 1)
                act.activation(silu_sb[:, c % 2, :], ps[:, 2 * (c % 2), :], ACT.Silu).then_inc(ff_silu, 1)
                high_to(ff_slot("up", c) + CUT)
                act.wait_ge(ff_hid, c + 1)
                if c >= 2:
                    act.wait_ge(slot_done, ff_slot("down", c - 2) + 1)
                act.activation(hT_hi[:, c % 2, :], hid[:, c % 2, :], ACT.Copy).then_inc(ff_hi, 1)
            high_to(S_IN1 - 2 + CUT)
            for q, piece in enumerate(BY_TOKEN):
                act.wait_ge(ff_added, q + 1)
                mean_squares(3, h, [piece])
            turned_high(3)
            products(S_IN1 + 1)
            for i in (0, 2):
                act.activation(qg[0:DK, i, :], ps[0:DK, 4 + i, 0:T], ACT.Copy,
                               scale=float(DK) ** -0.5).then_inc(in1_copied_a, 1)
            products(S_IN1 + 3)
            for i in (0, 2):
                act.activation(kg[0:DK, i, :], ps[0:DK, i, 0:T], ACT.Copy).then_inc(in1_copied_a, 1)
            for c in range(2):
                products(S_IN1 + 4 + 2 * c + 1)
                act.activation(v1[:, 0, 384 * c:384 * (c + 1)], ps[:, 4 + 2 * c, 0:384],
                               ACT.Copy).then_inc(in1_copied_a, 1)
            for c in range(2):
                products(S_IN1 + 8 + 2 * c + 1)
                for t in range(TT):
                    act.activation(sg[:, t, 384 * c:384 * (c + 1)], ps[:, 2 * c + t, 0:384],
                                   ACT.Silu).then_inc(in1_copied_a, 1)
            products(S_IN1 + 12)
            act.wait_ge(slot_done, S_IN1 + 14)
            for t in range(TT):
                act.activation(z_sb[:, t, :], ps[:, 4 + t, 0:32], ACT.Copy).then_inc(in1_copied_a, 1)
            attention(16, 4, s_b, pT_b, range(0, 2))
            for i in range(4):
                act.wait_ge(gate_done, i + 1)
                act.activation(glog[:, i // 2, i % 2, :], ps[:, 4 + i, 0:KW], ACT.Abs).then_inc(gate_abs, 1)
            for i in range(4):
                g = glog[:, i // 2, i % 2, :]
                act.wait_ge(gate_abs, i + 1)
                act.activation(g, g, ACT.Exp, scale=-1.0).then_inc(gate_exp, 1)
            attention(16, 4, s_b, pT_b, range(2, 4))
            for i in range(4):
                g = glog[:, i // 2, i % 2, :]
                act.wait_ge(gate_exp, i + 1)
                act.activation(g, g, ACT.Ln, bias=1.0).then_inc(gate_ln, 1)
            attention(16, 4, s_b, pT_b, range(4, 7))
            for d in range(2):
                act.wait_ge(diff_ready, d + 1)
                act.activation(bt[0:DK, d], bt[0:DK, d], ACT.Exp).then_inc(kd_exp, 1)
            for d in range(2):
                for dst, sign in ((qe, 1.0), (ke, -1.0)):
                    act.activation(dst[0:DK, d].rearrange("p (n c) -> p n c", c=CH), cum_ps(d), ACT.Exp,
                                   scale=sign).then_inc(exps_done, 1)
                act.activation(decay[0:DK, d], blast[0:DK, d], ACT.Exp).then_inc(decay_ready, 1)
            for i in range(4):
                act.wait_ge(kd_turned, i + 1)
                act.activation(kdt[:, i // 2, i % 2, :], ps[:, i, 0:KW], ACT.Copy).then_inc(kdt_ready, 1)
            high_to(S_IN1 + 13 + CUT)
            for i in range(GH):
                act.wait_ge(o_done, i + 1)
                for t in range(TT):
                    k = 2 * i + t
                    if k >= 2:
                        act.wait_ge(o_squared, k - 1)
                    act.activation(junk[:, k % 2, :], o_ps(i, t), ACT.Square,
                                   accum_out=gss[:, 0, k:k + 1]).then_inc(o_squared, 1)
            for b in range(3):
                act.wait_ge(o_turned, b + 1)
                act.activation(xt_hi[:, 2 * b:2 * b + 2, :],
                               ps[:, b, :].rearrange("p (k t) -> p k t", k=2), ACT.Copy).then_inc(mix_hi, 1)
            norm_after_out(4, S_OUT1, 4)
            high_to(S_MOE - 1 + CUT)
            act.wait_ge(gap_ready, 1)
            act.activation(r_gap_exp, r_gap, ACT.Exp).then_inc(gap_exp, 1)

            def gather_high(v):
                for b in range(2):
                    act.wait_ge(gathered, v * 2 + (b + 1))
                    act.activation(gx_hi[:, 4 * b:4 * b + 4, :],
                                   ps[:, 2 + b, :].rearrange("p (k t) -> p k t", k=4),
                                   ACT.Copy).then_inc(gx_hi_ready, 1)

            gather_high(0)
            act.wait_ge(units_ready, 1)
            n_more = act.value_load(unit_i[0:1, 0:1], min_val=0, max_val=3)
            with act.Fori(0, n_more + E) as u:
                done = [CUT]

                def high_unit(last):
                    while done[0] <= last:
                        n = S_MOE + done[0]
                        act.wait_ge(landed[n % RAW], u * UNIT_LAND + 16 * (n // RAW + 1))
                        act.wait_ge(slot_done, u * UNIT_SLOTS + (n - CUT + 1))
                        act.activation(w_hi[:, n % CUT, :], raw[:, n % RAW, :], ACT.Copy).then_inc(hi_ready, 1)
                        done[0] += 1

                def unit_products(j):
                    high_unit(j + CUT)
                    act.wait_ge(slot_done, u * UNIT_SLOTS + (S_MOE + j + 1))

                def hT_high(i):
                    act.wait_ge(hid_turned, u * NC + (i + 1))
                    if i >= 2:
                        act.wait_ge(slot_done, u * UNIT_SLOTS + (S_MOE + moe_slot("down", i - 2, 1) + 1))
                    act.activation(hT_hi[:, i % 2, :], ps[:, 4, :], ACT.Copy).then_inc(hT_hi_ready, 1)

                for c in range(NC):
                    unit_products(moe_slot("gate", c, 1))
                    if c >= 2:
                        act.wait_ge(hid_ready, u * NC + (c - 1))
                    act.activation(silu_sb[:, c % 2, :], ps[:, 2 * (c % 2), :], ACT.Silu).then_inc(silu_ready, 1)
                    if c >= 1:
                        hT_high(c - 1)
                    if c == 4:
                        act.wait_ge(pick_turned, u + 1)
                        act.activation(pick_wT.rearrange("p t s -> p (t s)"), ps[:, 7, 0:2 * P],
                                       ACT.Copy).then_inc(pickT_ready, 1)
                high_unit(UNIT_SLOTS - 1)
                hT_high(NC - 1)
                high_unit(moe_slot("down", NC - 2, 1) + CUT)
                gather_high(u + 1)
                high_unit(moe_slot("down", NC - 1, 0) + CUT)
                act.wait_ge(slot_done, u * UNIT_SLOTS + (S_MOE + UNIT_SLOTS))
                act.activation(y_sb[:, 0:512], ps[:, 5, :], ACT.Copy).then_inc(y_ready_a, 1)
                high_unit(UNIT_SLOTS - 1 + CUT)

            for q, piece in enumerate(BY_TOKEN):
                act.wait_ge(h_added, (n_more + (E - 1)) * 4 + (q + 1))
                mean_squares(5, h, [piece])

        @block.gpsimd
        def _(pool):
            nc.gpsimd.memset(rp_a, 0.0).then_inc(rp_zeroed, 1)
            nc.gpsimd.memset(mhalf[:], -0.5).then_inc(half_ready, 1)
            pool.wait_ge(half_ready, 1)

            def inverse_root(i, pieces):
                for t in range(TT):
                    k = TT * i + t
                    pool.wait_ge(sumsq_ready, 4 * i + pieces.index((t, 1)) + 1)
                    pool.tensor_scalar(ss[:, k, 0:1], ss[:, k, 0:1], ss[:, k, 1:2], EPS, ALU.add,
                                       ALU.add).then_inc(eps_added, 1)
                    pool.wait_ge(eps_added, k + 1)
                    pool.tensor_tensor(rstd[:, k:k + 1], ss[:, k, 0:1], mhalf[:, 0:1], ALU.pow
                                       ).then_inc(rstd_ready, 1)

            inverse_root(0, BY_TOKEN)
            inverse_root(1, BY_TOKEN)
            inverse_root(2, BY_HALF)
            inverse_root(3, BY_TOKEN)
            pool.wait_ge(ff_added, 4)
            nc.gpsimd.memset(zT[0:32], 1.0).then_inc(zT_ones, 1)
            pool.wait_ge(turned, 16)
            nc.gpsimd.memset(at, 0.0).then_inc(at_zeroed, 1)
            for i in range(GH):
                pool.wait_ge(o_squared, TT * (i + 1))
                k = slice(TT * i, TT * (i + 1))
                pool.tensor_scalar(gss[:, 1, k], gss[:, 0, k], 1.0 / DV, EPS, ALU.mult, ALU.add).then_inc(o_ms, 1)
                pool.wait_ge(o_ms, i + 1)
                pool.tensor_tensor(gss[:, 2, k], gss[:, 1, k], mhalf[:, 0:TT], ALU.pow).then_inc(o_rstd, 1)
            inverse_root(4, BY_HALF)
            inverse_root(5, BY_TOKEN)

        @block.vector
        def _(dve):
            cut = [0]
            own = [0]

            def mark(ins):
                ins.then_inc(dve_own, 1)
                own[0] += 1

            def settle():
                dve.wait_ge(dve_own, own[0])

            def low_to(last):
                while cut[0] <= last:
                    n = cut[0]
                    w = slot_width(n)
                    dve.wait_ge(hi_ready, n + 1)
                    dve.tensor_tensor(w_lo[:, n % CUT, 0:w], raw[:, n % RAW, 0:w],
                                      w_hi[:, n % CUT, 0:w].bitcast(F32), ALU.subtract).then_inc(lo_ready, 1)
                    cut[0] += 1

            def products(n):
                low_to(n + CUT)
                dve.wait_ge(slot_done, n + 1)

            def norm(i, src):
                dve.wait_ge(gain_in, 16 * (i + 1))
                for t, n in BY_TOKEN:
                    cols = slice(512 * n, 512 * (n + 1))
                    k = TT * i + t
                    dve.wait_ge(rstd_ready, k + 1)
                    dve.scalar_tensor_tensor(xn[:, t, cols], src[:, t, cols], rstd[:, k:k + 1], gain[:, cols],
                                             ALU.mult, ALU.mult).then_inc(xn_ready, 1)

            def turned_low(i):
                for b in range(4):
                    dve.wait_ge(xt_hi_ready, 4 * i + b + 1)
                    dve.tensor_tensor(xt_lo[:, 2 * b:2 * b + 2, :],
                                      ps[:, b, :].rearrange("p (k t) -> p k t", k=2),
                                      xt_hi[:, 2 * b:2 * b + 2, :].bitcast(F32),
                                      ALU.subtract).then_inc(xt_lo_ready, 1)

            def attention(first, n, s, pairs0, steps):
                for step in steps:
                    if step < n:
                        i = first + step
                        dve.wait_ge(scores_done, i + 1)
                        if step >= 3:
                            dve.wait_ge(probs_turned, i - 2)
                        for t in range(2):
                            src = ps[:, i % 2, T * t:T * (t + 1)]
                            if i < NA_HEADS:
                                x0 = i * NDR + 2 - 2 * t
                                mark(dve.scalar_tensor_tensor(
                                    s[:, i % 3, t, :], src, float(HEAD) ** -0.5,
                                    bias[:, x0:x0 + ROWS, :].rearrange("p x c -> p (x c)"), ALU.mult, ALU.add))
                            else:
                                mark(dve.tensor_scalar(s[:, i % 3, t, :], src, float(HEAD) ** -0.5, None, ALU.mult))
                        settle()
                        dve.tensor_reduce(stat[:, i, :, 0], s[:, i % 3], AX_X, ALU.max,
                                          negate=True).then_inc(scores_max, 1)
                    if 1 <= step <= n:
                        i = first + step - 1
                        dve.wait_ge(probs_exp, 2 * i + 2)
                        mark(dve.reciprocal(stat[:, i, :, 2], stat[:, i, :, 1]))
                        settle()
                        for t in range(2):
                            dve.tensor_scalar(s[:, i % 3, t, :], s[:, i % 3, t, :], stat[:, i, t, 2:3], None,
                                              ALU.mult).then_inc(probs_ready, 1)
                    if step >= 4 and step % 2 == 0:
                        i = first + step - 3
                        dve.wait_ge(mix_hi, pairs0 + step // 2 - 1)
                        dve.tensor_tensor(xt_lo[:, mix_tile(i), :], ps[:, 4 + i // 2 % 2, 0:T],
                                          xt_hi[:, mix_tile(i), :].bitcast(F32), ALU.subtract).then_inc(mix_lo, 1)

            def add_out(slot0, banks, first_bank):
                for c in range(2):
                    low_to(slot0 + 2 * c + CUT)
                    for t in range(TT):
                        if t == 0:
                            dve.wait_ge(out_bank, banks + c + 1)
                        else:
                            dve.wait_ge(slot_done, slot0 + 2 * c + 2)
                        hs = h[:, t, 512 * c:512 * (c + 1)]
                        dve.tensor_tensor(hs, hs, out_ps(first_bank, c, t), ALU.add).then_inc(out_added, 1)

            def bias_copy(g0, g1):
                for g in range(g0, g1):
                    n = min(7, GRID_W - 7 * g)
                    dve.wait_ge(bias_mm, g + 1)
                    dve.tensor_tensor(
                        bias[:, :, 7 * g:7 * g + n],
                        ps[:, 6 + g % 2, 0:72 * n].rearrange("p (c x) -> p x c", c=n),
                        const("col_mask")[:, 7 * g:7 * g + n].unsqueeze(1).broadcast_to([P, 72, n]),
                        ALU.add).then_inc(bias_ready, 1)

            dve.wait_ge(rpb_in, 5 * 16)
            dve.tensor_copy(rp_cut, rp_a[:, :, DR0:DR0 + NDR]).then_inc(rp_parts, 1)
            dve.tensor_copy(shift_r, shift).then_inc(rp_parts, 1)
            dve.wait_ge(rp_parts, 1)
            dve.tensor_tensor(rp_cut[64:], rp_a[64:, :, DR0:DR0 + NDR], rp_cut[64:].bitcast(F32),
                              ALU.subtract).then_inc(rp_parts, 1)
            dve.wait_ge(tables_in, 16)
            bias_copy(0, BIAS_A)
            norm(0, mem_sb)
            low_to(0)
            bias_copy(BIAS_A, BIAS_B)
            turned_low(0)
            low_to(1)
            norm(1, h)
            low_to(2)
            dve.wait_ge(slot_done, 2)
            for t in range(TT):
                dve.tensor_copy(mv[:, t, :], ps[:, 6 + t, 0:256]).then_inc(kv_copied_v, 1)
            turned_low(1)
            bias_copy(BIAS_B, BIAS_GROUPS)
            dve.wait_ge(router_in, 16)
            dve.tensor_copy(rt_hi[:], rt_sb[:]).then_inc(rt_cut, 1)
            dve.wait_ge(rt_cut, 1)
            dve.tensor_tensor(rt_lo[:], rt_sb[:], rt_hi[:].bitcast(F32), ALU.subtract).then_inc(rt_cut, 1)
            for c in range(5):
                products(S_IN0 + 2 * c)
                if c == 4:
                    attention(0, 16, s_a, 0, range(0, 2))
                if c < 4:
                    products(S_IN0 + 2 * c + 1)
                else:
                    dve.wait_ge(slot_done, S_IN0 + 10)
                for i in (2, 3):
                    b = 4 * ((c + 1) % 2) + i
                    if c < 3:
                        dst, src = qkT[:, 4 * c + i, :], ps[:, b, 0:T]
                    elif c == 3:
                        dst, src = v0[:, 1, 256 * (i - 2):256 * (i - 1)], ps[:, b, 0:256]
                    else:
                        dst, src = qkT[:, 12 + i - 2, :], ps[:, b, 0:T]
                    dve.tensor_copy(dst, src).then_inc(in0_copied_v, 1)
            attention(0, 16, s_a, 0, range(2, 19))
            add_out(S_OUT0, 0, 2)
            norm(2, h)
            turned_low(2)
            for c in range(FF_N):
                products(ff_slot("up", c))
                dve.wait_ge(ff_silu, c + 1)
                if c >= 2:
                    dve.wait_ge(ff_lo, c - 1)
                dve.tensor_tensor(hid[:, c % 2, :], silu_sb[:, c % 2, :], ps[:, 2 * (c % 2) + 1, :],
                                  ALU.mult).then_inc(ff_hid, 1)
                dve.wait_ge(ff_hi, c + 1)
                dve.tensor_tensor(hT_lo[:, c % 2, :], hid[:, c % 2, :], hT_hi[:, c % 2, :].bitcast(F32),
                                  ALU.subtract).then_inc(ff_lo, 1)
            low_to(S_IN1 - 2 + CUT)
            for q, (t, n) in enumerate(BY_TOKEN):
                if q < 3:
                    dve.wait_ge(ff_bank, q + 1)
                else:
                    dve.wait_ge(slot_done, S_IN1)
                hs = h[:, t, 512 * n:512 * (n + 1)]
                dve.tensor_tensor(hs, hs, ps[:, 4 + 2 * t + n, :], ALU.add).then_inc(ff_added, 1)
            norm(3, h)
            turned_low(3)
            products(S_IN1 + 1)
            for i in (1, 3):
                dve.tensor_scalar(qg[0:DK, i, :], ps[0:DK, 4 + i, 0:T], float(DK) ** -0.5, None,
                                  ALU.mult).then_inc(in1_copied_v, 1)
            products(S_IN1 + 3)
            for i in (1, 3):
                dve.tensor_copy(kg[0:DK, i, :], ps[0:DK, i, 0:T]).then_inc(in1_copied_v, 1)
            for c in range(2):
                products(S_IN1 + 4 + 2 * c + 1)
                dve.tensor_copy(v1[:, 1, 384 * c:384 * (c + 1)], ps[:, 4 + 2 * c + 1, 0:384]).then_inc(in1_copied_v, 1)
            products(S_IN1 + 11)
            low_to(S_IN1 + 12 + CUT)
            dve.wait_ge(slot_done, S_IN1 + 14)
            for i in range(2):
                dve.tensor_copy(qm1[:, i, :], ps[:, 6 + i, 0:T]).then_inc(in1_copied_v, 1)
            dve.wait_ge(zT_done, 1)
            dve.wait_ge(zT_ones, 1)
            dve.tensor_copy(zT[0:RANK], ps[0:RANK, 4, :].rearrange("p (d t) -> p d t", d=2)).then_inc(zT_ready, 1)
            attention(16, 4, s_b, 8, range(0, 4))
            for i in range(4):
                g = glog[:, i // 2, i % 2, :]
                dve.wait_ge(gate_ln, i + 1)
                dve.scalar_tensor_tensor(g, ps[:, 4 + i, 0:KW], 0.0, g, ALU.min, ALU.subtract
                                         ).then_inc(gate_ready, 1)
            attention(16, 4, s_b, 8, range(4, 7))
            for d in range(2):
                dve.wait_ge(cum_done, 2 * d + 2)
                dve.tensor_copy(blast[0:DK, d], cum_ps(d)[:, :, CH - 1 if d == 0 else 0]).then_inc(blast_ready, 1)
                dve.wait_ge(blast_ready, d + 1)
                dve.tensor_tensor(bt[0:DK, d].rearrange("p (n c) -> p n c", c=CH),
                                  blast[0:DK, d].unsqueeze(2).broadcast_to([DK, GH * NCH, CH]), cum_ps(d),
                                  ALU.subtract).then_inc(diff_ready, 1)
            for d in range(2):
                dve.wait_ge(kd_exp, d + 1)
                dve.tensor_tensor(bt[0:DK, d], bt[0:DK, d], kg[0:DK].rearrange("p h t -> p (h t)"),
                                  ALU.mult).then_inc(kd_ready, 1)
            for d in range(2):
                for x, (dst, src) in enumerate(((qe, qg), (ke, kg))):
                    dve.wait_ge(exps_done, 2 * d + x + 1)
                    dve.tensor_tensor(dst[0:DK, d], dst[0:DK, d], src[0:DK].rearrange("p h t -> p (h t)"),
                                      ALU.mult).then_inc(qk_ready, 1)
            dve.wait_ge(gnorm_in, 16)
            sg8 = sg.rearrange("p t (h n) -> p (t h) n", n=DV)
            dve.wait_ge(in1_copied_a, 12)
            dve.tensor_tensor(sg8, sg8, gnb[:].unsqueeze(1).broadcast_to([P, TT * GH, DV]),
                              ALU.mult).then_inc(sgn_ready, 1)
            low_to(S_IN1 + 13 + CUT)

            def o_norm(i):
                c = slice(DV * i, DV * (i + 1))
                dve.wait_ge(o_rstd, i + 1)
                for t in range(TT):
                    dve.scalar_tensor_tensor(o1[:, t, c], o_ps(i, t), gss[:, 2, TT * i + t:TT * i + t + 1],
                                             sg[:, t, c], ALU.mult, ALU.mult).then_inc(o_ready, 1)

            dve.wait_ge(decay_ready, 2)
            dve.wait_ge(at_zeroed, 1)
            mask_f = const("tri_f").bitcast(I32)
            mask_b = const("strict_b").bitcast(I32)
            for i in range(GH):
                dve.wait_ge(state_done, i + 1)
                if i >= 1:
                    dve.wait_ge(o_done, i)
                for d in range(2):
                    mark(dve.tensor_copy(states[0:DK, d, 0, :], STATE_PS(d, 0)))
                for k in (1, 2):
                    settle()
                    for d in range(2):
                        n = k if d == 0 else 3 - k
                        f = decay[0:DK, d, NCH * i + n:NCH * i + n + 1]
                        ins = dve.scalar_tensor_tensor(states[0:DK, d, k, :], states[0:DK, d, k - 1, :], f,
                                                       STATE_PS(d, k), ALU.mult, ALU.add)
                        if k == 1:
                            mark(ins)
                        else:
                            ins.then_inc(states_ready, 1)
                dve.wait_ge(at_done, i + 1)
                for half in range(2):
                    r = slice(CH * half, CH * (half + 1))
                    for d, mask in enumerate((mask_f, mask_b)):
                        dve.copy_predicated(
                            at[r, i % 2, :, r], mask[r, r].unsqueeze(1).broadcast_to([CH, TT, CH]),
                            ps[r, 3 + i % 2, P * d:P * (d + 1)].rearrange("p (t c) -> p t c", t=TT)
                        ).then_inc(at_ready, 1)
                        if d == 0:
                            dve.wait_ge(at_ready, 4 * i + 2 * half + 1)
                if i >= 1:
                    dve.wait_ge(sgn_ready, 1)
                    o_norm(i - 1)
            o_norm(GH - 1)
            for b in range(3):
                dve.wait_ge(mix_hi, 10 + b + 1)
                dve.tensor_tensor(xt_lo[:, 2 * b:2 * b + 2, :], ps[:, b, :].rearrange("p (k t) -> p k t", k=2),
                                  xt_hi[:, 2 * b:2 * b + 2, :].bitcast(F32), ALU.subtract).then_inc(mix_lo, 1)
            add_out(S_OUT1, 2, 0)
            norm(4, h)
            turned_low(4)
            low_to(S_MOE - 1 + CUT)

            i8 = iota[:, 0:E]

            def over_t(a, n=E):
                return a.unsqueeze(1).broadcast_to([P, TT, n])

            def over_e(a):
                return a.unsqueeze(2).broadcast_to([P, TT, E])

            def first_of_largest(src, m, cand, idx, onehot):
                mark(dve.tensor_reduce(m, src, AX_X, ALU.max))
                settle()
                mark(dve.tensor_tensor(cand, src, over_e(m), ALU.is_equal))
                settle()
                mark(dve.scalar_tensor_tensor(cand, cand, -100.0, over_t(i8), ALU.mult, ALU.add))
                settle()
                mark(dve.tensor_reduce(idx, cand, AX_X, ALU.min))
                settle()
                mark(dve.tensor_tensor(onehot, cand, over_e(idx), ALU.is_equal))
                settle()

            dve.wait_ge(logits_done, 1)
            mark(dve.tensor_copy(r_logit, ps[:, 0, 0:TT * E].rearrange("p (t e) -> p t e", t=TT)))
            settle()
            first_of_largest(r_logit, r_m1, r_cand, r_idx, r_one1)
            mark(dve.scalar_tensor_tensor(r_rest, r_one1, NEG, r_logit, ALU.mult, ALU.add))
            settle()
            first_of_largest(r_rest, r_m2, r_cand, r_idx, r_one2)
            dve.tensor_tensor(r_gap, r_m2, r_m1, ALU.subtract).then_inc(gap_ready, 1)
            dve.tensor_tensor(r_mask, r_one1, r_one2, ALU.add).then_inc(masks_ready, 1)
            mark(dve.memset(u_slot, -1.0))
            mark(dve.memset(u_wt, 0.0))
            dve.wait_ge(gap_exp, 1)
            mark(dve.tensor_scalar(r_w1, r_gap_exp, 1.0, None, ALU.add))
            settle()
            mark(dve.reciprocal(r_w1, r_w1))
            settle()
            mark(dve.tensor_tensor(r_w2, r_gap_exp, r_w1, ALU.mult))
            settle()
            mark(dve.tensor_tensor(r_one1, r_one1, over_e(r_w1), ALU.mult))
            mark(dve.tensor_tensor(r_one2, r_one2, over_e(r_w2), ALU.mult))
            settle()
            mark(dve.tensor_tensor(u_wt[:, :, 0:E], r_one1, r_one2, ALU.add))
            dve.wait_ge(ranks_done, 1)
            dve.wait_ge(masks_ready, 1)
            mark(dve.scalar_tensor_tensor(r_cand, ps[:, 1, 0:TT * E].rearrange("p (t e) -> p t e", t=TT), 1.0,
                                          r_mask, ALU.add, ALU.mult))
            settle()
            mark(dve.tensor_scalar(u_slot[:, :, 0:E], r_cand, -1.0, None, ALU.add))
            def build_picks(v):
                for t in range(TT):
                    place, wt = u_slot[:, t, bass.ds(v, 1)], u_wt[:, t, bass.ds(v, 1)]
                    dve.tensor_scalar(pick[:, t, :], iota, place, None, ALU.is_equal).then_inc(pick_ready, 1)
                    dve.tensor_scalar(pick_w[:, t, :], iota, place, wt, ALU.is_equal, ALU.mult
                                      ).then_inc(pick_ready, 1)

            def gather_low(v):
                for b in range(2):
                    dve.wait_ge(gx_hi_ready, v * 2 + (b + 1))
                    dve.tensor_tensor(gx_lo[:, 4 * b:4 * b + 4, :],
                                      ps[:, 2 + b, :].rearrange("p (k t) -> p k t", k=4),
                                      gx_hi[:, 4 * b:4 * b + 4, :].bitcast(F32), ALU.subtract
                                      ).then_inc(gx_lo_ready, 1)

            settle()
            build_picks(0)
            mark(dve.tensor_scalar(r_over, ps[:, 1, TT * E:TT * E + E], float(P), None, ALU.is_gt))
            settle()
            mark(dve.tensor_tensor_scan(r_number, const("ones")[:, 0:E], r_over, 0.0, ALU.mult, ALU.add))
            settle()
            for j in range(3):
                mark(dve.scalar_tensor_tensor(r_sel[:, j, :], r_number, float(j + 1), r_over,
                                              ALU.is_equal, ALU.mult))
            settle()
            for dst, vals, off in ([(unit_f[:, 1:4], i8, 0.0)]
                                   + [(u_slot[:, t, E:E + 3], u_slot[:, t, 0:E], -float(P)) for t in range(TT)]
                                   + [(u_wt[:, t, E:E + 3], u_wt[:, t, 0:E], 0.0) for t in range(TT)]):
                mark(dve.tensor_tensor(r_prod, r_sel, vals.unsqueeze(1).broadcast_to([P, 3, E]), ALU.mult))
                settle()
                mark(dve.tensor_reduce(r_sum, r_prod, AX_X, ALU.add))
                settle()
                mark(dve.tensor_scalar(dst, r_sum, off, None, ALU.add))
                settle()
            mark(dve.tensor_copy(unit_f[:, 0:1], r_number[:, E - 1:E]))
            settle()
            dve.tensor_copy(unit_i[:], unit_f).then_inc(units_ready, 1)

            gather_low(0)
            dve.wait_ge(units_ready, 1)
            n_more = dve.value_load(unit_i[0:1, 0:1], min_val=0, max_val=3)
            with dve.Fori(0, n_more + E) as u:
                done = [CUT]

                def low_unit(last):
                    while done[0] <= last:
                        n = S_MOE + done[0]
                        dve.wait_ge(hi_ready, u * UNIT_SLOTS + (n + 1))
                        dve.tensor_tensor(w_lo[:, n % CUT, :], raw[:, n % RAW, :],
                                          w_hi[:, n % CUT, :].bitcast(F32), ALU.subtract).then_inc(lo_ready, 1)
                        done[0] += 1

                def unit_products(j):
                    low_unit(j + CUT)
                    dve.wait_ge(slot_done, u * UNIT_SLOTS + (S_MOE + j + 1))

                def hT_low(i):
                    dve.wait_ge(hT_hi_ready, u * NC + (i + 1))
                    dve.tensor_tensor(hT_lo[:, i % 2, :], ps[:, 4, :], hT_hi[:, i % 2, :].bitcast(F32),
                                      ALU.subtract).then_inc(hT_lo_ready, 1)

                for c in range(NC):
                    if c >= 1:
                        low_unit(moe_slot("gate", c, 1) + CUT)
                        hT_low(c - 1)
                    unit_products(moe_slot("up", c, 1))
                    dve.wait_ge(silu_ready, u * NC + (c + 1))
                    dve.tensor_tensor(hid[:, c % 2, :], silu_sb[:, c % 2, :], ps[:, 2 * (c % 2) + 1, :],
                                      ALU.mult).then_inc(hid_ready, 1)
                    if c == 5:
                        dve.wait_ge(pick_turned, u + 1)
                        build_picks(u + 1)
                low_unit(UNIT_SLOTS - 1)
                hT_low(NC - 1)
                low_unit(moe_slot("down", NC - 2, 1) + CUT)
                gather_low(u + 1)
                low_unit(moe_slot("down", NC - 1, 0) + CUT)
                dve.wait_ge(slot_done, u * UNIT_SLOTS + (S_MOE + UNIT_SLOTS))
                dve.tensor_copy(y_sb[:, 512:1024], ps[:, 6, :]).then_inc(y_ready_v, 1)
                for q in range(4):
                    hs = h[:, q // 2, 512 * (q % 2):512 * (q % 2) + 512]
                    dve.wait_ge(scattered, u * 4 + (q + 1))
                    dve.tensor_tensor(hs, hs, ps[:, q, :], ALU.add).then_inc(h_added, 1)
                    if q == 1:
                        low_unit(UNIT_SLOTS - 1 + CUT)
            norm(5, h)

        @block.tensor
        def _(pe):
            def mul3(dst, a, b, start, stop):
                pe.matmul(dst, a[0], b[0], start=start, stop=False)
                pe.matmul(dst, a[0], b[1], start=False, stop=False)
                return pe.matmul(dst, a[1], b[0], start=False, stop=stop)

            def slot(n, k):
                w = slot_width(n)
                return [a[:, n % CUT, 0:w].rearrange("p (k n) -> p k n", k=k) for a in (w_hi, w_lo)]

            def part(pair, *idx):
                return [a[(slice(None),) + idx] for a in pair]

            xt = (xt_hi, xt_lo)
            hT = (hT_hi, hT_lo)

            def turn(i):
                for t in range(TT):
                    for k in range(KD):
                        if k % 4 == 0:
                            pe.wait_ge(xn_ready, 4 * i + 2 * t + k // 4 + 1)
                        o = T * (k % 2) + P * t
                        ins = pe.transpose(ps[:, k // 2, o:o + P], xn[:, t, P * k:P * (k + 1)], ident)
                        if t == 1 and k % 2 == 1:
                            ins.then_inc(turned, 1)

            def project(n0, groups, fresh=None, bank_done=None, halves=range(2)):
                for half in halves:
                    n = n0 + half
                    w = slot(n, 4)
                    pe.wait_ge(lo_ready, n + 1)
                    if fresh is not None:
                        pe.wait_ge(*fresh[half])
                    for g, (dst, form, tok, cols) in enumerate(groups):
                        for k4 in range(4):
                            k = 4 * half + k4
                            a = part(w, k4, cols)
                            b = part(xt, k, tok)
                            if form == "by token":
                                a, b = b, a
                            ins = mul3(dst, a, b, k == 0, k == KD - 1)
                        if bank_done is not None and half == 1 and g < len(groups) - 1:
                            ins.then_inc(bank_done, 1)
                    ins.then_inc(slot_done, 1)

            all_t = slice(0, T)
            tok = [slice(P * t, P * (t + 1)) for t in range(TT)]

            def norm_halves(i):
                return [(xt_lo_ready, 4 * i + 2), (xt_lo_ready, 4 * i + 4)]

            def attention(first, n, pT, q_of, k_of, v_of, pairs0, steps):
                for step in steps:
                    if step < n:
                        i = first + step
                        r = slice(HEAD * (i % 2), HEAD * (i % 2) + HEAD)
                        if step >= 2:
                            pe.wait_ge(scores_max, i - 1)
                        for t in range(TT):
                            ins = pe.matmul(ps[:, i % 2, T * t:T * (t + 1)], q_of(i)[r, tok[t]], k_of(i)[r, :],
                                            start=True, stop=True)
                        ins.then_inc(scores_done, 1)
                    if 2 <= step < n + 2:
                        i = first + step - 2
                        pe.wait_ge(probs_ready, 2 * i + 2)
                        if step >= 4:
                            pe.wait_ge(probsT_ready, i - 1)
                        s = s_a if first == 0 else s_b
                        for t in range(TT):
                            for j in range(2):
                                o = T * j + P * t
                                ins = pe.transpose(ps[:, 2 + i % 2, o:o + P], s[:, i % 3, t, P * j:P * (j + 1)],
                                                   ident)
                        ins.then_inc(probs_turned, 1)
                    if step >= 3:
                        i = first + step - 3
                        r = slice(HEAD * (i % 2), HEAD * (i % 2) + HEAD)
                        pe.wait_ge(probsT_ready, i + 1)
                        if first == 16 and i % 2 == 0:
                            pe.wait_ge(gate_ready, (i - first) // 2 + 1)
                        if step >= 7 and i % 2 == 0:
                            pe.wait_ge(mix_lo, pairs0 + (i - first) // 2 - 1)
                        for j in range(2):
                            ins = pe.matmul(ps[r, 4 + i // 2 % 2, 0:T], v_of(i, j), pT[:, i % 2, j, :],
                                            start=(j == 0), stop=(j == 1))
                        ins.then_inc(heads_done, 1)

            def bias_products(g0, g1):
                for g in range(g0, g1):
                    if g >= 2:
                        pe.wait_ge(bias_ready, g - 1)
                    for cc in range(min(7, GRID_W - 7 * g)):
                        c = 7 * g + cc
                        ins = pe.matmul(ps[:, 6 + g % 2, 72 * cc:72 * cc + 72], shift_r[:, 63 - c:191 - c], rp_cut,
                                        start=True, stop=True)
                    ins.then_inc(bias_mm, 1)

            pe.wait_ge(tables_in, 16)
            pe.wait_ge(rp_parts, 3)
            bias_products(0, BIAS_A)
            turn(0)
            bias_products(BIAS_A, BIAS_B)
            pe.wait_ge(bias_ready, BIAS_B)
            project(0, [(ps[:, 4 + i, 0:T], "by feature", all_t, slice(P * i, P * (i + 1))) for i in range(2)]
                    + [(ps[:, 6 + t, 0:256], "by token", tok[t], slice(256, 512)) for t in range(TT)], fresh=norm_halves(0))
            turn(1)
            pe.wait_ge(kv_copied_v, 2)
            bias_products(BIAS_B, BIAS_GROUPS)
            attention0 = (0, 16, pT_a,
                          lambda i: qkT[:, i // 2 if i < 12 else 12 + (i - 12) // 2, :],
                          lambda i: qkT[:, 6 + i // 2, :] if i < 12 else mkT[:, (i - 12) // 2, :],
                          lambda i, j: v0[:, j, HEAD * i:HEAD * (i + 1)] if i < 12
                          else mv[:, j, HEAD * (i - 12):HEAD * (i - 11)], 0)
            pe.wait_ge(kv_copied_a, 2)
            pe.wait_ge(bias_ready, BIAS_GROUPS)
            for c in range(5):
                if c >= 2:
                    pe.wait_ge(in0_copied_a, 2 * (c - 1))
                    pe.wait_ge(in0_copied_v, 2 * (c - 1))
                b = 4 * ((c + 1) % 2)
                if c < 3:
                    gs = [(ps[:, b + i, 0:T], "by feature", all_t, slice(P * i, P * (i + 1))) for i in range(4)]
                elif c == 3:
                    gs = [(ps[:, b + i, 0:256], "by token", tok[i // 2], slice(256 * (i % 2), 256 * (i % 2) + 256))
                          for i in range(4)]
                else:
                    gs = [(ps[:, b + t, 0:256], "by token", tok[t], slice(0, 256)) for t in range(TT)]
                    gs += [(ps[:, b + 2 + i, 0:T], "by feature", all_t, slice(256 + P * i, 256 + P * (i + 1)))
                           for i in range(2)]
                project(S_IN0 + 2 * c, gs, fresh=norm_halves(1) if c == 0 else None, halves=range(1) if c == 4 else range(2))
            pe.wait_ge(in0_copied_a, 8)
            pe.wait_ge(in0_copied_v, 8)
            attention(*attention0, range(0, 2))
            project(S_IN0 + 8, gs, halves=range(1, 2))
            pe.wait_ge(in0_copied_a, 10)
            pe.wait_ge(in0_copied_v, 10)
            attention(*attention0, range(2, 19))

            def project_out(slot0, first_bank, fresh):
                for c in range(2):
                    project(slot0 + 2 * c, [(out_ps(first_bank, c, t), "by token", tok[t], slice(0, 512))
                                            for t in range(TT)], fresh=fresh if c == 0 else None,
                            bank_done=out_bank)

            project_out(S_OUT0, 2, [(mix_lo, 4), (mix_lo, 8)])
            turn(2)
            for c in range(FF_N + 1):
                if c < FF_N:
                    for kind in ("gate", "up"):
                        n = ff_slot(kind, c)
                        w = slot(n, KD)
                        pe.wait_ge(lo_ready, n + 1)
                        if c >= 2:
                            pe.wait_ge(ff_silu if kind == "gate" else ff_hid, c - 1)
                        for j in range(2):
                            for k in range(KD):
                                if n == S_FF and j == 0 and k % 2 == 0:
                                    pe.wait_ge(xt_lo_ready, 8 + k // 2 + 1)
                                ins = mul3(ps[:, 2 * (c % 2) + (kind == "up"), T * j:T * (j + 1)],
                                           part(w, k, slice(P * j, P * (j + 1))), part(xt, k, all_t),
                                           k == 0, k == KD - 1)
                        ins.then_inc(slot_done, 1)
                if c >= 1:
                    i = c - 1
                    n = ff_slot("down", i)
                    w = slot(n, 2)
                    pe.wait_ge(lo_ready, n + 1)
                    pe.wait_ge(ff_lo, i + 1)
                    for t in range(TT):
                        for half in range(2):
                            for j in range(2):
                                ins = mul3(ps[:, 4 + 2 * t + half, :],
                                           part(hT, i % 2, slice(T * j + P * t, T * j + P * (t + 1))),
                                           part(w, j, slice(512 * half, 512 * (half + 1))),
                                           i == 0 and j == 0, i == FF_N - 1 and j == 1)
                            if i == FF_N - 1 and (t, half) != BY_TOKEN[-1]:
                                ins.then_inc(ff_bank, 1)
                    ins.then_inc(slot_done, 1)
            turn(3)
            for part_i, b0 in ((0, 4), (1, 0)):
                project(S_IN1 + 2 * part_i,
                        [(ps[0:DK, b0 + i, 0:T], "by feature", all_t, slice(DK * i, DK * (i + 1)))
                         for i in range(GH)], fresh=norm_halves(3) if part_i == 0 else None)
            for c in range(4):
                b0 = (4 + 2 * c) % 8
                pe.wait_ge(in1_copied_a, 2 if c < 2 else 4)
                pe.wait_ge(in1_copied_v, 2 if c < 2 else 4)
                project(S_IN1 + 4 + 2 * c, [(ps[:, b0 + t, 0:384], "by token", tok[t], slice(0, 384))
                                            for t in range(TT)])
            pe.wait_ge(in1_copied_a, 6)
            pe.wait_ge(in1_copied_v, 6)
            project(S_IN1 + 12,
                    [(ps[:, 4 + t, 0:2 * RANK], "by token", tok[t], slice(0, 2 * RANK)) for t in range(TT)]
                    + [(ps[:, 6 + i, 0:T], "by feature", all_t, slice(32 + P * i, 32 + P * (i + 1)))
                       for i in range(2)])
            pe.wait_ge(in1_copied_a, 12)
            pe.wait_ge(in1_copied_v, 8)
            for d in range(2):
                for t in range(TT):
                    ins = pe.matmul(ps[0:RANK, 4, T * d + P * t:T * d + P * (t + 1)],
                                    z_sb[:, t, RANK * d:RANK * (d + 1)], ident, start=True, stop=True)
            ins.then_inc(zT_done, 1)
            attention1 = (16, 4, pT_b, lambda i: qm1[:, (i - 16) // 2, :], lambda i: mkT[:, (i - 16) // 2, :],
                          lambda i, j: mv[:, j, HEAD * (i - 16):HEAD * (i - 15)], 8)
            attention(*attention1, range(0, 2))
            pe.wait_ge(zT_ready, 1)
            pe.wait_ge(gate_w_in, 16)
            for i in range(4):
                d, t = i // 2, i % 2
                pe.matmul(ps[:, 4 + i, 0:KW], zT[0:RANK + 1, d, tok[t]], gk_w[0:RANK + 1, KW * d:KW * (d + 1)],
                          start=True, stop=True).then_inc(gate_done, 1)
            attention(*attention1, range(2, 6))
            pe.wait_ge(gate_ready, 4)
            for i in range(4):
                d = i // 2
                if i == 2:
                    attention(*attention1, range(6, 7))
                    pe.wait_ge(mix_lo, 10)
                tri = const("tri_f" if d == 0 else "tri_b")
                for hh in range(2):
                    hd = 2 * (i % 2) + hh
                    for t in range(TT):
                        ins = pe.matmul(ps[0:DK, 6 - 2 * d + i % 2, T * hh + P * t:T * hh + P * (t + 1)],
                                        glog[:, d, t, DK * hd:DK * (hd + 1)], tri, start=True, stop=True)
                ins.then_inc(cum_done, 1)
            for i in range(4):
                d, t = i // 2, i % 2
                pe.wait_ge(kd_ready, d + 1)
                for hd in range(GH):
                    o = T * hd + P * t
                    ins = pe.transpose(ps[:, i, DK * hd:DK * (hd + 1)], bt[0:DK, d, o:o + P], ident[0:DK, 0:DK])
                ins.then_inc(kd_turned, 1)

            def state_products(i):
                for d in range(2):
                    for k in range(3):
                        n = k if d == 0 else 3 - k
                        r = slice(CH * (n % 2), CH * (n % 2) + CH)
                        ins = pe.matmul(STATE_PS(d, k), kdt[r, d, n // 2, DK * i:DK * (i + 1)],
                                        v1[r, n // 2, DV * i:DV * (i + 1)], start=True, stop=True)
                ins.then_inc(state_done, 1)

            def chunk_products(i):
                for t in range(TT):
                    for half in range(2):
                        o = T * i + P * t + CH * half
                        for d in range(2):
                            c0 = P * d + CH * t
                            ins = pe.matmul(ps[CH * half:CH * half + CH, 3 + i % 2, c0:c0 + CH],
                                            ke[0:DK, d, o:o + CH], qe[0:DK, d, o:o + CH], start=True, stop=True)
                ins.then_inc(at_done, 1)

            pe.wait_ge(qk_ready, 4)
            pe.wait_ge(kdt_ready, 4)
            state_products(0)
            chunk_products(0)
            for i in range(GH):
                if i + 1 < GH:
                    if i >= 1:
                        pe.wait_ge(at_ready, 4 * i)
                    chunk_products(i + 1)
                    pe.wait_ge(states_ready, 2 * (i + 1))
                    state_products(i + 1)
                pe.wait_ge(states_ready, 2 * (i + 1))
                pe.wait_ge(at_ready, 4 * (i + 1))
                if i >= 2:
                    pe.wait_ge(o_ready, TT * (i - 1))
                for t in range(TT):
                    c0 = DV * t
                    pe.matmul(ps[:, 6 + i % 2, c0:c0 + DV], at[:, i % 2, t, :], v1[:, t, DV * i:DV * (i + 1)],
                              start=True, stop=False, skip_group_check=True)
                    for half in range(2):
                        n = 2 * t + half
                        o = T * i + CH * n
                        for d, k in ((0, n - 1), (1, 2 - n)):
                            if 0 <= k <= 2:
                                ins = pe.matmul(ps[CH * half:CH * half + CH, 6 + i % 2, c0:c0 + DV],
                                                qe[0:DK, d, o:o + CH], states[0:DK, d, k, :],
                                                start=False, stop=True, skip_group_check=True)
                ins.then_inc(o_done, 1)
            for b in range(3):
                pe.wait_ge(o_ready, TT * (b + 2))
                for k in (2 * b, 2 * b + 1):
                    for t in range(TT):
                        o = T * (k % 2) + P * t
                        ins = pe.transpose(ps[:, b, o:o + P], o1[:, t, P * k:P * (k + 1)], ident)
                ins.then_inc(o_turned, 1)
            project_out(S_OUT1, 0, [(mix_lo, 12), (mix_lo, 13)])
            turn(4)
            pe.wait_ge(rt_cut, 2)
            for t in range(TT):
                for k in range(KD):
                    if t == 0 and k % 2 == 0:
                        pe.wait_ge(xt_lo_ready, 16 + k // 2 + 1)
                    ins = mul3(ps[:, 0, E * t:E * (t + 1)], part(xt, k, tok[t]), part((rt_hi, rt_lo), k),
                               k == 0, k == KD - 1)
            ins.then_inc(logits_done, 1)
            pe.wait_ge(masks_ready, 1)
            before, ones = const("before"), const("ones")
            pe.matmul(ps[:, 1, 0:E], before, r_mask[:, 0, :], start=True, stop=True)
            for dst, second in ((slice(E, 2 * E), before), (slice(2 * E, 3 * E), ones)):
                pe.matmul(ps[:, 1, dst], ones, r_mask[:, 0, :], start=True, stop=False)
                ins = pe.matmul(ps[:, 1, dst], second, r_mask[:, 1, :], start=False, stop=True)
            ins.then_inc(ranks_done, 1)

            def gather(v):
                pe.wait_ge(pick_ready, v * 4 + 4)
                for b in range(2):
                    for k in range(4 * b, 4 * b + 4):
                        for t in range(TT):
                            ins = pe.matmul(ps[:, 2 + b, P * (k % 4):P * (k % 4 + 1)], xn[:, t, P * k:P * (k + 1)],
                                            pick[:, t, :], start=(t == 0), stop=(t == 1))
                    ins.then_inc(gathered, 1)

            gather(0)
            pe.wait_ge(units_ready, 1)
            n_more = pe.value_load(unit_i[0:1, 0:1], min_val=0, max_val=3)
            gx = (gx_hi, gx_lo)
            with pe.Fori(0, n_more + E) as u:
                def cut_slot(j, k):
                    pe.wait_ge(lo_ready, u * UNIT_SLOTS + (S_MOE + j + 1))
                    return [a[:, (S_MOE + j) % CUT, :].rearrange("p (k n) -> p k n", k=k) for a in (w_hi, w_lo)]

                def hidden(kind, c):
                    for half in range(2):
                        w = cut_slot(moe_slot(kind, c, half), 4)
                        for k4 in range(4):
                            k = 4 * half + k4
                            ins = mul3(ps[:, 2 * (c % 2) + (kind == "up"), :], part(gx, k), part(w, k4),
                                       k == 0, k == KD - 1)
                        ins.then_inc(slot_done, 1)

                def turn_hidden(i):
                    pe.wait_ge(hid_ready, u * NC + (i + 1))
                    if i >= 1:
                        pe.wait_ge(hT_lo_ready, u * NC + i)
                    for j in range(4):
                        ins = pe.transpose(ps[:, 4, P * j:P * (j + 1)], hid[:, i % 2, P * j:P * (j + 1)], ident)
                    ins.then_inc(hid_turned, 1)

                def down(i):
                    pe.wait_ge(hT_lo_ready, u * NC + (i + 1))
                    for half in range(2):
                        w = cut_slot(moe_slot("down", i, half), 2)
                        for k2 in range(2):
                            j = 2 * half + k2
                            for n in range(2):
                                ins = mul3(ps[:, 5 + n, :], part(hT, i % 2, slice(P * j, P * (j + 1))),
                                           part(w, k2, slice(512 * n, 512 * (n + 1))),
                                           i == 0 and j == 0, i == NC - 1 and j == 3)
                        ins.then_inc(slot_done, 1)

                pe.wait_ge(gx_lo_ready, u * 2 + 2)
                for c in range(NC):
                    if c >= 2:
                        pe.wait_ge(silu_ready, u * NC + (c - 1))
                    hidden("gate", c)
                    if c >= 1:
                        turn_hidden(c - 1)
                    if c >= 2:
                        pe.wait_ge(hid_ready, u * NC + (c - 1))
                    hidden("up", c)
                    if c >= 1:
                        down(c - 1)
                    if c == 3:
                        for t in range(TT):
                            ins = pe.transpose(ps[:, 7, P * t:P * (t + 1)], pick_w[:, t, :], ident)
                        ins.then_inc(pick_turned, 1)
                turn_hidden(NC - 1)
                gather(u + 1)
                down(NC - 1)
                pe.wait_ge(pickT_ready, u + 1)
                for q in range(4):
                    if q % 2 == 0:
                        pe.wait_ge(y_ready_a, u + 1)
                    else:
                        pe.wait_ge(y_ready_v, u + 1)
                    if q == 2:
                        pe.wait_ge(gx_lo_ready, u * 2 + 4)
                    pe.matmul(ps[:, q, :], pick_wT[:, q // 2, :], y_sb[:, 512 * (q % 2):512 * (q % 2) + 512],
                              start=True, stop=True).then_inc(scattered, 1)
                pe.wait_ge(h_added, u * 4 + 2)


def kernel(**inputs):
    import numpy as np
    import concourse.bacc as bacc
    from concourse.bass_utils import run_bass_kernel_spmd as run

    a = {k: np.ascontiguousarray(v) for k, v in inputs.items()}
    tables, col, shifts = shape_constants(np)
    arrays = {
        "tables": tables,
        "shifts": shifts,
        "x": a["x"][0],
        "mem": a["mem"][0],
        "gains": np.stack([a["mem_norm"], a["even_norm1"][0], a["even_norm2"][0], a["odd_norm1"][0],
                           a["odd_norm2"][0], a["final_norm"]]),
        "rpb": np.ascontiguousarray(np.transpose(a["even_rpb"][0], (2, 0, 1))),
        "gate_aug": np.concatenate([
            np.concatenate([a["odd_w_gk_fwd"][0], a["odd_w_gk_bwd"][0]], 1),
            np.concatenate([a["odd_b_gk_fwd"][0], a["odd_b_gk_bwd"][0]])[None, :]], 0),
        "g_norm": a["odd_g_norm"],
        "router": a["odd_w_router"][0],
        "mem_kv": a["w_mem_kv"],
        "even_in": a["even_w_in"][0],
        "even_out": a["even_w_out"][0],
        "even_gate": a["even_w_gate"][0],
        "even_up": a["even_w_up"][0],
        "even_down": a["even_w_down"][0],
        "odd_in": a["odd_w_in"][0],
        "odd_out": a["odd_w_out"][0],
        "exp_gate": a["odd_w_gate"][0],
        "exp_up": a["odd_w_up"][0],
        "exp_down": a["odd_w_down"][0],
    }
    nc = bacc.Bacc("TRN2", target_bir_lowering=False, num_devices=1)
    args = [nc.dram_tensor(n, v.shape, mybir.dt.from_np(v.dtype), kind="ExternalInput").ap()
            for n, v in arrays.items()]
    args.append(nc.dram_tensor("out", (T, D), F32, kind="ExternalOutput").ap())
    build(nc, col, *args)
    r = run(nc, [arrays], core_ids=[0])
    return r.results[0]["out"].reshape(1, T, D)
```

```python
from contextlib import ExitStack

import concourse.bass as bass
from concourse import mybir

ALU = mybir.AluOpType
ACT = mybir.ActivationFunctionType
F32 = mybir.dt.float32
F32R = mybir.dt.float32r
I32 = mybir.dt.int32
AX_X = mybir.AxisListType.X

P = 128
D = 1024
T = 256
TT = T // P
KD = D // P
EPS = 1e-6
HEAD = 64
NA_HEADS, MEM_HEADS = 12, 4
GRID_W = 64
ROWS = T // GRID_W
RPB_R, RPB_C = 15, 31
SHIFT_W = 3 * GRID_W - 1
DR0 = 5
NDR = 6
GH, DK, DV = 4, 96, 192
KW, VW = GH * DK, GH * DV
CH = 64
NCH = T // CH
RANK = 16
D_FF = 2816
E = 8
FE = 3584
NEG = -1e30

RAW = 6
CUT = 3
SLOT = 2048

FF_W = 256
FF_N = D_FF // FF_W
FC = 512
NC = FE // FC
UNIT_SLOTS = 6 * NC
HALF = SLOT // 2
RAW_PLACES, ARENA_PLACES = 2 * RAW, 8
PLACES = RAW_PLACES + ARENA_PLACES + 1
MOE_AHEAD = PLACES // 2
MOE_SEMS = 14
assert 2 * UNIT_SLOTS % PLACES == 0 and UNIT_SLOTS % MOE_SEMS == 0 and MOE_SEMS > MOE_AHEAD
MAX_UNITS = E + 3
UCOLS = MAX_UNITS + 1

N_KV, N_IN0, N_OUT, N_FF, N_IN1 = 2, 10, 4, 3 * FF_N, 14
S_IN0 = N_KV
S_OUT0 = S_IN0 + N_IN0
S_FF = S_OUT0 + N_OUT
S_IN1 = S_FF + N_FF
S_OUT1 = S_IN1 + N_IN1
S_MOE = S_OUT1 + N_OUT
IN1_COLS = [(0, KW), (KW, KW)] + [(2 * KW + 384 * i, 384) for i in range(4)] + [(2 * KW + 2 * VW, 2 * RANK + 256)]


BY_TOKEN = [(t, n) for t in range(TT) for n in range(2)]
BY_HALF = [(t, n) for n in range(2) for t in range(TT)]
BIAS_A, BIAS_B, BIAS_GROUPS = 4, 6, -(-GRID_W // 7)


def moe_pieces(j):
    found = []
    for place in (2 * j % PLACES, (2 * j + 1) % PLACES):
        if place < RAW_PLACES:
            found.append(("raw", (place + 2 * (S_MOE % RAW)) % RAW_PLACES, 1))
        elif place < RAW_PLACES + ARENA_PLACES:
            found.append(("arena", place - RAW_PLACES, 1))
        else:
            found.append(("states", 0, 1))
    (a, i, _), (b, k, _) = found
    return [(a, i, 2)] if a == b and k == i + 1 else found


def moe_landed(j):
    j %= UNIT_SLOTS
    mine = [16 * len(moe_pieces(i)) for i in range(j % MOE_SEMS, UNIT_SLOTS, MOE_SEMS)]
    return sum(mine[:j // MOE_SEMS + 1]), sum(mine)


def slot_width(n):
    return 4 * IN1_COLS[(n - S_IN1) // 2][1] if S_IN1 <= n < S_OUT1 else SLOT


def ff_slot(kind, c):
    if kind == "down":
        return S_FF + (3 * (c + 1) + 1 if c + 1 < FF_N else 3 * FF_N - 1)
    return S_FF + (0 if c == 0 else 3 * c - 1) + (1 if kind == "up" else 0)


def mix_tile(item):
    return item // 2 if item < 16 else 6 + (item - 16) // 2


def shape_constants(np):
    i = np.arange(P)[:, None]
    j = np.arange(P)[None, :]
    same = (i // CH) == (j // CH)
    col = {}
    parts = []

    def put(name, a):
        full = np.zeros((P, a.shape[1]), np.float32)
        full[: a.shape[0]] = a
        col[name] = (sum(x.shape[1] for x in parts), a.shape[1])
        parts.append(full)

    put("ident", (i == j) * 1.0)
    put("tri_f", (same & (i <= j)) / 16.0)
    put("tri_b", (same & (i >= j)) / 16.0)
    put("strict_b", (same & (i > j)) * 1.0)
    put("before", (i < j) * 1.0)
    put("ones", np.ones((P, P)))
    put("iota", np.broadcast_to(np.arange(P), (P, P)))
    c = np.arange(P) % GRID_W
    start = np.clip(c - 8, 0, GRID_W - 16)[:, None]
    cc = np.arange(GRID_W)[None, :]
    put("col_mask", np.where((cc >= start) & (cc < start + 16), 0.0, NEG))
    x, dc = np.arange(SHIFT_W)[None, :], np.arange(RPB_C)[:, None]
    shifts = np.zeros((2, 2, 32, SHIFT_W), np.float32)
    shifts[:, 0, :RPB_C] = x + dc == 78
    shifts[:, 1, :RPB_C] = x + dc == 78 + GRID_W
    shifts = shifts.reshape(P, SHIFT_W)
    return np.concatenate(parts, 1), col, shifts


def moe_slot(kind, c, half):
    if kind == "down":
        return (4 + 6 * c + 4 if c + 1 < NC else 4 + 6 * c) + half
    base = 0 if c == 0 else 4 + 6 * (c - 1)
    return base + (2 if kind == "up" else 0) + half


def build(nc, col, tables, shifts, x, mem, gains, rpb, gate_aug, g_norm, router, mem_kv, even_in, even_out,
          even_gate, even_up, even_down, odd_in, odd_out, exp_gate, exp_up, exp_down, out):
    with ExitStack() as ctx:
        def sb(name, shape, dt=F32):
            return ctx.enter_context(nc.sbuf_tensor(name, shape, dt))

        def sem(name):
            return ctx.enter_context(nc.semaphore(name))

        ps = ctx.enter_context(nc.psum_tensor("ps", [P, 8, 512], F32))

        raw = sb("raw", [P, RAW, SLOT])
        w_hi = sb("w_hi", [P, CUT, SLOT], F32R)
        w_lo = sb("w_lo", [P, CUT, SLOT], F32R)
        h = sb("h", [P, TT, D])
        xn = sb("xn", [P, TT, D])
        xt_hi = sb("xt_hi", [P, KD, T], F32R)
        xt_lo = sb("xt_lo", [P, KD, T], F32R)
        hT_hi = sb("hT_hi", [P, 2, 512], F32R)
        hT_lo = sb("hT_lo", [P, 2, 512], F32R)
        gain = sb("gain", [P, D])
        cst = sb("cst", [P, max(a + n for a, n in col.values())])
        mkT = sb("mkT", [P, 2, T])
        mv = sb("mv", [P, 2, 256])
        ss = sb("ss", [P, 6 * TT, 2])
        rstd = sb("rstd", [P, 6 * TT])
        mhalf = sb("mhalf", [P, 8])
        stat = sb("stat", [P, 20, 2, 3])
        gnb = sb("gnb", [P, DV])
        pickT = sb("pickT", [P, TT, P], F32R)
        rt_hi = sb("rt_hi", [P, KD, E], F32R)
        rt_lo = sb("rt_lo", [P, KD, E], F32R)
        unit_i = sb("unit_i", [P, 4], I32)
        states = sb("states", [P, 2, 3, DV])
        ARENA = 13464
        rt_sb = states[:].rearrange("p d k n -> p (d k n)")[:, 0:KD * E].rearrange("p (k e) -> p k e", k=KD)
        arena = sb("arena", [P, ARENA])
        top = [0]

        def take(n):
            a = top[0]
            top[0] += n
            assert top[0] <= ARENA, top[0]
            return arena[:, a:a + n]

        def const(name, rows=P):
            a, n = col[name]
            return cst[0:rows, a:a + n]

        ident, iota = const("ident"), const("iota")

        qkT = take(14 * T).rearrange("p (i t) -> p i t", t=T)
        v0 = take(TT * 768).rearrange("p (t n) -> p t n", t=TT)
        bias = take(NA_HEADS * NDR * GRID_W).rearrange("p (x c) -> p x c", c=GRID_W)
        s_a = take(3 * 2 * T).rearrange("p (b t m) -> p b t m", b=3, t=2)
        pT_a = take(2 * 2 * T).rearrange("p (b j q) -> p b j q", b=2, j=2)
        rp_a = take(NA_HEADS * RPB_R).rearrange("p (h r) -> p h r", r=RPB_R)
        shift = take(SHIFT_W)
        shift_r = hT_hi[:, 0, 0:SHIFT_W]
        rp_cut = hT_lo[:, 0, 0:NA_HEADS * NDR].rearrange("p (h r) -> p h r", r=NDR)
        mem_sb = arena[:, 0:TT * D].rearrange("p (t d) -> p t d", t=TT)
        top[0] = 0
        qg = take(GH * T).rearrange("p (h t) -> p h t", h=GH)
        kg = take(GH * T).rearrange("p (h t) -> p h t", h=GH)
        v1 = take(TT * VW).rearrange("p (t n) -> p t n", t=TT)
        sg = take(TT * VW).rearrange("p (t n) -> p t n", t=TT)
        qm1 = take(2 * T).rearrange("p (i t) -> p i t", i=2)
        z_sb = take(TT * 32).rearrange("p (t n) -> p t n", t=TT)
        glog = take(2 * TT * KW).rearrange("p (d t n) -> p d t n", d=2, t=TT)
        kdt = glog
        bt = take(2 * GH * T).rearrange("p (d x) -> p d x", d=2)
        qe_at = top[0]
        qe = take(2 * GH * T).rearrange("p (d x) -> p d x", d=2)
        ke_at = top[0]
        ke = take(2 * GH * T).rearrange("p (d x) -> p d x", d=2)
        blast = take(2 * GH * NCH).rearrange("p (d n) -> p d n", d=2)
        decay = take(2 * GH * NCH).rearrange("p (d n) -> p d n", d=2)
        gss = take(3 * 2 * GH).rearrange("p (x n) -> p x n", x=3)
        junk = arena[:, qe_at - 2 * DV:qe_at].rearrange("p (b n) -> p b n", b=2)
        state_bufs = [states, arena[:, qe_at - 2 * GH * T:qe_at - 2 * GH * T + 6 * DV].rearrange(
            "p (d k n) -> p d k n", d=2, k=3)]
        top[0] = qe_at
        s_b = take(3 * 2 * T).rearrange("p (b t m) -> p b t m", b=3, t=2)
        pT_b = states[:].rearrange("p d k n -> p (d k n)")[:, 0:4 * T].rearrange("p (b j q) -> p b j q", b=2, j=2)
        top[0] = ke_at
        gk_w = take(2 * KW)
        zT = take(2 * T).rearrange("p (d t) -> p d t", d=2)
        xn_flat = xn[:].rearrange("p t d -> p (t d)")
        o1 = xn_flat[:, 0:TT * VW].rearrange("p (t n) -> p t n", t=TT)
        at = xn_flat[:, TT * VW:TT * VW + 2 * TT * P].rearrange("p (b t s) -> p b t s", b=2, t=TT)
        top[0] = 0
        silu_sb = take(2 * 512).rearrange("p (b n) -> p b n", b=2)
        hid = take(2 * 512).rearrange("p (b n) -> p b n", b=2)
        pick = take(TT * P).rearrange("p (t s) -> p t s", t=TT)
        u_slot = take(TT * UCOLS).rearrange("p (t u) -> p t u", t=TT)
        u_wt = take(TT * UCOLS).rearrange("p (t u) -> p t u", t=TT)
        unit_f = take(4)
        r_at = top[0]
        gx_hi, gx_lo = xt_hi[:, :, 0:P], xt_lo[:, :, 0:P]
        y_hi, y_lo = xt_hi[:, :, P:T], xt_lo[:, :, P:T]

        def moe_raw(j):
            flat = {"raw": raw[:].rearrange("p r n -> p (r n)"),
                    "arena": arena[:, ARENA - ARENA_PLACES * HALF:ARENA],
                    "states": states[:].rearrange("p d k n -> p (d k n)")}
            at, pieces = 0, []
            for where, i, halves in moe_pieces(j):
                pieces.append((at, flat[where][:, HALF * i:HALF * (i + halves)]))
                at += HALF * halves
            return pieces

        def cum_ps(d):
            return ps[0:DK, 6 - 2 * d:8 - 2 * d, :].rearrange("p b (n c) -> p (b n) c", c=CH)

        def score_bank(i):
            return (0, 1, 6, 7)[i % 4] if i < 16 else i % 2

        def o_ps(i, t):
            return ps[:, 6 + i % 2, DV * t:DV * (t + 1)]

        def out_ps(first_bank, c, t):
            return ps[:, 4 + (first_bank + 2 * c + t) % 4, :]

        top[0] = r_at

        def by_expert():
            return take(TT * E).rearrange("p (t e) -> p t e", t=TT)

        r_logit, r_cand, r_one1, r_one2, r_rest, r_mask = (by_expert() for _ in range(6))
        r_m1, r_m2, r_idx, r_gap, r_gap_exp, r_w1, r_w2 = (take(TT) for _ in range(7))
        r_over, r_number = take(E), take(E)
        r_sel = take(3 * E).rearrange("p (j e) -> p j e", j=3)
        r_prod = take(3 * E).rearrange("p (j e) -> p j e", j=3)
        r_sum = take(3)
        r_logitT = take(T)
        assert top[0] <= ARENA - ARENA_PLACES * HALF

        def STATE_PS(d, k):
            bank, place = ((0, 0), (1, 0), (0, 1))[k] if d == 0 else ((1, 1), (2, 0), (5, 0))[k]
            return ps[0:DK, bank, DV * place:DV * (place + 1)]

        landed = [sem(f"landed_{r}") for r in range(RAW)]
        moe_land = [sem(f"moe_land_{q}") for q in range(MOE_SEMS)]
        hi_ready, lo_ready, slot_done = sem("hi_ready"), sem("lo_ready"), sem("slot_done")
        tables_in, rpb_in, mem_in, x_in, gain_in = (
            sem("tables_in"), sem("rpb_in"), sem("mem_in"), sem("x_in"), sem("gain_in"))
        gnorm_in, router_in, gate_w_in, stored = (
            sem("gnorm_in"), sem("router_in"), sem("gate_w_in"), sem("stored"))
        half_ready, zT_ones, at_zeroed = sem("half_ready"), sem("zT_ones"), sem("at_zeroed")
        sumsq_ready, eps_added, rstd_ready, xn_ready = (
            sem("sumsq_ready"), sem("eps_added"), sem("rstd_ready"), sem("xn_ready"))
        turned, xt_hi_ready, xt_lo_ready = sem("turned"), sem("xt_hi_ready"), sem("xt_lo_ready")
        kv_copied_a, kv_copied_v = sem("kv_copied_a"), sem("kv_copied_v")
        rp_zeroed, rp_parts, bias_mm, bias_ready = sem("rp_zeroed"), sem("rp_parts"), sem("bias_mm"), sem("bias_ready")
        in0_copied_a, in0_copied_v = sem("in0_copied_a"), sem("in0_copied_v")
        scores_done, scores_max, probs_exp, probs_ready, probs_turned, probsT_ready, heads_done = (
            sem("scores_done"), sem("scores_max"), sem("probs_exp"), sem("probs_ready"),
            sem("probs_turned"), sem("probsT_ready"), sem("heads_done"))
        mix_hi, mix_lo, out_bank, out_added = sem("mix_hi"), sem("mix_lo"), sem("out_bank"), sem("out_added")
        ff_silu, ff_hid, ff_hi, ff_lo, ff_bank, ff_added = (
            sem("ff_silu"), sem("ff_hid"), sem("ff_hi"), sem("ff_lo"), sem("ff_bank"), sem("ff_added"))
        in1_copied_a, in1_copied_v = sem("in1_copied_a"), sem("in1_copied_v")
        zT_done, zT_ready, gate_done, gate_abs, gate_exp, gate_ln, gate_ready = (
            sem("zT_done"), sem("zT_ready"), sem("gate_done"), sem("gate_abs"), sem("gate_exp"),
            sem("gate_ln"), sem("gate_ready"))
        cum_done, blast_ready, decay_ready, exps_done, diff_ready, qk_ready = (
            sem("cum_done"), sem("blast_ready"), sem("decay_ready"),
            sem("exps_done"), sem("diff_ready"), sem("qk_ready"))
        kd_exp, kd_ready, kd_turned, kdt_ready = (
            sem("kd_exp"), sem("kd_ready"), sem("kd_turned"), sem("kdt_ready"))
        state_done, states_ready, at_done, at_ready, o_done, o_squared, o_ms, o_rstd, o_ready = (
            sem("state_done"), sem("states_ready"), sem("at_done"), sem("at_ready"), sem("o_done"),
            sem("o_squared"), sem("o_ms"), sem("o_rstd"), sem("o_ready"))
        sgn_ready, o_turned = sem("sgn_ready"), sem("o_turned")
        rt_cut = sem("rt_cut")
        dve_own = sem("dve_own")
        logitsT_done, logitsT_copied, logits_done, gap_ready, gap_exp, masks_ready, ranks_done, units_ready = (
            sem("logitsT_done"), sem("logitsT_copied"), sem("logits_done"), sem("gap_ready"), sem("gap_exp"), sem("masks_ready"),
            sem("ranks_done"), sem("units_ready"))
        silu_ready, hid_ready, hid_turned, hT_hi_ready, hT_lo_ready = (
            sem("silu_ready"), sem("hid_ready"), sem("hid_turned"), sem("hT_hi_ready"), sem("hT_lo_ready"))
        pick_ready, pick_turned, pickT_ready, gathered, gx_hi_ready, gx_lo_ready = (
            sem("pick_ready"), sem("pick_turned"), sem("pickT_ready"), sem("gathered"),
            sem("gx_hi_ready"), sem("gx_lo_ready"))
        y_half, y_hi_ready, y_lo_ready, scattered, h_added = (
            sem("y_half"), sem("y_hi_ready"), sem("y_lo_ready"), sem("scattered"), sem("h_added"))

        kp = "(k p) n -> p k n"
        block = ctx.enter_context(nc.Block())

        @block.sync
        def _(sp):
            def put(n, src):
                if n >= RAW:
                    sp.wait_ge(lo_ready, n - RAW + 1)
                k, width = src.shape[1], src.shape[2]
                sp.dma_start(raw[:, n % RAW, 0:k * width].rearrange("p (k n) -> p k n", k=k),
                             src).then_inc(landed[n % RAW], 16)

            def halves(n, w, c0, width):
                for half in range(2):
                    put(n + half, w.rearrange(kp, p=P)[:, 4 * half:4 * half + 4, c0:c0 + width])

            def next_gain(i):
                if i >= 1:
                    sp.wait_ge(xn_ready, 4 * i)
                sp.dma_start(gain[:], gains[i:i + 1, :].partition_broadcast(P)).then_inc(gain_in, 16)

            sp.dma_start(cst[:], tables).then_inc(tables_in, 16)
            sp.dma_start(shift, shifts).then_inc(rpb_in, 16)
            sp.wait_ge(rp_zeroed, 1)
            for q in (0, 64):
                sp.dma_start(rp_a[q:q + RPB_C], rpb).then_inc(rpb_in, 16)
                sp.dma_start(rp_a[q + 32:q + 32 + RPB_C, :, 1:RPB_R], rpb[:, :, 0:RPB_R - 1]).then_inc(rpb_in, 16)
            sp.dma_start(mem_sb, mem.rearrange("(t p) d -> p t d", p=P)).then_inc(mem_in, 16)
            next_gain(0)
            put(0, mem_kv.rearrange(kp, p=P)[:, 0:4, :])
            sp.dma_start(h[:], x.rearrange("(t p) d -> p t d", p=P)).then_inc(x_in, 16)
            put(1, mem_kv.rearrange(kp, p=P)[:, 4:8, :])
            halves(S_IN0, even_in, 0, 512)
            next_gain(1)
            sp.dma_start(rt_sb[:], router.rearrange(kp, p=P)).then_inc(router_in, 16)
            sp.dma_start(gnb[:], g_norm.partition_broadcast(P)).then_inc(gnorm_in, 16)
            for c in range(1, 5):
                halves(S_IN0 + 2 * c, even_in, 512 * c, 512)
            next_gain(2)
            for c in range(2):
                halves(S_OUT0 + 2 * c, even_out, 512 * c, 512)
            g3, u3, d3 = (w.rearrange(kp, p=P) for w in (even_gate, even_up, even_down))
            for c in range(FF_N + 1):
                if c < FF_N:
                    put(ff_slot("gate", c), g3[:, :, FF_W * c:FF_W * (c + 1)])
                    put(ff_slot("up", c), u3[:, :, FF_W * c:FF_W * (c + 1)])
                if c >= 1:
                    put(ff_slot("down", c - 1), d3[:, 2 * (c - 1):2 * c, :])
                if c == 3:
                    next_gain(3)
            for i, (c0, width) in enumerate(IN1_COLS):
                halves(S_IN1 + 2 * i, odd_in, c0, width)
                if i == 2:
                    sp.wait_ge(ff_added, 4)
                    sp.dma_start(gk_w[0:RANK + 1, :], gate_aug).then_inc(gate_w_in, 16)
                    next_gain(4)
            for c in range(2):
                halves(S_OUT1 + 2 * c, odd_out, 512 * c, 512)

            def expert_loads(base, e, count=UNIT_SLOTS, first_unit=False):
                wg, wu, wd = (w[bass.ds(e, 1)].rearrange("e (k p) f -> p (e k) f", p=P)
                              for w in (exp_gate, exp_up, exp_down))
                src = {}
                for c in range(NC):
                    for half in range(2):
                        cols = slice(FC * c, FC * (c + 1))
                        src[moe_slot("gate", c, half)] = wg[:, 4 * half:4 * half + 4, cols]
                        src[moe_slot("up", c, half)] = wu[:, 4 * half:4 * half + 4, cols]
                        src[moe_slot("down", c, half)] = wd[:, 4 * c + 2 * half:4 * c + 2 * half + 2, :]
                for j in range(count):
                    if first_unit and j < MOE_AHEAD + 1:
                        if j == RAW:
                            sp.wait_ge(o_turned, 3)
                        if j < RAW or j == MOE_AHEAD:
                            sp.wait_ge(lo_ready, S_MOE + (j - RAW if j < RAW else j - MOE_AHEAD) + 1)
                    else:
                        sp.wait_ge(lo_ready, base + (S_MOE + j - MOE_AHEAD + 1))
                    pieces = moe_raw(j)
                    k = src[j].shape[1] // len(pieces)
                    for i, (_, dst) in enumerate(pieces):
                        sp.dma_start(dst.rearrange("p (k n) -> p k n", k=k),
                                     src[j][:, k * i:k * (i + 1), :]).then_inc(moe_land[j % MOE_SEMS], 16)

            expert_loads(0, 0, first_unit=True)
            with sp.Fori(1, E) as u:
                expert_loads(u * UNIT_SLOTS, u)
            sp.wait_ge(units_ready, 1)
            n_more = sp.value_load(unit_i[0:1, 0:1], min_val=0, max_val=3)
            for i in range(MAX_UNITS - E):
                with sp.If(n_more > i):
                    e = sp.value_load(unit_i[0:1, 1 + i:2 + i], min_val=0, max_val=E - 1)
                    expert_loads((E + i) * UNIT_SLOTS, e)
            expert_loads((n_more + E) * UNIT_SLOTS, 0, count=CUT - 1)
            next_gain(5)
            for t in range(TT):
                sp.wait_ge(xn_ready, 20 + 2 * (t + 1))
                sp.dma_start(out[P * t:P * (t + 1), :], xn[:, t, :]).then_inc(stored, 16)
            sp.wait_ge(stored, 16 * TT)

        @block.scalar
        def _(act):
            cut = [0]

            def high_to(last):
                while cut[0] <= last:
                    n = cut[0]
                    w = slot_width(n)
                    if n < S_MOE:
                        act.wait_ge(landed[n % RAW], 16 * (n // RAW + 1))
                    else:
                        act.wait_ge(moe_land[n - S_MOE], 16)
                    if n >= CUT:
                        act.wait_ge(slot_done, n - CUT + 1)
                    act.activation(w_hi[:, n % CUT, 0:w], raw[:, n % RAW, 0:w], ACT.Copy).then_inc(hi_ready, 1)
                    cut[0] += 1

            def products(n):
                high_to(n + CUT)
                act.wait_ge(slot_done, n + 1)

            def mean_squares(i, src, pieces):
                for t, n in pieces:
                    cols = slice(512 * n, 512 * (n + 1))
                    act.activation(xn[:, t, cols], src[:, t, cols], ACT.Square, scale=float(D) ** -0.5,
                                   accum_out=ss[:, TT * i + t, n:n + 1]).then_inc(sumsq_ready, 1)

            def turned_high(i):
                for b in range(4):
                    act.wait_ge(turned, 4 * i + b + 1)
                    act.activation(xt_hi[:, 2 * b:2 * b + 2, :],
                                   ps[:, b, :].rearrange("p (k t) -> p k t", k=2),
                                   ACT.Copy).then_inc(xt_hi_ready, 1)

            def attention(first, n, s, pT, steps):
                for step in steps:
                    if step < n:
                        i = first + step
                        act.wait_ge(scores_max, i + 1)
                        for t in range(2):
                            act.activation(s[:, i % 3, t, :], s[:, i % 3, t, :], ACT.Exp,
                                           bias=stat[:, i, t, 0:1],
                                           accum_out=stat[:, i, t, 1:2]).then_inc(probs_exp, 1)
                    if 2 <= step < n + 2:
                        i = first + step - 2
                        act.wait_ge(probs_turned, i + 1)
                        if step >= 4:
                            act.wait_ge(heads_done, i - 1)
                        act.activation(pT[:, i % 2].rearrange("p j q -> p (j q)"), ps[:, 2 + i % 2, :],
                                       ACT.Copy).then_inc(probsT_ready, 1)
                    if step >= 4 and step % 2 == 0:
                        i = first + step - 3
                        act.wait_ge(heads_done, i + 1)
                        act.activation(xt_hi[:, mix_tile(i), :], ps[:, 4 + i // 2 % 2, 0:T],
                                       ACT.Copy).then_inc(mix_hi, 1)

            act.wait_ge(mem_in, 16)
            mean_squares(0, mem_sb, BY_TOKEN)
            high_to(0)
            turned_high(0)
            act.wait_ge(x_in, 16)
            mean_squares(1, h, BY_TOKEN)
            high_to(2)
            act.wait_ge(slot_done, 2)
            for b in range(2):
                act.activation(mkT[:, b, :], ps[:, 4 + b, 0:T], ACT.Copy).then_inc(kv_copied_a, 1)
            turned_high(1)
            for c in range(5):
                products(S_IN0 + 2 * c)
                if c == 4:
                    attention(0, 16, s_a, pT_a, range(0, 1))
                if c < 4:
                    products(S_IN0 + 2 * c + 1)
                else:
                    act.wait_ge(slot_done, S_IN0 + 10)
                for i in range(2):
                    b = 4 * ((c + 1) % 2) + i
                    if c < 3:
                        dst, src = qkT[:, 4 * c + i, :], ps[:, b, 0:T]
                    elif c == 3:
                        dst, src = v0[:, 0, 256 * i:256 * (i + 1)], ps[:, b, 0:256]
                    else:
                        dst, src = v0[:, i, 512:768], ps[:, b, 0:256]
                    act.activation(dst, src, ACT.Copy).then_inc(in0_copied_a, 1)
            attention(0, 16, s_a, pT_a, range(1, 19))

            def norm_after_out(i, slot0, added):
                for c in range(2):
                    high_to(slot0 + 2 * c + 1 - c + CUT)
                    for t in range(TT):
                        act.wait_ge(out_added, added + 2 * c + t + 1)
                        mean_squares(i, h, [(t, c)])
                turned_high(i)

            norm_after_out(2, S_OUT0, 0)
            for c in range(FF_N):
                products(ff_slot("gate", c))
                if c >= 2:
                    act.wait_ge(ff_hid, c - 1)
                act.activation(silu_sb[:, c % 2, :], ps[:, 2 * (c % 2), :], ACT.Silu).then_inc(ff_silu, 1)
                high_to(ff_slot("up", c) + CUT)
                act.wait_ge(ff_hid, c + 1)
                if c >= 2:
                    act.wait_ge(slot_done, ff_slot("down", c - 2) + 1)
                act.activation(hT_hi[:, c % 2, :], hid[:, c % 2, :], ACT.Copy).then_inc(ff_hi, 1)
            high_to(S_IN1 - 2 + CUT)
            for q, piece in enumerate(BY_TOKEN):
                act.wait_ge(ff_added, q + 1)
                mean_squares(3, h, [piece])
            turned_high(3)
            products(S_IN1 + 1)
            for i in (0, 2):
                act.activation(qg[0:DK, i, :], ps[0:DK, 4 + i, 0:T], ACT.Copy,
                               scale=float(DK) ** -0.5).then_inc(in1_copied_a, 1)
            products(S_IN1 + 3)
            for i in (0, 2):
                act.activation(kg[0:DK, i, :], ps[0:DK, i, 0:T], ACT.Copy).then_inc(in1_copied_a, 1)
            for c in range(2):
                products(S_IN1 + 4 + 2 * c + 1)
                act.activation(v1[:, 0, 384 * c:384 * (c + 1)], ps[:, 4 + 2 * c, 0:384],
                               ACT.Copy).then_inc(in1_copied_a, 1)
            for c in range(2):
                products(S_IN1 + 8 + 2 * c + 1)
                for t in range(TT):
                    act.activation(sg[:, t, 384 * c:384 * (c + 1)], ps[:, 2 * c + t, 0:384],
                                   ACT.Silu).then_inc(in1_copied_a, 1)
            products(S_IN1 + 12)
            act.wait_ge(slot_done, S_IN1 + 14)
            for t in range(TT):
                act.activation(z_sb[:, t, :], ps[:, 4 + t, 0:32], ACT.Copy).then_inc(in1_copied_a, 1)
            attention(16, 4, s_b, pT_b, range(0, 2))
            for i in range(4):
                act.wait_ge(gate_done, i + 1)
                act.activation(glog[:, i // 2, i % 2, :], ps[:, 4 + i, 0:KW], ACT.Abs).then_inc(gate_abs, 1)
            for i in range(4):
                g = glog[:, i // 2, i % 2, :]
                act.wait_ge(gate_abs, i + 1)
                act.activation(g, g, ACT.Exp, scale=-1.0).then_inc(gate_exp, 1)
            attention(16, 4, s_b, pT_b, range(2, 3))
            for i in range(4):
                g = glog[:, i // 2, i % 2, :]
                act.wait_ge(gate_exp, i + 1)
                act.activation(g, g, ACT.Ln, bias=1.0).then_inc(gate_ln, 1)
            attention(16, 4, s_b, pT_b, range(3, 6))
            for d in range(2):
                if d == 1:
                    attention(16, 4, s_b, pT_b, range(6, 7))
                act.wait_ge(diff_ready, d + 1)
                act.activation(bt[0:DK, d], bt[0:DK, d], ACT.Exp).then_inc(kd_exp, 1)
            for d in (1, 0):
                for dst, sign in ((qe, 1.0), (ke, -1.0)):
                    act.activation(dst[0:DK, d].rearrange("p (n c) -> p n c", c=CH), cum_ps(d), ACT.Exp,
                                   scale=sign).then_inc(exps_done, 1)
                act.activation(decay[0:DK, d], blast[0:DK, d], ACT.Exp).then_inc(decay_ready, 1)
                if d == 1:
                    for i in range(4):
                        act.wait_ge(kd_turned, i + 1)
                        act.activation(kdt[:, i // 2, i % 2, :], ps[:, i, 0:KW], ACT.Copy).then_inc(kdt_ready, 1)
            high_to(S_IN1 + 13 + CUT)
            def heads_high(b):
                act.wait_ge(o_turned, b + 1)
                act.activation(xt_hi[:, 2 * b:2 * b + 2, :],
                               ps[:, b, :].rearrange("p (k t) -> p k t", k=2), ACT.Copy).then_inc(mix_hi, 1)

            for i in range(GH):
                if i == GH - 1:
                    heads_high(0)
                act.wait_ge(o_done, i + 1)
                for t in range(TT):
                    k = 2 * i + t
                    if k >= 2:
                        act.wait_ge(o_squared, k - 1)
                    act.activation(junk[:, k % 2, :], o_ps(i, t), ACT.Square,
                                   accum_out=gss[:, 0, k:k + 1]).then_inc(o_squared, 1)
            heads_high(1)
            heads_high(2)
            norm_after_out(4, S_OUT1, 4)
            high_to(S_MOE - 2 + CUT)
            act.wait_ge(gap_ready, 1)
            act.activation(r_gap_exp, r_gap, ACT.Exp).then_inc(gap_exp, 1)

            def gather_high(v):
                for b in range(2):
                    act.wait_ge(gathered, v * 2 + (b + 1))
                    act.activation(gx_hi[:, 4 * b:4 * b + 4, :],
                                   ps[:, 2 + b, :].rearrange("p (k t) -> p k t", k=4),
                                   ACT.Copy).then_inc(gx_hi_ready, 1)

            gather_high(0)
            act.wait_ge(units_ready, 1)
            n_more = act.value_load(unit_i[0:1, 0:1], min_val=0, max_val=3)
            with act.Fori(0, n_more + E) as u:
                done = [CUT - 1]

                def high_unit(last):
                    while done[0] <= last:
                        j, n = done[0], S_MOE + done[0]
                        so_far, per_unit = moe_landed(j)
                        act.wait_ge(moe_land[j % MOE_SEMS],
                                    u * per_unit + (so_far + (per_unit if j >= UNIT_SLOTS else 0)))
                        act.wait_ge(slot_done, u * UNIT_SLOTS + (n - CUT + 1))
                        for at, src in moe_raw(j):
                            ins = act.activation(w_hi[:, n % CUT, at:at + src.shape[1]], src, ACT.Copy)
                        ins.then_inc(hi_ready, 1)
                        done[0] += 1

                def unit_products(j):
                    high_unit(j + CUT)
                    act.wait_ge(slot_done, u * UNIT_SLOTS + (S_MOE + j + 1))

                def hT_high(i):
                    act.wait_ge(hid_turned, u * NC + (i + 1))
                    if i >= 2:
                        act.wait_ge(slot_done, u * UNIT_SLOTS + (S_MOE + moe_slot("down", i - 2, 1) + 1))
                    act.activation(hT_hi[:, i % 2, :], ps[:, 4, :], ACT.Copy).then_inc(hT_hi_ready, 1)

                high_unit(CUT - 1)
                for c in range(NC):
                    unit_products(moe_slot("gate", c, 1))
                    if c >= 2:
                        act.wait_ge(hid_ready, u * NC + (c - 1))
                    act.activation(silu_sb[:, c % 2, :], ps[:, 2 * (c % 2), :], ACT.Silu).then_inc(silu_ready, 1)
                    if c >= 1:
                        hT_high(c - 1)
                    if c == 4:
                        act.wait_ge(pick_turned, u + 1)
                        act.activation(pickT[:].rearrange("p t s -> p (t s)"), ps[:, 7, 0:2 * P],
                                       ACT.Copy).then_inc(pickT_ready, 1)
                high_unit(UNIT_SLOTS - 1)
                hT_high(NC - 1)
                high_unit(moe_slot("down", NC - 2, 1) + CUT)
                gather_high(u + 1)
                high_unit(moe_slot("down", NC - 1, 0) + CUT)
                for n in range(2):
                    if n == 0:
                        act.wait_ge(y_half, u + 1)
                    else:
                        act.wait_ge(slot_done, u * UNIT_SLOTS + (S_MOE + UNIT_SLOTS))
                    act.activation(y_hi[:, 4 * n:4 * n + 4, :], ps[:, 5 + n, :].rearrange("p (k t) -> p k t", k=4),
                                   ACT.Copy).then_inc(y_hi_ready, 1)

            for q, piece in enumerate(BY_HALF):
                act.wait_ge(h_added, (n_more + (E - 1)) * 4 + (q + 1))
                mean_squares(5, h, [piece])

        @block.gpsimd
        def _(pool):
            nc.gpsimd.memset(rp_a, 0.0).then_inc(rp_zeroed, 1)
            nc.gpsimd.memset(mhalf[:], -0.5).then_inc(half_ready, 1)
            pool.wait_ge(half_ready, 1)

            def inverse_root(i, pieces):
                for t in range(TT):
                    k = TT * i + t
                    pool.wait_ge(sumsq_ready, 4 * i + pieces.index((t, 1)) + 1)
                    pool.tensor_scalar(ss[:, k, 0:1], ss[:, k, 0:1], ss[:, k, 1:2], EPS, ALU.add,
                                       ALU.add).then_inc(eps_added, 1)
                    pool.wait_ge(eps_added, k + 1)
                    pool.tensor_tensor(rstd[:, k:k + 1], ss[:, k, 0:1], mhalf[:, 0:1], ALU.pow
                                       ).then_inc(rstd_ready, 1)

            inverse_root(0, BY_TOKEN)
            inverse_root(1, BY_TOKEN)
            inverse_root(2, BY_HALF)
            inverse_root(3, BY_TOKEN)
            pool.wait_ge(ff_added, 4)
            nc.gpsimd.memset(zT[0:32], 1.0).then_inc(zT_ones, 1)
            pool.wait_ge(turned, 16)
            nc.gpsimd.memset(at, 0.0).then_inc(at_zeroed, 1)
            for i in range(GH):
                pool.wait_ge(o_squared, TT * (i + 1))
                k = slice(TT * i, TT * (i + 1))
                pool.tensor_scalar(gss[:, 1, k], gss[:, 0, k], 1.0 / DV, EPS, ALU.mult, ALU.add).then_inc(o_ms, 1)
                pool.wait_ge(o_ms, i + 1)
                pool.tensor_tensor(gss[:, 2, k], gss[:, 1, k], mhalf[:, 0:TT], ALU.pow).then_inc(o_rstd, 1)
            inverse_root(4, BY_HALF)
            inverse_root(5, BY_HALF)

        @block.vector
        def _(dve):
            cut = [0]
            own = [0]

            def mark(ins):
                ins.then_inc(dve_own, 1)
                own[0] += 1

            def settle():
                dve.wait_ge(dve_own, own[0])

            def low_to(last):
                while cut[0] <= last:
                    n = cut[0]
                    w = slot_width(n)
                    dve.wait_ge(hi_ready, n + 1)
                    dve.tensor_tensor(w_lo[:, n % CUT, 0:w], raw[:, n % RAW, 0:w],
                                      w_hi[:, n % CUT, 0:w].bitcast(F32), ALU.subtract).then_inc(lo_ready, 1)
                    cut[0] += 1

            def products(n):
                low_to(n + CUT)
                dve.wait_ge(slot_done, n + 1)

            def norm(i, src):
                dve.wait_ge(gain_in, 16 * (i + 1))
                for t, n in BY_TOKEN:
                    cols = slice(512 * n, 512 * (n + 1))
                    k = TT * i + t
                    dve.wait_ge(rstd_ready, k + 1)
                    dve.scalar_tensor_tensor(xn[:, t, cols], src[:, t, cols], rstd[:, k:k + 1], gain[:, cols],
                                             ALU.mult, ALU.mult).then_inc(xn_ready, 1)

            def turned_low(i):
                for b in range(4):
                    dve.wait_ge(xt_hi_ready, 4 * i + b + 1)
                    dve.tensor_tensor(xt_lo[:, 2 * b:2 * b + 2, :],
                                      ps[:, b, :].rearrange("p (k t) -> p k t", k=2),
                                      xt_hi[:, 2 * b:2 * b + 2, :].bitcast(F32),
                                      ALU.subtract).then_inc(xt_lo_ready, 1)

            def attention(first, n, s, pairs0, steps):
                for step in steps:
                    if step < n:
                        i = first + step
                        dve.wait_ge(scores_done, i + 1)
                        if step >= 3:
                            dve.wait_ge(probs_turned, i - 2)
                        for t in range(2):
                            src = ps[:, score_bank(i), T * t:T * (t + 1)]
                            if i < NA_HEADS:
                                x0 = i * NDR + 2 - 2 * t
                                mark(dve.scalar_tensor_tensor(
                                    s[:, i % 3, t, :], src, float(HEAD) ** -0.5,
                                    bias[:, x0:x0 + ROWS, :].rearrange("p x c -> p (x c)"), ALU.mult, ALU.add))
                            else:
                                mark(dve.tensor_scalar(s[:, i % 3, t, :], src, float(HEAD) ** -0.5, None, ALU.mult))
                        settle()
                        dve.tensor_reduce(stat[:, i, :, 0], s[:, i % 3], AX_X, ALU.max,
                                          negate=True).then_inc(scores_max, 1)
                    if 1 <= step <= n:
                        i = first + step - 1
                        dve.wait_ge(probs_exp, 2 * i + 2)
                        mark(dve.reciprocal(stat[:, i, :, 2], stat[:, i, :, 1]))
                        settle()
                        for t in range(2):
                            dve.tensor_scalar(s[:, i % 3, t, :], s[:, i % 3, t, :], stat[:, i, t, 2:3], None,
                                              ALU.mult).then_inc(probs_ready, 1)
                    if step >= 5 and step % 2 == 1:
                        i = first + step - 4
                        dve.wait_ge(mix_hi, pairs0 + step // 2 - 1)
                        dve.tensor_tensor(xt_lo[:, mix_tile(i), :], ps[:, 4 + i // 2 % 2, 0:T],
                                          xt_hi[:, mix_tile(i), :].bitcast(F32), ALU.subtract).then_inc(mix_lo, 1)

            def add_out(slot0, banks, first_bank):
                for c in range(2):
                    low_to(slot0 + 2 * c + CUT)
                    for t in range(TT):
                        if t == 0:
                            dve.wait_ge(out_bank, banks + c + 1)
                        else:
                            dve.wait_ge(slot_done, slot0 + 2 * c + 2)
                        hs = h[:, t, 512 * c:512 * (c + 1)]
                        dve.tensor_tensor(hs, hs, out_ps(first_bank, c, t), ALU.add).then_inc(out_added, 1)

            def bias_copy(g0, g1):
                for g in range(g0, g1):
                    n = min(7, GRID_W - 7 * g)
                    dve.wait_ge(bias_mm, g + 1)
                    dve.tensor_tensor(
                        bias[:, :, 7 * g:7 * g + n],
                        ps[:, 6 + g % 2, 0:72 * n].rearrange("p (c x) -> p x c", c=n),
                        const("col_mask")[:, 7 * g:7 * g + n].unsqueeze(1).broadcast_to([P, 72, n]),
                        ALU.add).then_inc(bias_ready, 1)

            dve.wait_ge(rpb_in, 5 * 16)
            dve.tensor_copy(rp_cut, rp_a[:, :, DR0:DR0 + NDR]).then_inc(rp_parts, 1)
            dve.tensor_copy(shift_r, shift).then_inc(rp_parts, 1)
            dve.wait_ge(rp_parts, 1)
            dve.tensor_tensor(rp_cut[64:], rp_a[64:, :, DR0:DR0 + NDR], rp_cut[64:].bitcast(F32),
                              ALU.subtract).then_inc(rp_parts, 1)
            dve.wait_ge(tables_in, 16)
            bias_copy(0, BIAS_A)
            norm(0, mem_sb)
            low_to(0)
            bias_copy(BIAS_A, BIAS_B)
            turned_low(0)
            low_to(1)
            norm(1, h)
            low_to(2)
            dve.wait_ge(slot_done, 2)
            for t in range(TT):
                dve.tensor_copy(mv[:, t, :], ps[:, 6 + t, 0:256]).then_inc(kv_copied_v, 1)
            turned_low(1)
            bias_copy(BIAS_B, BIAS_GROUPS)
            dve.wait_ge(router_in, 16)
            dve.tensor_copy(rt_hi[:], rt_sb[:]).then_inc(rt_cut, 1)
            dve.wait_ge(rt_cut, 1)
            dve.tensor_tensor(rt_lo[:], rt_sb[:], rt_hi[:].bitcast(F32), ALU.subtract).then_inc(rt_cut, 1)
            for c in range(5):
                products(S_IN0 + 2 * c)
                if c == 4:
                    attention(0, 16, s_a, 0, range(0, 1))
                if c < 4:
                    products(S_IN0 + 2 * c + 1)
                else:
                    dve.wait_ge(slot_done, S_IN0 + 10)
                for i in (2, 3):
                    b = 4 * ((c + 1) % 2) + i
                    if c < 3:
                        dst, src = qkT[:, 4 * c + i, :], ps[:, b, 0:T]
                    elif c == 3:
                        dst, src = v0[:, 1, 256 * (i - 2):256 * (i - 1)], ps[:, b, 0:256]
                    else:
                        dst, src = qkT[:, 12 + i - 2, :], ps[:, b, 0:T]
                    dve.tensor_copy(dst, src).then_inc(in0_copied_v, 1)
            attention(0, 16, s_a, 0, range(1, 20))
            add_out(S_OUT0, 0, 2)
            norm(2, h)
            turned_low(2)
            for c in range(FF_N):
                products(ff_slot("up", c))
                dve.wait_ge(ff_silu, c + 1)
                if c >= 2:
                    dve.wait_ge(ff_lo, c - 1)
                dve.tensor_tensor(hid[:, c % 2, :], silu_sb[:, c % 2, :], ps[:, 2 * (c % 2) + 1, :],
                                  ALU.mult).then_inc(ff_hid, 1)
                dve.wait_ge(ff_hi, c + 1)
                dve.tensor_tensor(hT_lo[:, c % 2, :], hid[:, c % 2, :], hT_hi[:, c % 2, :].bitcast(F32),
                                  ALU.subtract).then_inc(ff_lo, 1)
            low_to(S_IN1 - 2 + CUT)
            for q, (t, n) in enumerate(BY_TOKEN):
                if q < 3:
                    dve.wait_ge(ff_bank, q + 1)
                else:
                    dve.wait_ge(slot_done, S_IN1)
                hs = h[:, t, 512 * n:512 * (n + 1)]
                dve.tensor_tensor(hs, hs, ps[:, 4 + 2 * t + n, :], ALU.add).then_inc(ff_added, 1)
            norm(3, h)
            turned_low(3)
            products(S_IN1 + 1)
            for i in (1, 3):
                dve.tensor_scalar(qg[0:DK, i, :], ps[0:DK, 4 + i, 0:T], float(DK) ** -0.5, None,
                                  ALU.mult).then_inc(in1_copied_v, 1)
            products(S_IN1 + 3)
            for i in (1, 3):
                dve.tensor_copy(kg[0:DK, i, :], ps[0:DK, i, 0:T]).then_inc(in1_copied_v, 1)
            for c in range(2):
                products(S_IN1 + 4 + 2 * c + 1)
                dve.tensor_copy(v1[:, 1, 384 * c:384 * (c + 1)], ps[:, 4 + 2 * c + 1, 0:384]).then_inc(in1_copied_v, 1)
            products(S_IN1 + 11)
            low_to(S_IN1 + 12 + CUT)
            dve.wait_ge(slot_done, S_IN1 + 14)
            for i in range(2):
                dve.tensor_copy(qm1[:, i, :], ps[:, 6 + i, 0:T]).then_inc(in1_copied_v, 1)
            dve.wait_ge(zT_done, 1)
            dve.wait_ge(zT_ones, 1)
            dve.tensor_copy(zT[0:RANK], ps[0:RANK, 4, :].rearrange("p (d t) -> p d t", d=2)).then_inc(zT_ready, 1)
            attention(16, 4, s_b, 8, range(0, 3))
            for i in range(4):
                g = glog[:, i // 2, i % 2, :]
                dve.wait_ge(gate_ln, i + 1)
                dve.scalar_tensor_tensor(g, ps[:, 4 + i, 0:KW], 0.0, g, ALU.min, ALU.subtract
                                         ).then_inc(gate_ready, 1)
            attention(16, 4, s_b, 8, range(3, 5))
            def kd_times_k(d):
                dve.wait_ge(kd_exp, d + 1)
                dve.tensor_tensor(bt[0:DK, d], bt[0:DK, d], kg[0:DK].rearrange("p h t -> p (h t)"),
                                  ALU.mult).then_inc(kd_ready, 1)

            for d in range(2):
                if d == 1:
                    attention(16, 4, s_b, 8, range(5, 8))
                    kd_times_k(0)
                dve.wait_ge(cum_done, 2 * d + 2)
                dve.tensor_copy(blast[0:DK, d], cum_ps(d)[:, :, CH - 1 if d == 0 else 0]).then_inc(blast_ready, 1)
                dve.wait_ge(blast_ready, d + 1)
                dve.tensor_tensor(bt[0:DK, d].rearrange("p (n c) -> p n c", c=CH),
                                  blast[0:DK, d].unsqueeze(2).broadcast_to([DK, GH * NCH, CH]), cum_ps(d),
                                  ALU.subtract).then_inc(diff_ready, 1)
            kd_times_k(1)
            for d in (1, 0):
                for x, (dst, src) in enumerate(((qe, qg), (ke, kg))):
                    dve.wait_ge(exps_done, 2 * (1 - d) + x + 1)
                    dve.tensor_tensor(dst[0:DK, d], dst[0:DK, d], src[0:DK].rearrange("p h t -> p (h t)"),
                                      ALU.mult).then_inc(qk_ready, 1)

            def o_norm(i):
                c = slice(DV * i, DV * (i + 1))
                dve.wait_ge(o_rstd, i + 1)
                for t in range(TT):
                    dve.scalar_tensor_tensor(o1[:, t, c], o_ps(i, t), gss[:, 2, TT * i + t:TT * i + t + 1],
                                             sg[:, t, c], ALU.mult, ALU.mult).then_inc(o_ready, 1)

            dve.wait_ge(decay_ready, 2)
            dve.wait_ge(at_zeroed, 1)
            mask_f = const("tri_f").bitcast(I32)
            mask_b = const("strict_b").bitcast(I32)
            for i in range(GH):
                dve.wait_ge(state_done, i + 1)
                st = state_bufs[i % 2]
                if i >= 2:
                    dve.wait_ge(o_done, i - 1)
                for d in range(2):
                    mark(dve.tensor_copy(st[0:DK, d, 0, :], STATE_PS(d, 0)))
                for k in (1, 2):
                    settle()
                    for d in range(2):
                        n = k if d == 0 else 3 - k
                        f = decay[0:DK, d, NCH * i + n:NCH * i + n + 1]
                        ins = dve.scalar_tensor_tensor(st[0:DK, d, k, :], st[0:DK, d, k - 1, :], f,
                                                       STATE_PS(d, k), ALU.mult, ALU.add)
                        if k == 1:
                            mark(ins)
                        else:
                            ins.then_inc(states_ready, 1)
                dve.wait_ge(at_done, i + 1)
                for half in range(2):
                    r = slice(CH * half, CH * (half + 1))
                    for d, mask in enumerate((mask_f, mask_b)):
                        dve.copy_predicated(
                            at[r, i % 2, :, r], mask[r, r].unsqueeze(1).broadcast_to([CH, TT, CH]),
                            ps[r, 3 + i % 2, P * d:P * (d + 1)].rearrange("p (t c) -> p t c", t=TT)
                        ).then_inc(at_ready, 1)
                        if d == 0:
                            dve.wait_ge(at_ready, 4 * i + 2 * half + 1)
                if i == 0:
                    dve.wait_ge(gnorm_in, 16)
                    sg8 = sg.rearrange("p t (h n) -> p (t h) n", n=DV)
                    dve.wait_ge(in1_copied_a, 12)
                    dve.tensor_tensor(sg8, sg8, gnb[:].unsqueeze(1).broadcast_to([P, TT * GH, DV]),
                                      ALU.mult).then_inc(sgn_ready, 1)
                if i == 1:
                    low_to(S_IN1 + 13 + CUT)
                if i >= 1:
                    dve.wait_ge(sgn_ready, 1)
                    o_norm(i - 1)
            for b in range(3):
                if b == 2:
                    o_norm(GH - 1)
                dve.wait_ge(mix_hi, 10 + b + 1)
                dve.tensor_tensor(xt_lo[:, 2 * b:2 * b + 2, :], ps[:, b, :].rearrange("p (k t) -> p k t", k=2),
                                  xt_hi[:, 2 * b:2 * b + 2, :].bitcast(F32), ALU.subtract).then_inc(mix_lo, 1)
            add_out(S_OUT1, 2, 0)
            norm(4, h)
            turned_low(4)
            low_to(S_MOE - 2 + CUT)

            i8 = iota[:, 0:E]

            def over_t(a, n=E):
                return a.unsqueeze(1).broadcast_to([P, TT, n])

            def over_e(a):
                return a.unsqueeze(2).broadcast_to([P, TT, E])

            def first_of_largest(src, m, cand, idx, onehot):
                mark(dve.tensor_reduce(m, src, AX_X, ALU.max))
                settle()
                mark(dve.tensor_tensor(cand, src, over_e(m), ALU.is_equal))
                settle()
                mark(dve.scalar_tensor_tensor(cand, cand, -100.0, over_t(i8), ALU.mult, ALU.add))
                settle()
                mark(dve.tensor_reduce(idx, cand, AX_X, ALU.min))
                settle()
                mark(dve.tensor_tensor(onehot, cand, over_e(idx), ALU.is_equal))
                settle()

            dve.wait_ge(logitsT_done, 1)
            dve.tensor_copy(r_logitT[0:E], ps[0:E, 0, 0:T]).then_inc(logitsT_copied, 1)
            dve.wait_ge(logits_done, 1)
            mark(dve.tensor_copy(r_logit, ps[:, 0, 0:TT * E].rearrange("p (t e) -> p t e", t=TT)))
            settle()
            first_of_largest(r_logit, r_m1, r_cand, r_idx, r_one1)
            mark(dve.scalar_tensor_tensor(r_rest, r_one1, NEG, r_logit, ALU.mult, ALU.add))
            settle()
            first_of_largest(r_rest, r_m2, r_cand, r_idx, r_one2)
            dve.tensor_tensor(r_gap, r_m2, r_m1, ALU.subtract).then_inc(gap_ready, 1)
            dve.tensor_tensor(r_mask, r_one1, r_one2, ALU.add).then_inc(masks_ready, 1)
            mark(dve.memset(u_slot, -1.0))
            mark(dve.memset(u_wt, 0.0))
            dve.wait_ge(gap_exp, 1)
            mark(dve.tensor_scalar(r_w1, r_gap_exp, 1.0, None, ALU.add))
            settle()
            mark(dve.reciprocal(r_w1, r_w1))
            settle()
            mark(dve.tensor_tensor(r_w2, r_gap_exp, r_w1, ALU.mult))
            settle()
            mark(dve.tensor_tensor(r_one1, r_one1, over_e(r_w1), ALU.mult))
            mark(dve.tensor_tensor(r_one2, r_one2, over_e(r_w2), ALU.mult))
            settle()
            mark(dve.tensor_tensor(u_wt[:, :, 0:E], r_one1, r_one2, ALU.add))
            dve.wait_ge(ranks_done, 1)
            dve.wait_ge(masks_ready, 1)
            mark(dve.scalar_tensor_tensor(r_cand, ps[:, 1, 0:TT * E].rearrange("p (t e) -> p t e", t=TT), 1.0,
                                          r_mask, ALU.add, ALU.mult))
            settle()
            mark(dve.tensor_scalar(u_slot[:, :, 0:E], r_cand, -1.0, None, ALU.add))
            def build_picks(v):
                for t in range(TT):
                    dve.tensor_scalar(pick[:, t, :], iota, u_slot[:, t, bass.ds(v, 1)], None,
                                      ALU.is_equal).then_inc(pick_ready, 1)

            def gather_low(v):
                for b in range(2):
                    dve.wait_ge(gx_hi_ready, v * 2 + (b + 1))
                    dve.tensor_tensor(gx_lo[:, 4 * b:4 * b + 4, :],
                                      ps[:, 2 + b, :].rearrange("p (k t) -> p k t", k=4),
                                      gx_hi[:, 4 * b:4 * b + 4, :].bitcast(F32), ALU.subtract
                                      ).then_inc(gx_lo_ready, 1)

            settle()
            build_picks(0)
            dve.wait_ge(ranks_done, 2)
            mark(dve.tensor_scalar(r_over, ps[:, 0, 0:E], float(P), None, ALU.is_gt))
            settle()
            mark(dve.tensor_tensor_scan(r_number, const("ones")[:, 0:E], r_over, 0.0, ALU.mult, ALU.add))
            settle()
            for j in range(3):
                mark(dve.scalar_tensor_tensor(r_sel[:, j, :], r_number, float(j + 1), r_over,
                                              ALU.is_equal, ALU.mult))
            settle()
            for dst, vals, off in ([(unit_f[:, 1:4], i8, 0.0)]
                                   + [(u_slot[:, t, E:E + 3], u_slot[:, t, 0:E], -float(P)) for t in range(TT)]
                                   + [(u_wt[:, t, E:E + 3], u_wt[:, t, 0:E], 0.0) for t in range(TT)]):
                mark(dve.tensor_tensor(r_prod, r_sel, vals.unsqueeze(1).broadcast_to([P, 3, E]), ALU.mult))
                settle()
                mark(dve.tensor_reduce(r_sum, r_prod, AX_X, ALU.add))
                settle()
                mark(dve.tensor_scalar(dst, r_sum, off, None, ALU.add))
                settle()
            mark(dve.tensor_copy(unit_f[:, 0:1], r_number[:, E - 1:E]))
            settle()
            dve.tensor_copy(unit_i[:], unit_f).then_inc(units_ready, 1)

            gather_low(0)
            dve.wait_ge(units_ready, 1)
            n_more = dve.value_load(unit_i[0:1, 0:1], min_val=0, max_val=3)
            with dve.Fori(0, n_more + E) as u:
                done = [CUT - 1]

                def low_unit(last):
                    while done[0] <= last:
                        n = S_MOE + done[0]
                        dve.wait_ge(hi_ready, u * UNIT_SLOTS + (n + 1))
                        for at, src in moe_raw(done[0]):
                            cols = slice(at, at + src.shape[1])
                            ins = dve.tensor_tensor(w_lo[:, n % CUT, cols], src,
                                                    w_hi[:, n % CUT, cols].bitcast(F32), ALU.subtract)
                        ins.then_inc(lo_ready, 1)
                        done[0] += 1

                def unit_products(j):
                    low_unit(j + CUT)
                    dve.wait_ge(slot_done, u * UNIT_SLOTS + (S_MOE + j + 1))

                def hT_low(i):
                    dve.wait_ge(hT_hi_ready, u * NC + (i + 1))
                    dve.tensor_tensor(hT_lo[:, i % 2, :], ps[:, 4, :], hT_hi[:, i % 2, :].bitcast(F32),
                                      ALU.subtract).then_inc(hT_lo_ready, 1)

                low_unit(CUT - 1)
                for c in range(NC):
                    if c >= 1:
                        low_unit(moe_slot("gate", c, 1) + CUT)
                        hT_low(c - 1)
                    unit_products(moe_slot("up", c, 1))
                    dve.wait_ge(silu_ready, u * NC + (c + 1))
                    dve.tensor_tensor(hid[:, c % 2, :], silu_sb[:, c % 2, :], ps[:, 2 * (c % 2) + 1, :],
                                      ALU.mult).then_inc(hid_ready, 1)
                    if c == 5:
                        dve.wait_ge(pick_turned, u + 1)
                        build_picks(u + 1)
                low_unit(UNIT_SLOTS - 1)
                hT_low(NC - 1)
                low_unit(moe_slot("down", NC - 2, 1) + CUT)
                gather_low(u + 1)
                for n in range(2):
                    k = slice(4 * n, 4 * n + 4)
                    dve.wait_ge(y_hi_ready, u * 2 + (n + 1))
                    dve.tensor_tensor(y_lo[:, k, :], ps[:, 5 + n, :].rearrange("p (k t) -> p k t", k=4),
                                      y_hi[:, k, :].bitcast(F32), ALU.subtract).then_inc(y_lo_ready, 1)
                for q, (t, n) in enumerate(BY_HALF):
                    hs = h[:, t, 512 * n:512 * (n + 1)]
                    dve.wait_ge(scattered, u * 4 + (q + 1))
                    dve.scalar_tensor_tensor(hs, ps[:, q, :], u_wt[:, t, bass.ds(u, 1)], hs, ALU.mult, ALU.add
                                             ).then_inc(h_added, 1)
                low_unit(UNIT_SLOTS - 2 + CUT)
            norm(5, h)

        @block.tensor
        def _(pe):
            def mul3(dst, a, b, start, stop):
                pe.matmul(dst, a[0], b[0], start=start, stop=False)
                pe.matmul(dst, a[0], b[1], start=False, stop=False)
                return pe.matmul(dst, a[1], b[0], start=False, stop=stop)

            def slot(n, k):
                w = slot_width(n)
                return [a[:, n % CUT, 0:w].rearrange("p (k n) -> p k n", k=k) for a in (w_hi, w_lo)]

            def part(pair, *idx):
                return [a[(slice(None),) + idx] for a in pair]

            xt = (xt_hi, xt_lo)
            hT = (hT_hi, hT_lo)

            def turn(i):
                for t in range(TT):
                    for k in range(KD):
                        if k % 4 == 0:
                            pe.wait_ge(xn_ready, 4 * i + 2 * t + k // 4 + 1)
                        o = T * (k % 2) + P * t
                        ins = pe.transpose(ps[:, k // 2, o:o + P], xn[:, t, P * k:P * (k + 1)], ident)
                        if t == 1 and k % 2 == 1:
                            ins.then_inc(turned, 1)

            def project(n0, groups, fresh=None, bank_done=None, halves=range(2), before_last=None):
                for half in halves:
                    n = n0 + half
                    w = slot(n, 4)
                    pe.wait_ge(lo_ready, n + 1)
                    if fresh is not None:
                        pe.wait_ge(*fresh[half])
                    for g, (dst, form, tok, cols) in enumerate(groups):
                        if before_last is not None and half == 0 and g == len(groups) - 1:
                            before_last()
                        for k4 in range(4):
                            k = 4 * half + k4
                            a = part(w, k4, cols)
                            b = part(xt, k, tok)
                            if form == "by token":
                                a, b = b, a
                            ins = mul3(dst, a, b, k == 0, k == KD - 1)
                        if bank_done is not None and half == 1 and g < len(groups) - 1:
                            ins.then_inc(bank_done, 1)
                    ins.then_inc(slot_done, 1)

            all_t = slice(0, T)
            tok = [slice(P * t, P * (t + 1)) for t in range(TT)]

            def norm_halves(i):
                return [(xt_lo_ready, 4 * i + 2), (xt_lo_ready, 4 * i + 4)]

            def attention(first, n, pT, q_of, k_of, v_of, pairs0, steps):
                ahead = 1 if first == 0 else 0
                for step in steps:
                    if step < n:
                        i = first + step
                        r = slice(HEAD * (i % 2), HEAD * (i % 2) + HEAD)
                        banks = 4 if first == 0 else 2
                        if step >= banks:
                            pe.wait_ge(scores_max, i - banks + 1)
                        for t in range(TT):
                            ins = pe.matmul(ps[:, score_bank(i), T * t:T * (t + 1)], q_of(i)[r, tok[t]], k_of(i)[r, :],
                                            start=True, stop=True)
                        ins.then_inc(scores_done, 1)
                    if 2 + ahead <= step < n + 2 + ahead:
                        i = first + step - 2 - ahead
                        pe.wait_ge(probs_ready, 2 * i + 2)
                        if i >= first + 2:
                            pe.wait_ge(probsT_ready, i - 1)
                        s = s_a if first == 0 else s_b
                        for t in range(TT):
                            for j in range(2):
                                o = T * j + P * t
                                ins = pe.transpose(ps[:, 2 + i % 2, o:o + P], s[:, i % 3, t, P * j:P * (j + 1)],
                                                   ident)
                        ins.then_inc(probs_turned, 1)
                    if step >= 3 + ahead:
                        i = first + step - 3 - ahead
                        r = slice(HEAD * (i % 2), HEAD * (i % 2) + HEAD)
                        pe.wait_ge(probsT_ready, i + 1)
                        if first == 16 and i % 2 == 0:
                            pe.wait_ge(gate_ready, (i - first) // 2 + 1)
                        if i >= first + 4 and i % 2 == 0:
                            pe.wait_ge(mix_lo, pairs0 + (i - first) // 2 - 1)
                        for j in range(2):
                            ins = pe.matmul(ps[r, 4 + i // 2 % 2, 0:T], v_of(i, j), pT[:, i % 2, j, :],
                                            start=(j == 0), stop=(j == 1))
                        ins.then_inc(heads_done, 1)

            def bias_products(g0, g1):
                for g in range(g0, g1):
                    if g >= 2:
                        pe.wait_ge(bias_ready, g - 1)
                    for cc in range(min(7, GRID_W - 7 * g)):
                        c = 7 * g + cc
                        ins = pe.matmul(ps[:, 6 + g % 2, 72 * cc:72 * cc + 72], shift_r[:, 63 - c:191 - c], rp_cut,
                                        start=True, stop=True)
                    ins.then_inc(bias_mm, 1)

            pe.wait_ge(tables_in, 16)
            pe.wait_ge(rp_parts, 3)
            bias_products(0, BIAS_A)
            turn(0)
            bias_products(BIAS_A, BIAS_B)
            pe.wait_ge(bias_ready, BIAS_B)
            project(0, [(ps[:, 4 + i, 0:T], "by feature", all_t, slice(P * i, P * (i + 1))) for i in range(2)]
                    + [(ps[:, 6 + t, 0:256], "by token", tok[t], slice(256, 512)) for t in range(TT)], fresh=norm_halves(0))
            turn(1)
            pe.wait_ge(kv_copied_v, 2)
            bias_products(BIAS_B, BIAS_GROUPS)
            attention0 = (0, 16, pT_a,
                          lambda i: qkT[:, i // 2 if i < 12 else 12 + (i - 12) // 2, :],
                          lambda i: qkT[:, 6 + i // 2, :] if i < 12 else mkT[:, (i - 12) // 2, :],
                          lambda i, j: v0[:, j, HEAD * i:HEAD * (i + 1)] if i < 12
                          else mv[:, j, HEAD * (i - 12):HEAD * (i - 11)], 0)
            pe.wait_ge(kv_copied_a, 2)
            pe.wait_ge(bias_ready, BIAS_GROUPS)
            for c in range(5):
                if c >= 2:
                    pe.wait_ge(in0_copied_a, 2 * (c - 1))
                    pe.wait_ge(in0_copied_v, 2 * (c - 1))
                b = 4 * ((c + 1) % 2)
                if c < 3:
                    gs = [(ps[:, b + i, 0:T], "by feature", all_t, slice(P * i, P * (i + 1))) for i in range(4)]
                elif c == 3:
                    gs = [(ps[:, b + i, 0:256], "by token", tok[i // 2], slice(256 * (i % 2), 256 * (i % 2) + 256))
                          for i in range(4)]
                else:
                    gs = [(ps[:, b + t, 0:256], "by token", tok[t], slice(0, 256)) for t in range(TT)]
                    gs += [(ps[:, b + 2 + i, 0:T], "by feature", all_t, slice(256 + P * i, 256 + P * (i + 1)))
                           for i in range(2)]
                project(S_IN0 + 2 * c, gs, fresh=norm_halves(1) if c == 0 else None, halves=range(1) if c == 4 else range(2))
            pe.wait_ge(in0_copied_a, 8)
            pe.wait_ge(in0_copied_v, 8)
            attention(*attention0, range(0, 2))
            project(S_IN0 + 8, gs, halves=range(1, 2))
            pe.wait_ge(in0_copied_a, 10)
            pe.wait_ge(in0_copied_v, 10)
            attention(*attention0, range(2, 20))

            def project_out(slot0, first_bank, fresh, before_last=None):
                for c in range(2):
                    project(slot0 + 2 * c, [(out_ps(first_bank, c, t), "by token", tok[t], slice(0, 512))
                                            for t in range(TT)], fresh=fresh if c == 0 else None,
                            bank_done=out_bank, before_last=before_last if c == 0 else None)

            project_out(S_OUT0, 2, [(mix_lo, 4), (mix_lo, 8)])
            turn(2)
            for c in range(FF_N + 1):
                if c < FF_N:
                    for kind in ("gate", "up"):
                        n = ff_slot(kind, c)
                        w = slot(n, KD)
                        pe.wait_ge(lo_ready, n + 1)
                        if c >= 2:
                            pe.wait_ge(ff_silu if kind == "gate" else ff_hid, c - 1)
                        for j in range(2):
                            for k in range(KD):
                                if n == S_FF and j == 0 and k % 2 == 0:
                                    pe.wait_ge(xt_lo_ready, 8 + k // 2 + 1)
                                ins = mul3(ps[:, 2 * (c % 2) + (kind == "up"), T * j:T * (j + 1)],
                                           part(w, k, slice(P * j, P * (j + 1))), part(xt, k, all_t),
                                           k == 0, k == KD - 1)
                        ins.then_inc(slot_done, 1)
                if c >= 1:
                    i = c - 1
                    n = ff_slot("down", i)
                    w = slot(n, 2)
                    pe.wait_ge(lo_ready, n + 1)
                    pe.wait_ge(ff_lo, i + 1)
                    for t in range(TT):
                        for half in range(2):
                            for j in range(2):
                                ins = mul3(ps[:, 4 + 2 * t + half, :],
                                           part(hT, i % 2, slice(T * j + P * t, T * j + P * (t + 1))),
                                           part(w, j, slice(512 * half, 512 * (half + 1))),
                                           i == 0 and j == 0, i == FF_N - 1 and j == 1)
                            if i == FF_N - 1 and (t, half) != BY_TOKEN[-1]:
                                ins.then_inc(ff_bank, 1)
                    ins.then_inc(slot_done, 1)
            turn(3)
            for part_i, b0 in ((0, 4), (1, 0)):
                project(S_IN1 + 2 * part_i,
                        [(ps[0:DK, b0 + i, 0:T], "by feature", all_t, slice(DK * i, DK * (i + 1)))
                         for i in range(GH)], fresh=norm_halves(3) if part_i == 0 else None)
            for c in range(4):
                b0 = (4 + 2 * c) % 8
                pe.wait_ge(in1_copied_a, 2 if c < 2 else 4)
                pe.wait_ge(in1_copied_v, 2 if c < 2 else 4)
                project(S_IN1 + 4 + 2 * c, [(ps[:, b0 + t, 0:384], "by token", tok[t], slice(0, 384))
                                            for t in range(TT)])
            pe.wait_ge(in1_copied_a, 6)
            pe.wait_ge(in1_copied_v, 6)
            project(S_IN1 + 12,
                    [(ps[:, 4 + t, 0:2 * RANK], "by token", tok[t], slice(0, 2 * RANK)) for t in range(TT)]
                    + [(ps[:, 6 + i, 0:T], "by feature", all_t, slice(32 + P * i, 32 + P * (i + 1)))
                       for i in range(2)])
            pe.wait_ge(in1_copied_a, 12)
            pe.wait_ge(in1_copied_v, 8)
            for d in range(2):
                for t in range(TT):
                    ins = pe.matmul(ps[0:RANK, 4, T * d + P * t:T * d + P * (t + 1)],
                                    z_sb[:, t, RANK * d:RANK * (d + 1)], ident, start=True, stop=True)
            ins.then_inc(zT_done, 1)
            attention1 = (16, 4, pT_b, lambda i: qm1[:, (i - 16) // 2, :], lambda i: mkT[:, (i - 16) // 2, :],
                          lambda i, j: mv[:, j, HEAD * (i - 16):HEAD * (i - 15)], 8)
            attention(*attention1, range(0, 2))
            pe.wait_ge(zT_ready, 1)
            pe.wait_ge(gate_w_in, 16)
            for i in range(4):
                d, t = i // 2, i % 2
                pe.matmul(ps[:, 4 + i, 0:KW], zT[0:RANK + 1, d, tok[t]], gk_w[0:RANK + 1, KW * d:KW * (d + 1)],
                          start=True, stop=True).then_inc(gate_done, 1)
            attention(*attention1, range(2, 4))
            pe.wait_ge(gate_ready, 4)
            for i in range(4):
                d = i // 2
                if i == 2:
                    attention(*attention1, range(4, 7))
                if i >= 2:
                    pe.wait_ge(mix_lo, 9 + i - 2)
                tri = const("tri_f" if d == 0 else "tri_b")
                for hh in range(2):
                    hd = 2 * (i % 2) + hh
                    for t in range(TT):
                        ins = pe.matmul(ps[0:DK, 6 - 2 * d + i % 2, T * hh + P * t:T * hh + P * (t + 1)],
                                        glog[:, d, t, DK * hd:DK * (hd + 1)], tri, start=True, stop=True)
                ins.then_inc(cum_done, 1)
            for i in range(4):
                d, t = i // 2, i % 2
                pe.wait_ge(kd_ready, d + 1)
                for hd in range(GH):
                    o = T * hd + P * t
                    ins = pe.transpose(ps[:, i, DK * hd:DK * (hd + 1)], bt[0:DK, d, o:o + P], ident[0:DK, 0:DK])
                ins.then_inc(kd_turned, 1)

            def state_products(i):
                for d in range(2):
                    for k in range(3):
                        n = k if d == 0 else 3 - k
                        r = slice(CH * (n % 2), CH * (n % 2) + CH)
                        ins = pe.matmul(STATE_PS(d, k), kdt[r, d, n // 2, DK * i:DK * (i + 1)],
                                        v1[r, n // 2, DV * i:DV * (i + 1)], start=True, stop=True)
                ins.then_inc(state_done, 1)

            def chunk_products(i):
                for t in range(TT):
                    for d in range(2):
                        for half in range(2):
                            o = T * i + P * t + CH * half
                            c0 = P * d + CH * t
                            ins = pe.matmul(ps[CH * half:CH * half + CH, 3 + i % 2, c0:c0 + CH],
                                            ke[0:DK, d, o:o + CH], qe[0:DK, d, o:o + CH], start=True, stop=True)
                ins.then_inc(at_done, 1)

            def turn_heads(b):
                pe.wait_ge(o_ready, TT * (b + 2))
                for k in (2 * b, 2 * b + 1):
                    for t in range(TT):
                        o = T * (k % 2) + P * t
                        ins = pe.transpose(ps[:, b, o:o + P], o1[:, t, P * k:P * (k + 1)], ident)
                ins.then_inc(o_turned, 1)

            pe.wait_ge(kdt_ready, 4)
            state_products(0)
            pe.wait_ge(qk_ready, 4)
            chunk_products(0)
            for i in range(GH):
                if i + 1 < GH:
                    if i >= 1:
                        pe.wait_ge(at_ready, 4 * i)
                    chunk_products(i + 1)
                    pe.wait_ge(states_ready, 2 * (i + 1))
                    state_products(i + 1)
                pe.wait_ge(states_ready, 2 * (i + 1))
                pe.wait_ge(at_ready, 4 * (i + 1))
                if i == GH - 1:
                    turn_heads(0)
                if i >= 2:
                    pe.wait_ge(o_ready, TT * (i - 1))
                for t in range(TT):
                    c0 = DV * t
                    pe.matmul(ps[:, 6 + i % 2, c0:c0 + DV], at[:, i % 2, t, :], v1[:, t, DV * i:DV * (i + 1)],
                              start=True, stop=False, skip_group_check=True)
                    for d in range(2):
                        for half in range(2):
                            n = 2 * t + half
                            o = T * i + CH * n
                            k = n - 1 if d == 0 else 2 - n
                            if 0 <= k <= 2:
                                ins = pe.matmul(ps[CH * half:CH * half + CH, 6 + i % 2, c0:c0 + DV],
                                                qe[0:DK, d, o:o + CH], state_bufs[i % 2][0:DK, d, k, :],
                                                start=False, stop=True, skip_group_check=True)
                ins.then_inc(o_done, 1)
            turn_heads(1)
            project_out(S_OUT1, 0, [(mix_lo, 12), (mix_lo, 13)], before_last=lambda: turn_heads(2))
            turn(4)
            pe.wait_ge(rt_cut, 2)
            pe.wait_ge(xt_hi_ready, 20)
            for k in range(KD):
                if k % 2 == 0:
                    pe.wait_ge(xt_lo_ready, 16 + k // 2 + 1)
                ins = mul3(ps[0:E, 0, 0:T], part((rt_hi, rt_lo), k), part(xt, k), k == 0, k == KD - 1)
            ins.then_inc(logitsT_done, 1)
            pe.wait_ge(logitsT_copied, 1)
            for t in range(TT):
                ins = pe.transpose(ps[:, 0, E * t:E * (t + 1)], r_logitT[0:E, tok[t]], ident[0:E, 0:E])
            ins.then_inc(logits_done, 1)
            pe.wait_ge(masks_ready, 1)
            before, ones = const("before"), const("ones")
            pe.matmul(ps[:, 1, 0:E], before, r_mask[:, 0, :], start=True, stop=True)
            for dst, second in ((ps[:, 1, E:2 * E], before), (ps[:, 0, 0:E], ones)):
                pe.matmul(dst, ones, r_mask[:, 0, :], start=True, stop=False)
                pe.matmul(dst, second, r_mask[:, 1, :], start=False, stop=True).then_inc(ranks_done, 1)

            def gather(v):
                pe.wait_ge(pick_ready, v * 2 + 2)
                for b in range(2):
                    for k in range(4 * b, 4 * b + 4):
                        for t in range(TT):
                            ins = pe.matmul(ps[:, 2 + b, P * (k % 4):P * (k % 4 + 1)], xn[:, t, P * k:P * (k + 1)],
                                            pick[:, t, :], start=(t == 0), stop=(t == 1))
                    ins.then_inc(gathered, 1)

            gather(0)
            pe.wait_ge(units_ready, 1)
            n_more = pe.value_load(unit_i[0:1, 0:1], min_val=0, max_val=3)
            gx = (gx_hi, gx_lo)
            with pe.Fori(0, n_more + E) as u:
                def cut_slot(j, k):
                    pe.wait_ge(lo_ready, u * UNIT_SLOTS + (S_MOE + j + 1))
                    return [a[:, (S_MOE + j) % CUT, :].rearrange("p (k n) -> p k n", k=k) for a in (w_hi, w_lo)]

                def hidden(kind, c):
                    for half in range(2):
                        if kind == "gate" and c == 0:
                            pe.wait_ge(gx_lo_ready, u * 2 + (half + 1))
                        w = cut_slot(moe_slot(kind, c, half), 4)
                        for k4 in range(4):
                            k = 4 * half + k4
                            ins = mul3(ps[:, 2 * (c % 2) + (kind == "up"), :], part(gx, k), part(w, k4),
                                       k == 0, k == KD - 1)
                        ins.then_inc(slot_done, 1)

                def turn_hidden(i):
                    pe.wait_ge(hid_ready, u * NC + (i + 1))
                    if i >= 1:
                        pe.wait_ge(hT_lo_ready, u * NC + i)
                    for j in range(4):
                        ins = pe.transpose(ps[:, 4, P * j:P * (j + 1)], hid[:, i % 2, P * j:P * (j + 1)], ident)
                    ins.then_inc(hid_turned, 1)

                def down(i):
                    pe.wait_ge(hT_lo_ready, u * NC + (i + 1))
                    for half in range(2):
                        w = cut_slot(moe_slot("down", i, half), 2)
                        for n in range(2):
                            for k2 in range(2):
                                j = 2 * half + k2
                                ins = mul3(ps[:, 5 + n, :], part(hT, i % 2, slice(P * j, P * (j + 1))),
                                           part(w, k2, slice(512 * n, 512 * (n + 1))),
                                           i == 0 and j == 0, i == NC - 1 and j == 3)
                            if i == NC - 1 and half == 1 and n == 0:
                                ins.then_inc(y_half, 1)
                        ins.then_inc(slot_done, 1)

                for c in range(NC):
                    if c >= 2:
                        pe.wait_ge(silu_ready, u * NC + (c - 1))
                    hidden("gate", c)
                    if c >= 1:
                        turn_hidden(c - 1)
                    if c >= 2:
                        pe.wait_ge(hid_ready, u * NC + (c - 1))
                    hidden("up", c)
                    if c >= 1:
                        down(c - 1)
                    if c == 3:
                        for t in range(TT):
                            ins = pe.transpose(ps[:, 7, P * t:P * (t + 1)], pick[:, t, :], ident)
                        ins.then_inc(pick_turned, 1)
                turn_hidden(NC - 1)
                gather(u + 1)
                down(NC - 1)
                pe.wait_ge(pickT_ready, u + 1)
                for q, (t, n) in enumerate(BY_HALF):
                    pe.wait_ge(y_lo_ready, u * 2 + (n + 1))
                    if q == 2:
                        pe.wait_ge(gx_lo_ready, u * 2 + 4)
                    for y in (y_hi, y_lo):
                        ins = pe.matmul(ps[:, q, :].rearrange("p (k t) -> p k t", k=4), pickT[:, t, :],
                                        y[:, 4 * n:4 * n + 4, :], start=(y is y_hi), stop=(y is y_lo))
                    ins.then_inc(scattered, 1)
                pe.wait_ge(h_added, u * 4 + 2)


def kernel(**inputs):
    import numpy as np
    import concourse.bacc as bacc
    from concourse.bass_utils import run_bass_kernel_spmd as run

    a = {k: np.ascontiguousarray(v) for k, v in inputs.items()}
    tables, col, shifts = shape_constants(np)
    arrays = {
        "tables": tables,
        "shifts": shifts,
        "x": a["x"][0],
        "mem": a["mem"][0],
        "gains": np.stack([a["mem_norm"], a["even_norm1"][0], a["even_norm2"][0], a["odd_norm1"][0],
                           a["odd_norm2"][0], a["final_norm"]]),
        "rpb": np.ascontiguousarray(np.transpose(a["even_rpb"][0], (2, 0, 1))),
        "gate_aug": np.concatenate([
            np.concatenate([a["odd_w_gk_fwd"][0], a["odd_w_gk_bwd"][0]], 1),
            np.concatenate([a["odd_b_gk_fwd"][0], a["odd_b_gk_bwd"][0]])[None, :]], 0),
        "g_norm": a["odd_g_norm"],
        "router": a["odd_w_router"][0],
        "mem_kv": a["w_mem_kv"],
        "even_in": a["even_w_in"][0],
        "even_out": a["even_w_out"][0],
        "even_gate": a["even_w_gate"][0],
        "even_up": a["even_w_up"][0],
        "even_down": a["even_w_down"][0],
        "odd_in": a["odd_w_in"][0],
        "odd_out": a["odd_w_out"][0],
        "exp_gate": a["odd_w_gate"][0],
        "exp_up": a["odd_w_up"][0],
        "exp_down": a["odd_w_down"][0],
    }
    nc = bacc.Bacc("TRN2", target_bir_lowering=False, num_devices=1)
    args = [nc.dram_tensor(n, v.shape, mybir.dt.from_np(v.dtype), kind="ExternalInput").ap()
            for n, v in arrays.items()]
    args.append(nc.dram_tensor("out", (T, D), F32, kind="ExternalOutput").ap())
    build(nc, col, *args)
    r = run(nc, [arrays], core_ids=[0])
    return r.results[0]["out"].reshape(1, T, D)
```
